# Optimizing a Trainium2 kernel written in Bass

```python
import jax, jax.numpy as jnp
from jax import lax
import numpy as np

D_MODEL = 1024
BATCH = 1
SEQ = 256
DEPTH = 2
DEC_BATCH = 8
DEC_SEQ = 8
PAST_LEN = 2048
PAGE_SIZE = 128

D_MIX = D_MODEL
D_ATTN = D_MIX // 2
D_HG = D_MIX // 4
D_CONV = D_MIX - D_ATTN - D_HG
HEAD_DIM = 64
N_HEADS = D_ATTN // HEAD_DIM
N_KV_HEADS = 2
D_KV = N_KV_HEADS * HEAD_DIM
WINDOW = 128
ROPE_THETA = 10000.0
HG_DV = 64
HG_HEADS = D_HG // HG_DV
HG_DK = 64
D_FORGET = HG_HEADS * HG_DK
HG_CHUNK = 64
CONV_WIDTH = 3
D_IN = D_ATTN + 2 * D_KV + 2 * D_FORGET + 2 * D_HG + 3 * D_CONV
D_FF = 2816
FFN_RES_WEIGHT = 0.5
N_SUB = 3
RMS_EPS = 1e-6
NEG_BIG = -1e30

kernel_name = 'hymba_hgrn2_swa_conv_macaron_step'

F32 = jnp.float32

def rms_norm(x, g):
    xf = x.astype(F32)
    y = xf * lax.rsqrt(jnp.mean(xf * xf, axis=-1, keepdims=True) + RMS_EPS)
    return (y * g.astype(F32)).astype(x.dtype)

def rope(x, pos):
    half = x.shape[-1] // 2
    inv = jnp.power(ROPE_THETA, -jnp.arange(half, dtype=F32) / half)
    ang = pos.astype(F32)[:, None] * inv[None, :]
    cos = jnp.cos(ang)[None, :, None, :]
    sin = jnp.sin(ang)[None, :, None, :]
    xf = x.astype(F32)
    x1, x2 = xf[..., :half], xf[..., half:]
    return jnp.concatenate([x1 * cos - x2 * sin, x2 * cos + x1 * sin], axis=-1).astype(x.dtype)

def swiglu(h, w_in, w_out):
    g, u = jnp.split(h @ w_in, 2, axis=-1)
    return (jax.nn.silu(g) * u) @ w_out

def sink_attend(q, k, v, q_pos, k_pos, sinks):
    scale = HEAD_DIM ** -0.5
    s = jnp.einsum('bnqhgd,bnkhd->bnhgqk', q, k).astype(F32) * scale
    diff = q_pos[:, :, None] - k_pos[:, None, :]
    mask = (diff >= 0) & (diff < WINDOW) & (k_pos[:, None, :] >= 0)
    s = jnp.where(mask[None, :, None, None], s, NEG_BIG)
    sink = sinks.astype(F32).reshape(N_KV_HEADS, N_HEADS // N_KV_HEADS)[None, None, :, :, None, None]
    m = jnp.maximum(jnp.max(s, axis=-1, keepdims=True), sink)
    p = jnp.exp(s - m)
    p = p / (jnp.sum(p, axis=-1, keepdims=True) + jnp.exp(sink - m))
    return jnp.einsum('bnhgqk,bnkhd->bnqhgd', p.astype(v.dtype), v)

def window_attention(q, k, v, pos0, sinks, kv_prev):
    B, T = q.shape[0], q.shape[1]
    G = N_HEADS // N_KV_HEADS
    if kv_prev is None:
        nb = T // WINDOW
        qb = q.reshape(B, nb, WINDOW, N_KV_HEADS, G, HEAD_DIM)
        kb = k.reshape(B, nb, WINDOW, N_KV_HEADS, HEAD_DIM)
        vb = v.reshape(B, nb, WINDOW, N_KV_HEADS, HEAD_DIM)
        kk = jnp.concatenate([jnp.concatenate([jnp.zeros_like(kb[:, :1]), kb[:, :-1]], axis=1), kb], axis=2)
        vv = jnp.concatenate([jnp.concatenate([jnp.zeros_like(vb[:, :1]), vb[:, :-1]], axis=1), vb], axis=2)
        q_pos = pos0 + jnp.arange(T).reshape(nb, WINDOW)
        k_pos = pos0 + (jnp.arange(nb) * WINDOW)[:, None] + jnp.arange(-WINDOW, WINDOW)[None, :]
        o = sink_attend(qb, kk, vv, q_pos, k_pos, sinks)
        keep = min(WINDOW, T)
        new_k, new_v = k[:, T - keep:], v[:, T - keep:]
    else:
        k_prev, v_prev = kv_prev
        P = k_prev.shape[1]
        k_all = jnp.concatenate([k_prev.astype(k.dtype), k], axis=1)
        v_all = jnp.concatenate([v_prev.astype(v.dtype), v], axis=1)
        q_pos = (pos0 + jnp.arange(T))[None, :]
        k_pos = (pos0 - P + jnp.arange(P + T))[None, :]
        o = sink_attend(q.reshape(B, 1, T, N_KV_HEADS, G, HEAD_DIM), k_all[:, None], v_all[:, None],
                        q_pos, k_pos, sinks)
        new_k, new_v = k_all[:, T:], v_all[:, T:]
    return o.reshape(B, T, D_ATTN), new_k, new_v

def hgrn2_chunked(q, logf, v, S0):
    B, T = q.shape[0], q.shape[1]
    L = min(HG_CHUNK, T)
    nC = -(-T // L)
    pad = nC * L - T
    padw = ((0, 0), (0, pad), (0, 0), (0, 0))
    q = jnp.pad(q, padw)
    logf = jnp.pad(logf, padw)
    v = jnp.pad(v, padw)
    k = -jnp.expm1(logf)

    def to_chunks(a):
        return a.reshape(B, nC, L, HG_HEADS, a.shape[-1]).transpose(1, 0, 3, 2, 4)

    causal = jnp.tril(jnp.ones((L, L), dtype=bool))[None, None, :, :, None]

    def step(S, inp):
        qc, lfc, kc, vc = inp
        b = jnp.cumsum(lfc, axis=2)
        diff = b[:, :, :, None, :] - b[:, :, None, :, :]
        dec = jnp.exp(jnp.where(causal, diff, NEG_BIG))
        A = jnp.einsum('bhtk,bhsk,bhtsk->bhts', qc, kc, dec)
        o = jnp.einsum('bhts,bhsv->bhtv', A, vc) + jnp.einsum('bhtk,bhkv->bhtv', qc * jnp.exp(b), S)
        bL = b[:, :, -1:, :]
        S = jnp.exp(bL[:, :, 0, :])[..., None] * S + jnp.einsum('bhsk,bhsv->bhkv', kc * jnp.exp(bL - b), vc)
        return S, o

    S, o = lax.scan(step, S0, (to_chunks(q), to_chunks(logf), to_chunks(k), to_chunks(v)))
    o = o.transpose(1, 0, 3, 2, 4).reshape(B, nC * L, HG_HEADS, HG_DV)[:, :T]
    return o, S

def short_conv(u, prev, w):
    T = u.shape[1]
    full = jnp.concatenate([prev.astype(u.dtype), u], axis=1)
    y = full[:, 0:T] * w[0]
    for j in range(1, CONV_WIDTH):
        y = y + full[:, j:j + T] * w[j]
    return y, full[:, T:]

def mixer(h, pos0, kv_prev, S0, conv_prev, lb, w_in, w_out, sinks, gnorm, cw):
    B, T = h.shape[0], h.shape[1]
    sizes = [D_ATTN, D_KV, D_KV, D_FORGET, D_FORGET, D_HG, D_HG, D_CONV, D_CONV, D_CONV]
    z = h @ w_in
    qa, ka, va, qh, fh, ih, gh, bc, cc, hc = jnp.split(z, np.cumsum(sizes)[:-1].tolist(), axis=-1)
    pos = pos0 + jnp.arange(T)
    q = rope(qa.reshape(B, T, N_HEADS, HEAD_DIM), pos)
    k = rope(ka.reshape(B, T, N_KV_HEADS, HEAD_DIM), pos)
    v = va.reshape(B, T, N_KV_HEADS, HEAD_DIM)
    o_attn, new_k, new_v = window_attention(q, k, v, pos0, sinks, kv_prev)
    lbf = lb.reshape(HG_HEADS, HG_DK).astype(F32)
    f = lbf + (1.0 - lbf) * jax.nn.sigmoid(fh.reshape(B, T, HG_HEADS, HG_DK).astype(F32))
    logf = jnp.log(f)
    o_hg, S_new = hgrn2_chunked(qh.reshape(B, T, HG_HEADS, HG_DK).astype(F32), logf,
                                ih.reshape(B, T, HG_HEADS, HG_DV).astype(F32), S0.astype(F32))
    o_hg = rms_norm(o_hg, gnorm).reshape(B, T, D_HG).astype(h.dtype) * jax.nn.silu(gh)
    y_conv, conv_new = short_conv(cc * hc, conv_prev, cw)
    y_conv = bc * y_conv
    out = jnp.concatenate([o_attn, o_hg, y_conv], axis=-1) @ w_out
    return out, new_k, new_v, S_new, conv_new

def layer(x, c, pos0, kv_prev, S0, conv_prev, lb, p):
    a_w, a_b, g_pre, g_post, f_in, f_out, m_in, m_out, sinks, gnorm, cw = p
    B = x.shape[0]
    mod = (jax.nn.silu(c) @ a_w + a_b).reshape(B, N_SUB, 3, D_MODEL)[:, :, :, None, :]

    def modulate(y, i):
        return rms_norm(y, g_pre[i]) * (1.0 + mod[:, i, 1]) + mod[:, i, 0]

    def residual(y, out, i, w):
        return y + w * mod[:, i, 2] * rms_norm(out, g_post[i])

    x = residual(x, swiglu(modulate(x, 0), f_in[0], f_out[0]), 0, FFN_RES_WEIGHT)
    mix, new_k, new_v, S_new, conv_new = mixer(modulate(x, 1), pos0, kv_prev, S0, conv_prev, lb,
                                                m_in, m_out, sinks, gnorm, cw)
    x = residual(x, mix, 1, 1.0)
    x = residual(x, swiglu(modulate(x, 2), f_in[1], f_out[1]), 2, FFN_RES_WEIGHT)
    return x, new_k, new_v, S_new, conv_new

def setup_inputs(seed: int = 0) -> dict:
    key = jax.random.key(seed)
    ks = jax.random.split(key, 24)

    def nrm(k, shape, s):
        return jax.random.normal(k, shape, F32) * s

    win_buf = min(WINDOW, PAST_LEN)
    return {
        'x_prompt': nrm(ks[0], (BATCH, SEQ, D_MODEL), 1.0),
        'x_sample': nrm(ks[1], (DEC_BATCH, DEC_SEQ, D_MODEL), 1.0),
        'cache_k_win': nrm(ks[2], (DEPTH, DEC_BATCH, win_buf, N_KV_HEADS, HEAD_DIM), 1.0),
        'cache_v_win': nrm(ks[3], (DEPTH, DEC_BATCH, win_buf, N_KV_HEADS, HEAD_DIM), 1.0),
        'state_hgrn': nrm(ks[4], (DEPTH, DEC_BATCH, HG_HEADS, HG_DK, HG_DV), 0.5),
        'state_conv': nrm(ks[5], (DEPTH, DEC_BATCH, CONV_WIDTH - 1, D_CONV), 1.0),
        'c_prompt': nrm(ks[6], (BATCH, D_MODEL), 1.0),
        'c_sample': nrm(ks[7], (DEC_BATCH, D_MODEL), 1.0),
        'ada_w': nrm(ks[8], (DEPTH, D_MODEL, N_SUB * 3 * D_MODEL), 0.5 * D_MODEL ** -0.5),
        'ada_b': nrm(ks[9], (DEPTH, N_SUB * 3 * D_MODEL), 0.01),
        'norm_pre': 1.0 + nrm(ks[10], (DEPTH, N_SUB, D_MODEL), 0.05),
        'norm_post': 1.0 + nrm(ks[11], (DEPTH, N_SUB, D_MODEL), 0.05),
        'ffn_w_in': nrm(ks[12], (DEPTH, 2, D_MODEL, 2 * D_FF), D_MODEL ** -0.5),
        'ffn_w_out': nrm(ks[13], (DEPTH, 2, D_FF, D_MODEL), D_FF ** -0.5),
        'mix_w_in': nrm(ks[14], (DEPTH, D_MODEL, D_IN), D_MODEL ** -0.5),
        'mix_w_out': nrm(ks[15], (DEPTH, D_MIX, D_MODEL), D_MIX ** -0.5),
        'attn_sinks': nrm(ks[16], (DEPTH, N_HEADS), 0.5),
        'hgrn_lower_bounds': nrm(ks[17], (DEPTH, D_FORGET), 0.5),
        'hgrn_gnorm': 1.0 + nrm(ks[18], (DEPTH, HG_DV), 0.05),
        'conv_w': nrm(ks[19], (DEPTH, CONV_WIDTH, D_CONV), CONV_WIDTH ** -0.5),
    }

def reference(x_prompt, x_sample, cache_k_win, cache_v_win, state_hgrn, state_conv, c_prompt, c_sample,
              ada_w, ada_b, norm_pre, norm_post, ffn_w_in, ffn_w_out, mix_w_in, mix_w_out,
              attn_sinks, hgrn_lower_bounds, hgrn_gnorm, conv_w):
    sm = jax.nn.softmax(hgrn_lower_bounds.astype(F32), axis=0)
    lbs = jnp.cumsum(sm, axis=0) - sm[0:1]

    yp, ys = x_prompt, x_sample
    kp_l, vp_l, sp_l, cp_l = [], [], [], []
    ks_l, vs_l, ss_l, cs_l = [], [], [], []
    for l in range(DEPTH):
        p = (ada_w[l], ada_b[l], norm_pre[l], norm_post[l], ffn_w_in[l], ffn_w_out[l],
             mix_w_in[l], mix_w_out[l], attn_sinks[l], hgrn_gnorm[l], conv_w[l])
        S0p = jnp.zeros((yp.shape[0], HG_HEADS, HG_DK, HG_DV), F32)
        cv0p = jnp.zeros((yp.shape[0], CONV_WIDTH - 1, D_CONV), yp.dtype)
        yp, k1, v1, s1, c1 = layer(yp, c_prompt, 0, None, S0p, cv0p, lbs[l], p)
        ys, k2, v2, s2, c2 = layer(ys, c_sample, PAST_LEN, (cache_k_win[l], cache_v_win[l]),
                                   state_hgrn[l], state_conv[l], lbs[l], p)
        kp_l.append(k1); vp_l.append(v1); sp_l.append(s1.astype(state_hgrn.dtype)); cp_l.append(c1)
        ks_l.append(k2); vs_l.append(v2); ss_l.append(s2.astype(state_hgrn.dtype)); cs_l.append(c2)

    new_k_win_prompt = jnp.stack(kp_l)
    new_v_win_prompt = jnp.stack(vp_l)
    new_state_hgrn_prompt = jnp.stack(sp_l)
    new_state_conv_prompt = jnp.stack(cp_l)
    new_k_win_sample = jnp.stack(ks_l)
    new_v_win_sample = jnp.stack(vs_l)
    new_state_hgrn_sample = jnp.stack(ss_l)
    new_state_conv_sample = jnp.stack(cs_l)
    return (yp, ys, new_k_win_prompt, new_v_win_prompt, new_state_hgrn_prompt, new_state_conv_prompt,
            new_k_win_sample, new_v_win_sample, new_state_hgrn_sample, new_state_conv_sample)


_drawn_inputs = setup_inputs


def setup_inputs(seed=0):
    import zlib

    import numpy as np

    out = dict(_drawn_inputs(seed))
    spreads = {}
    factors = {}
    for name, (base, spread) in spreads.items():
        noise = np.random.default_rng([zlib.crc32(name.encode()), seed]).standard_normal(out[name].shape)
        drawn = base * np.exp(spread * noise) if base else spread * noise
        out[name] = __import__('jax').numpy.asarray(drawn.astype(out[name].dtype))
    for name, factor in factors.items():
        out[name] = (out[name] * factor).astype(out[name].dtype)
    return out
```

```python
from contextlib import ExitStack

import numpy as np

import concourse.bass as bass
from concourse import mybir

F32 = mybir.dt.float32
F32R = mybir.dt.float32r
ACT = mybir.ActivationFunctionType
ALU = mybir.AluOpType
AX = mybir.AxisListType

P = 128
D = 1024
KT = D // P
DEPTH = 2
TP, NB, TS = 256, 8, 8
T = TP + NB * TS
NS = 1 + NB
DFF = 2816
FT = DFF // P
NH, NKV, HD, WIN = 8, 2, 64, 128
NG = NH // NKV
PAST = 2048
THETA = 10000.0
EPS = 1e-6
NEG = -1e30
SCALE = HD ** -0.5
FMIN = 2.0 ** -63

IT_IN, IT_OUT, IT_MI, IT_MO = 11, 4, 5, 2
W_IN, W_OUT = KT * 256, (FT // 2) * 256
OFF_F0I = 0
OFF_F0O = OFF_F0I + IT_IN
OFF_MI = OFF_F0O + IT_OUT
OFF_MO = OFF_MI + IT_MI
OFF_F1I = OFF_MO + IT_MO
OFF_F1O = OFF_F1I + IT_IN
ITS = OFF_F1O + IT_OUT

START = 8
UNITS = 36
U_A, U_B, U_C = 0, 12, 24

Z_F, Z_Q, Z_I, Z_K, Z_V, Z_A, Z_CC, Z_CH, Z_G, Z_B = 0, 2, 4, 6, 7, 8, 12, 14, 16, 18
NZ = 20
DIAG = -1
LEVELS = [0, 1, 2, DIAG, 3, 4, 5]
NL = len(LEVELS)
NLS = 4
CH = 64

C_ID, C_ROT, C_ONE, C_BD, C_SEL = 0, 128, 256, 384, 512
C_COS = 528
C_SIN = C_COS + T
C_MP = C_SIN + T
C_MS = C_MP + 256
C_GR = C_MS + 2 * 192
C_SQ = C_GR + NL * CH
C_RS = C_SQ + NB
NC_ = C_RS + T

R_AB, R_PRE, R_POST, R_SINK, R_SINKS, R_GN, R_CW = 0, 72, 96, 120, 128, 130, 131
NR = 137

ACT_CHAIN = 7
DVE_CHAIN = 64
POOL_CHAIN = 7

SEG = TP + 2 + NB * (TS + 2)


def constants():
    c = np.zeros((P, NC_), np.float32)
    i = np.arange(P)
    c[i, C_ID + i] = 1
    lo = i % HD < HD // 2
    c[(i + 32)[lo], C_ROT + i[lo]] = -1
    c[(i - 32)[~lo], C_ROT + i[~lo]] = 1
    c[:, C_ONE:C_ONE + P] = 1
    c[:, C_BD:C_BD + P] = (i[:, None] // 64 == i[None, :] // 64)
    for j in range(4):
        for s in range(NS):
            c[32 * j + s, C_SEL + s] = 1
    half = HD // 2
    inv = np.power(np.float32(THETA), -np.arange(half, dtype=np.float32) / np.float32(half)).astype(np.float32)
    pos = np.concatenate([np.arange(TP), np.tile(PAST + np.arange(TS), NB)]).astype(np.float32)
    ang = (pos[None, :] * inv[i % half][:, None]).astype(np.float32)
    c[:, C_COS:C_COS + T] = np.cos(ang)
    c[:, C_SIN:C_SIN + T] = np.sin(ang)
    k = np.arange(256)[None, :]
    c[:, C_MP:C_MP + 256] = np.where((k > i[:, None]) & (k <= i[:, None] + 128), 0, NEG)
    tok = i % TS
    for hi in range(2):
        m = np.full((P, 192), NEG, np.float32)
        m[:, :128] = np.where(np.arange(128)[None, :] > tok[:, None], 0, NEG)
        b = 4 * hi + i // 32
        n = np.arange(64)[None, :]
        m[:, 128:] = np.where((n // TS == b[:, None]) & (n % TS <= tok[:, None]), 0, NEG)
        c[:, C_MS + 192 * hi:C_MS + 192 * (hi + 1)] = m
    s, t = (i % CH)[:, None], np.arange(CH)[None, :]
    for n, lv in enumerate(LEVELS):
        h = 1 << max(lv, 0)
        m = (s == t) if lv == DIAG else (s // (2 * h) == t // (2 * h)) & (s % (2 * h) < h) & (t % (2 * h) >= h)
        c[:, C_GR + n * CH:C_GR + (n + 1) * CH] = m
    c[:, C_SQ:C_SQ + NB] = (i[:, None] // TS == np.arange(NB)[None, :])
    r = np.ones(T, np.float32)
    r[0:TP:CH] = 0
    r[TP::TS] = 0
    c[:, C_RS:C_RS + T] = r
    return c


def trunk(nc, A, O):
    ctx = ExitStack()
    with ctx:
        def sb(name, shape, dt=F32):
            return ctx.enter_context(nc.sbuf_tensor(name, shape, dt))

        def sem(name):
            return ctx.enter_context(nc.semaphore(name))

        x = sb("x", [P, KT, T])
        y = sb("y", [P, KT, T])
        sq = sb("sq", [P, KT, T])
        hmh = sb("hmh", [P, KT, T], F32R)
        hml = sb("hml", [P, KT, T], F32R)
        raw = sb("raw", [P, 2, W_OUT])
        WHI = sb("WHI", [P, 2, W_OUT], F32R)
        WLO = sb("WLO", [P, 2, W_OUT], F32R)
        ada = sb("ada", [P, 2, 1024])
        cst = sb("cst", [P, NC_])
        par2 = sb("par2", [P, DEPTH, NR])
        par = sb("par", [P, NR])
        lb2 = sb("lb2", [P, DEPTH, 2])
        lbt = sb("lbt", [P, 4, 2])
        lbc = sb("lbc", [P, 2, 2])
        cpv = sb("cpv", [P, DEPTH, 2 * NB * 2])
        cso = sb("cso", [P, 2, NS, 2])
        cT = sb("cT", [P, KT, 32])
        adp = sb("adp", [P, 256])
        mod = [sb(f"mod{g}", [P, 24, NS]) for g in "ABC"]
        rt = sb("rt", [P, T])
        rst = sb("rst", [P, T])
        rst2 = sb("rst2", [P, T])
        acc = sb("acc", [P, T])
        dec = sb("dec", [P, 2, 12])
        mx = sb("mx1", [P, 20])
        den = sb("den", [P, 20])
        with ExitStack() as ffn_scope:
            hh = ffn_scope.enter_context(nc.sbuf_tensor("hh", [P, FT, T], F32R))
            hl = ffn_scope.enter_context(nc.sbuf_tensor("hl", [P, FT, T], F32R))
        z = sb("z", [P, NZ, T])
        kc = sb("kc", [P, NB, WIN + TS])
        vc = sb("vc", [P, NB, P])
        s0 = sb("s0", [P, 2, NB, 64])
        big = sb("big", [P, 4920])
        PS = ctx.enter_context(nc.psum_tensor("PS", [P, 8, 512], F32))

        sg = y[:, 0:2, :]
        hf = y[:, 2:4, :]
        yf = y[:, :, :].rearrange("p a b -> p (a b)")
        sf = sq[:, :, :].rearrange("p a b -> p (a b)")
        kk, bb, eb = yf[:, 0:640], yf[:, 640:1280], yf[:, 1280:1920]
        am = yf[:, 1920:1920 + NL * CH]
        it_, kt_, at_ = (sf[:, n * 768:(n + 1) * 768] for n in range(3))
        vtok = it_.rearrange("p (a b) -> p a b", a=3)
        ktok = kt_.rearrange("p (a b) -> p a b", a=3)
        AT = at_.rearrange("p (h c t) -> p h c t", h=4, c=3)
        LV = big[:, 0:3840].rearrange("p (l a t) -> p l (a t)", l=6, a=2)
        DS = big[:, 0:1024].rearrange("p (c a v) -> p c a v", c=4, a=2)
        vm = big[0:64, 1024:3072].rearrange("p (h b v) -> p h b v", h=4, b=NB)
        SC0 = big[:, 0:8 * 129].rearrange("p (h k) -> p h k", h=8)
        SC1 = big[:, 1032:3088].rearrange("p (h k) -> p h k", h=8)
        SS = big[:, 3088:3860].rearrange("p (n g k) -> p n g k", n=2, g=2)
        va = big[:, 3860:4244].rearrange("p (a b) -> p a b", a=3)
        up = big[:, 4244:4920].rearrange("p (a t) -> p a t", a=2)
        PT = yf[:, 0:2048].rearrange("p (s t) -> p s t", s=4)
        qs = yf[:, 1600:1856].rearrange("p (b r) -> p b r", b=NB)
        PC = sf[:, 0:512]
        PN = sf[0:64, 512:1024]

        ident = cst[:, C_ID:C_ID + P]
        rotm = cst[:, C_ROT:C_ROT + P]
        ones = cst[:, C_ONE:C_ONE + P]
        bd = cst[:, C_BD:C_BD + P]
        sel = cst[:, C_SEL:C_SEL + NS]
        cosT = cst[:, C_COS:C_COS + T]
        sinT = cst[:, C_SIN:C_SIN + T]
        mskp = cst[:, C_MP:C_MP + 256]
        msks = cst[:, C_MS:C_MS + 384].rearrange("p (g k) -> p g k", g=2)
        gram = cst[:, C_GR:C_GR + NL * CH]
        seqm = cst[:, C_SQ:C_SQ + NB]
        rset = cst[:, C_RS:C_RS + T]

        s_load = sem("s_load")
        s_raw = [sem(f"s_raw{i}") for i in (0, 1)]
        s_hi = [sem(f"s_hi{i}") for i in (0, 1)]
        s_lo = [sem(f"s_lo{i}") for i in (0, 1)]
        s_used = [sem(f"s_used{i}") for i in (0, 1)]
        s_ada = [sem(f"s_ada{i}") for i in (0, 1)]
        s_part = sem("s_part")
        s_adp = sem("s_adp")
        s_adt = sem("s_adt")
        s_mod = sem("s_mod")
        s_c = sem("s_c")
        s_gread = sem("s_gread")
        s_uread = sem("s_uread")
        s_hh = sem("s_hh")
        s_hl = sem("s_hl")
        s_sqp = sem("s_sqp")
        s_acc = sem("s_acc")
        s_acc0 = sem("s_acc0")
        s_pst = sem("s_pst")
        s_pr = sem("s_pr")
        s_x = sem("s_x")
        s_xs = sem("s_xs")
        s_sqx = sem("s_sqx")
        s_xst = sem("s_xst")
        s_r = sem("s_r")
        s_mt = sem("s_mt")
        s_hmh = sem("s_hmh")
        s_hml = sem("s_hml")
        s_za = sem("s_za")
        s_zd = sem("s_zd")
        s_cache = sem("s_cache")
        s_out = sem("s_out")
        s_st = sem("s_st")
        s_ach = sem("s_ach")
        s_dch = sem("s_dch")
        s_pch = sem("s_pch")
        s_held = sem("s_held")
        s_pch2 = sem("s_pch2")
        ev = {}
        for n in ("e f g b d0 e0 z0 ends eb kh0 kh itp it ktp kt gr am ds dss obk oev osq ost orr og oh "
                  "vm dsm s0n rot qk vtp vt sc scd ex exn pt ptd pv pvd ss ssd sex sexn spt sptd spv spvd "
                  "cv cst mixl kvo exd at lbd lbe pc").split():
            ev[n] = sem("e_" + n)

        WIN_ = A["w_in"].rearrange("l f u p n -> (l f u) p n")
        WOUT = A["w_out"].rearrange("l f u p n -> (l f u) p n")
        MIN_ = A["m_in"].rearrange("l u p n -> (l u) p n")
        MOUT = A["m_out"].rearrange("l u p n -> (l u) p n")
        ADA = A["ada_w"].rearrange("l u p n -> (l u) p n")

        class Chain:

            def __init__(self, eng, s, per_layer):
                self.eng, self.s, self.per, self.base, self.n = eng, s, per_layer, 0, 0

            def mark(self, ins):
                self.n += 1
                ins.then_inc(self.s, 1)
                return self.base + self.n

            def wait(self, value):
                self.eng.wait_ge(self.s, value)

            def link(self, ins):
                self.wait(self.mark(ins))

        def hold(eng):
            eng.sem_inc(s_held, 1)

        block = ctx.enter_context(nc.Block())

        @block.sync
        def _(sp):
            sp.dma_start(cT[:, :, 0:NS], A["c"]).then_inc(s_load, 16)
            sp.dma_start(cst[:], A["cst"]).then_inc(s_load, 16)
            sp.dma_start(par2[:], A["par"].rearrange("l p n -> p l n")).then_inc(s_load, 16)
            sp.dma_start(lb2[:], A["lb"]).then_inc(s_load, 16)
            sp.dma_start(cpv[:], A["cprev"]).then_inc(s_load, 16)
            sp.dma_start(y[:], A["x"]).then_inc(s_load, 16)

            def conditioning(u, src):
                sp.wait_ge(s_part, u + 1)
                for half in (0, 1):
                    sp.dma_start(ada[:, half, :], src[:, 1024 * half:1024 * (half + 1)]).then_inc(s_ada[half], 16)

            def weights(g, slot, src, width):
                sp.wait_ge(s_hi[slot], g + 1)
                sp.wait_ge(s_lo[slot], g + 1)
                sp.dma_start(raw[:, slot, 0:width], src).then_inc(s_raw[slot], 16)

            def ffn_in(l, f, off, uoff):
                conditioning(START + l * UNITS + uoff, ADA[l * UNITS + uoff])
                with sp.Fori(0, IT_IN) as it:
                    for slot in (0, 1):
                        weights(l * ITS + off + it, slot, WIN_[(l * 2 + f) * 2 * IT_IN + it * 2 + slot], W_IN)
                    conditioning(START + l * UNITS + uoff + 1 + it, ADA[l * UNITS + uoff + 1 + it])

            def ffn_out(l, f, off, uoff):
                with sp.Fori(0, IT_OUT) as it:
                    for slot in (0, 1):
                        weights(l * ITS + off + it, slot, WOUT[(l * 2 + f) * 2 * IT_OUT + it * 2 + slot], W_OUT)
                    if uoff is not None:
                        conditioning(START + l * UNITS + uoff + it, ADA[l * UNITS + uoff + it])

            with sp.Fori(0, START) as u:
                conditioning(u, ADA[(DEPTH - 1) * UNITS + U_C + 4 + u])
            with sp.Fori(0, DEPTH) as l:
                ffn_in(l, 0, OFF_F0I, U_A)
                ffn_out(l, 0, OFF_F0O, U_B)
                for it in range(IT_MI):
                    for slot in (0, 1):
                        weights(l * ITS + OFF_MI + it, slot, MIN_[l * 2 * IT_MI + it * 2 + slot], W_IN)
                    conditioning(START + l * UNITS + U_B + 4 + it, ADA[l * UNITS + U_B + 4 + it])
                    if it == 0:
                        sp.wait_ge(s_used[1], l * ITS + OFF_MI + 1)
                        sp.dma_start(kc[:, :, 0:WIN], A["k"][l]).then_inc(s_cache, 16)
                        sp.dma_start(vc[:], A["v"][l]).then_inc(s_cache, 16)
                        sp.dma_start(s0[:], A["s"][l]).then_inc(s_cache, 16)
                for it in range(IT_MO):
                    for slot in (0, 1):
                        weights(l * ITS + OFF_MO + it, slot, MOUT[l * 2 * IT_MO + it * 2 + slot], W_IN)
                    if it == 0:
                        conditioning(START + l * UNITS + U_B + 9, ADA[l * UNITS + U_B + 9])
                    conditioning(START + l * UNITS + U_B + 10 + it, ADA[l * UNITS + U_B + 10 + it])
                ffn_in(l, 1, OFF_F1I, U_C)
                ffn_out(l, 1, OFF_F1O, None)
            sp.wait_ge(s_x, 8 * (3 * DEPTH + 1))
            sp.dma_start(O["x"], x[:]).then_inc(s_out, 16)
            sp.wait_ge(s_out, 16 * (1 + 7 * DEPTH))
            sp.wait_ge(s_st, 32 * DEPTH)

        @block.tensor
        def _(pe):
            mm = nc.tensor.matmul

            def mm3(out, slot, col, rhi, rlo, first, last):
                hi, lo = WHI[:, slot, col:col + P], WLO[:, slot, col:col + P]
                mm(out, hi, rhi, start=first, stop=False)
                mm(out, hi, rlo, start=False, stop=False)
                return mm(out, lo, rhi, start=False, stop=last)

            def partial(u):
                pe.wait_ge(s_ada[0], 16 * (u + 1))
                pe.wait_ge(s_ada[1], 16 * (u + 1))
                pe.wait_ge(s_adp, u + 1)
                for i in (0, 1):
                    for j in range(4):
                        k = 2 * j + i
                        last = mm(PS[32 * j:32 * j + 32, 6, 0:256], cT[:, k, :],
                                  ada[:, k // 4, (k % 4) * 256:(k % 4 + 1) * 256], start=(i == 0), stop=(i == 1))
                last.then_inc(s_part, 1)

            def summed(u):
                pe.wait_ge(s_adp, u + 2)
                pe.wait_ge(s_mod, u + 1)
                for i in (0, 1):
                    last = mm(PS[:, 7, 16 * i:16 * i + NS], adp[:, i * P:(i + 1) * P], sel, start=True, stop=True)
                last.then_inc(s_adt, 1)

            def split_ready(slot, g):
                pe.wait_ge(s_hi[slot], g + 2)
                pe.wait_ge(s_lo[slot], g + 2)

            def pair(slot, bank, tiles=KT):
                for t in (0, 1):
                    for k in range(tiles):
                        last = mm3(PS[:, bank + t, 0:T], slot, k * 256 + t * P, hmh[:, k, :], hml[:, k, :],
                                   k == 0, k == tiles - 1)
                last.then_inc(s_used[slot], 1)

            def x_stats(n):
                for k in range(KT):
                    pe.wait_ge(s_sqx, KT * n + k + 1)
                    last = mm(PS[:, 5, 0:T], ones, sq[:, k, :], start=(k == 0), stop=(k == KT - 1))
                last.then_inc(s_xst, 1)

            def y_stats(n):
                pe.wait_ge(s_acc, 4 * n + 5)
                mm(PS[:, 4, 0:T], ones, acc[:], start=True, stop=True).then_inc(s_pst, 1)

            def ffn_in(l, f, off, uoff):
                u0 = START + l * UNITS + uoff
                partial(u0)
                summed(u0)
                pe.wait_ge(s_hml, (KT + 1) * (3 * l + 2 * f + 1))
                hold(pe)
                with pe.Fori(0, IT_IN) as it:
                    g = l * ITS + off + it
                    split_ready(0, g)
                    pe.wait_ge(s_gread, (2 * l + f) * IT_IN + it + 1)
                    pair(0, 0)
                    partial(u0 + 1 + it)
                    split_ready(1, g)
                    pe.wait_ge(s_uread, (2 * l + f) * IT_IN + it + 1)
                    pair(1, 2)
                    summed(u0 + 1 + it)

            def ffn_out(l, f, off, uoff):
                pe.wait_ge(s_hl, (2 * l + f + 1) * IT_IN + 1)
                hold(pe)
                with pe.Fori(0, IT_OUT) as it:
                    g = l * ITS + off + it
                    if uoff is not None:
                        partial(START + l * UNITS + uoff + it)
                    pe.wait_ge(s_sqp, 4 * (3 * l + 2 * f) + it + 1)
                    for slot in (0, 1):
                        split_ready(slot, g)
                        for t in (0, 1):
                            for i in range(FT // 2):
                                k = slot * (FT // 2) + i
                                last = mm3(PS[:, 4 + t, 0:T], slot, i * 256 + t * P, hh[:, k, :], hl[:, k, :],
                                           k == 0, k == FT - 1)
                        last.then_inc(s_used[slot], 1)
                    if uoff is not None:
                        summed(START + l * UNITS + uoff + it)

            def turn(src, bank, done):
                for t in range(3):
                    for a in (0, 1):
                        w = P if t < 2 else NB * TS
                        out = PS[0:w, bank + t // 2, (t % 2) * 256 + a * P:(t % 2) * 256 + (a + 1) * P]
                        last = nc.tensor.transpose(out, src(a)[:, t * P:t * P + w], ident)
                last.then_inc(done, 1)

            def recurrence(l):
                pe.wait_ge(s_za, 5 * l + 6)
                turn(lambda a: z[:, Z_I + a, :], 0, ev["itp"])
                pe.wait_ge(ev["z0"], l + 1)
                n = 0
                for h in range(4):
                    a, e = h // 2, h % 2
                    rows = slice(64 * e, 64 * e + 64)
                    for cp in range(3):
                        bank = 2 + n % 4
                        if n >= 4:
                            pe.wait_ge(ev["am"], 12 * l + n - 3)
                        hold(pe)
                        for c in ((2 * cp, 2 * cp + 1) if cp < 2 else (4,)):
                            col = a * T + c * CH
                            for i, lv in enumerate(LEVELS[:NL if cp < 2 else NLS]):
                                if lv == DIAG:
                                    left, right = kk[rows, col:col + CH], z[rows, Z_Q + a, c * CH:(c + 1) * CH]
                                else:
                                    left = right = LV[rows, lv, col:col + CH]
                                p0 = 64 * (c % 2)
                                last = mm(PS[p0:p0 + 64, bank, i * CH:(i + 1) * CH], left, right,
                                          start=True, stop=True)
                        last.then_inc(ev["gr"], 1)
                        n += 1
                pe.wait_ge(ev["kh"], l + 1)
                pe.wait_ge(ev["it"], l + 1)
                turn(lambda a: z[:, Z_F + a, :], 0, ev["ktp"])
                pe.wait_ge(ev["kt"], l + 1)
                hold(pe)
                for c in range(4):
                    rows = slice(64 * (c % 2), 64 * (c % 2) + 64)
                    for a in (0, 1):
                        last = mm(PS[:, c % 2, (c // 2) * 256 + a * P:(c // 2) * 256 + (a + 1) * P],
                                  ktok[rows, c // 2, a * P:(a + 1) * P], vtok[rows, c // 2, a * P:(a + 1) * P],
                                  start=True, stop=True)
                last.then_inc(ev["ds"], 1)
                pe.wait_ge(ev["dss"], l + 1)
                pe.wait_ge(ev["at"], 12 * (l + 1))
                hold(pe)
                for c in range(5):
                    rows = slice(64 * (c % 2), 64 * (c % 2) + 64)
                    for a in (0, 1):
                        w = 3 if c % 2 == 0 else 2
                        col = (a * w + c // 2) * CH
                        if 0 < c < 4:
                            mm(PS[:, 2 + c % 2, col:col + CH], DS[:, c - 1, a, :],
                               eb[:, a * T + c * CH:a * T + (c + 1) * CH], start=True, stop=False)
                        for e in (0, 1):
                            last = mm(PS[64 * e:64 * e + 64, 2 + c % 2, col:col + CH],
                                      vtok[rows, c // 2, a * P + 64 * e:a * P + 64 * e + 64],
                                      AT[rows, 2 * a + e, c // 2, :], start=(c in (0, 4)), stop=True)
                pe.wait_ge(s_cache, 48 * (l + 1))
                hold(pe)
                for e in (0, 1):
                    rows = slice(64 * e, 64 * e + 64)
                    for a in (0, 1):
                        for b in range(NB):
                            col = a * T + TP + TS * b
                            last = mm(PS[rows, 4 + e, a * 64 + TS * b:a * 64 + TS * (b + 1)],
                                      s0[rows, a, b, :], eb[rows, col:col + TS], start=True, stop=True)
                last.then_inc(ev["obk"], 1)
                pe.wait_ge(ev["vm"], l + 1)
                hold(pe)
                for h in range(4):
                    a, e = h // 2, h % 2
                    last = mm(PS[64 * e:64 * e + 64, a, :], ktok[0:64, 2, 64 * h:64 * h + 64],
                              vm[:, h].rearrange("p b v -> p (b v)"), start=True, stop=True)
                last.then_inc(ev["dsm"], 1)
                pe.wait_ge(ev["osq"], l + 1)
                for a in (0, 1):
                    last = mm(PS[:, 2 + a, 0:T], bd, z[:, Z_I + a, :], start=True, stop=True)
                last.then_inc(ev["ost"], 1)

            def attention(l):
                pe.wait_ge(ev["s0n"], l + 1)
                for n, t in enumerate((Z_K, Z_A, Z_A + 1, Z_A + 2, Z_A + 3)):
                    if n == 2:
                        pe.wait_ge(ev["orr"], l + 1)
                    if n == 4:
                        pe.wait_ge(ev["oev"], 2 * (l + 1))
                    last = mm(PS[:, n, 0:T], rotm, z[:, t, :], start=True, stop=True)
                last.then_inc(ev["rot"], 1)
                for t in range(3):
                    w = P if t < 2 else NB * TS
                    last = nc.tensor.transpose(PS[0:w, 5, t * P:(t + 1) * P], z[:, Z_V, t * P:t * P + w], ident)
                last.then_inc(ev["vtp"], 1)
                pe.wait_ge(ev["qk"], l + 1)
                pe.wait_ge(ev["vt"], l + 1)
                hold(pe)
                for n in (0, 1):
                    rows = slice(64 * n, 64 * n + 64)
                    for t in range(NG):
                        mm(PS[:, 4 + n, t * P:(t + 1) * P], z[rows, Z_A + t, 0:P], z[rows, Z_K, 0:P],
                           start=True, stop=True)
                    for t in range(NG):
                        last = mm(PS[:, 2 * n + t // 2, (t % 2) * 256:(t % 2 + 1) * 256],
                                  z[rows, Z_A + t, P:TP], z[rows, Z_K, 0:TP], start=True, stop=True)
                last.then_inc(ev["sc"], 1)
                pe.wait_ge(ev["scd"], l + 1)
                hold(pe)
                for n in (0, 1):
                    rows = slice(64 * n, 64 * n + 64)
                    for b in range(NB):
                        q = qs[rows, b, :]
                        p0, c0 = 32 * (b % 4), 192 * (b // 4)
                        mm(PS[p0:p0 + 32, n, c0:c0 + WIN], q, kc[rows, b, 0:WIN], start=True, stop=True)
                        last = mm(PS[p0:p0 + 32, n, c0 + WIN:c0 + 192], q, kc[rows, :, WIN:WIN + TS],
                                  start=True, stop=True)
                last.then_inc(ev["ss"], 1)
                pe.wait_ge(ev["exn"], l + 1)
                for n in (0, 1):
                    for t in range(NG):
                        last = nc.tensor.transpose(PS[:, 2 + n, t * P:(t + 1) * P], SC0[:, NG * n + t, 0:P], ident)
                last.then_inc(ev["pt"], 1)
                pe.wait_ge(ev["ptd"], 3 * l + 1)
                hold(pe)
                for n in (0, 1):
                    last = mm(PS[64 * n:64 * n + 64, 4, :], va[:, 0, 64 * n:64 * n + 64], PT[:, n, :],
                              start=True, stop=True)
                last.then_inc(ev["pv"], 1)
                pe.wait_ge(ev["ssd"], l + 1)
                for s in range(4):
                    kb, n = s // 2, s % 2
                    for t in range(NG):
                        last = nc.tensor.transpose(PS[:, s, t * P:(t + 1) * P],
                                                   SC1[:, NG * n + t, kb * P:(kb + 1) * P], ident)
                last.then_inc(ev["pt"], 1)
                pe.wait_ge(ev["ptd"], 3 * l + 2)
                hold(pe)
                for n in (0, 1):
                    for kb in (0, 1):
                        last = mm(PS[64 * n:64 * n + 64, 5, :], va[:, kb, 64 * n:64 * n + 64], PT[:, 2 * kb + n, :],
                                  start=(kb == 0), stop=(kb == 1))
                last.then_inc(ev["pv"], 1)
                pe.wait_ge(ev["sexn"], l + 1)
                for n in (0, 1):
                    for g in (0, 1):
                        c0 = (2 * n + g) * P
                        nc.tensor.transpose(PS[:, 0, c0:c0 + P], SS[:, n, g, 0:WIN], ident)
                        last = nc.tensor.transpose(PS[0:64, 1, c0:c0 + P], SS[:, n, g, WIN:192], ident)
                last.then_inc(ev["pt"], 1)
                pe.wait_ge(ev["ptd"], 3 * l + 3)
                hold(pe)
                for n in (0, 1):
                    rows = slice(64 * n, 64 * n + 64)
                    mm(PS[rows, 2, 0:256], va[0:64, 2, rows], PN[:, 256 * n:256 * (n + 1)], start=True, stop=True)
                    for b in range(NB):
                        c0 = (b // 4) * P + 32 * (b % 4)
                        last = mm(PS[rows, 2, c0:c0 + 32], vc[:, b, rows], PC[:, 256 * n + c0:256 * n + c0 + 32],
                                  start=False, stop=True, skip_group_check=True)
                last.then_inc(ev["pv"], 1)

            pe.wait_ge(s_c, 1)
            pe.wait_ge(s_load, 16 * 6)
            with pe.Fori(0, START) as u:
                partial(u)
                summed(u)
            with pe.Fori(0, DEPTH) as l:
                x_stats(3 * l)
                ffn_in(l, 0, OFF_F0I, U_A)
                ffn_out(l, 0, OFF_F0O, U_B)
                y_stats(3 * l)
                x_stats(3 * l + 1)
                pe.wait_ge(s_hml, (KT + 1) * (3 * l + 2))
                for it in range(IT_MI):
                    g = l * ITS + OFF_MI + it
                    split_ready(0, g)
                    pe.wait_ge(s_za, 5 * l + it + 1)
                    pair(0, 0)
                    partial(START + l * UNITS + U_B + 4 + it)
                    split_ready(1, g)
                    pe.wait_ge(s_zd, 5 * l + it + 1)
                    pair(1, 2)
                    summed(START + l * UNITS + U_B + 4 + it)
                recurrence(l)
                attention(l)
                for it in range(IT_MO):
                    g = l * ITS + OFF_MO + it
                    u = START + l * UNITS + U_B + 10 + it
                    if it == 0:
                        partial(u - 1)
                        summed(u - 1)
                        pe.wait_ge(ev["mixl"], 3 * (l + 1))
                    else:
                        pe.wait_ge(s_sqp, 12 * l + 6)
                    split_ready(0, g)
                    pair(0, 0)
                    partial(u)
                    split_ready(1, g)
                    if it == 1:
                        pe.wait_ge(s_sqp, 12 * l + 7)
                    pair(1, 2)
                    summed(u)
                y_stats(3 * l + 1)
                x_stats(3 * l + 2)
                ffn_in(l, 1, OFF_F1I, U_C)
                ffn_out(l, 1, OFF_F1O, None)
                y_stats(3 * l + 2)

        @block.scalar
        def _(act):
            a_ = nc.scalar.activation
            ch = Chain(act, s_ach, ACT_CHAIN)

            def hi_split(slot, g, width):
                act.wait_ge(s_raw[slot], 16 * (g + 1))
                act.wait_ge(s_used[slot], g + 1)
                a_(WHI[:, slot, 0:width], raw[:, slot, 0:width], ACT.Copy).then_inc(s_hi[slot], 1)

            def ada_copy(u):
                act.wait_ge(s_part, u + 2)
                act.wait_ge(s_adt, u + 1)
                a_(adp[:], PS[:, 6, 0:256], ACT.Copy).then_inc(s_adp, 1)

            def exp_set():
                hold(act)
                nc.scalar.preload_act_table_set("natural_log_exp_and_others")

            def silu_set():
                hold(act)
                nc.scalar.preload_act_table_set("silu_and_others")

            def rms(bank, out, done, scale, ready, value):
                act.wait_ge(ready, value)
                ch.link(a_(rt[:], PS[:, bank, 0:T], ACT.Ln, bias=EPS, scale=scale))
                a_(out, rt[:], ACT.Exp, scale=-0.5).then_inc(done, 1)

            def x_norm(n, m):
                for k in range(KT):
                    act.wait_ge(s_x, KT * n + k + 1)
                    a_(sq[:, k, :], x[:, k, :], ACT.Square).then_inc(s_sqx, 1)
                rms(5, rst[:], s_r, 1.0 / D, s_xst, n + 1)
                act.wait_ge(s_mt, (KT + 1) * n + 1)
                a_(hmh[:, :, TP:T], sq[:, :, TP:T], ACT.Copy).then_inc(s_hmh, 1)
                for k in range(KT):
                    act.wait_ge(s_mt, (KT + 1) * n + k + 2)
                    a_(hmh[:, k, 0:TP], sq[:, k, 0:TP], ACT.Identity, bias=mod[m][:, 8 + k, 0:1]).then_inc(s_hmh, 1)

            def y_norm(n):
                rms(4, rst2[:], s_pr, 1.0 / D, s_pst, n + 1)

            def squares(out_tiles, bank, pair_):
                a_(y[:, out_tiles, :], PS[:, bank:bank + 2, 0:T], ACT.Copy)
                act.wait_ge(s_acc, pair_ + 1)
                return a_(sq[:, 0:2, :], PS[:, bank:bank + 2, 0:T], ACT.Square)

            def ffn_in(l, f, off, uoff):
                silu_set()
                u0 = START + l * UNITS + uoff
                ada_copy(u0)

                def body(it, width):
                    g = l * ITS + off + it
                    i = (2 * l + f) * IT_IN + it
                    act.wait_ge(s_used[0], g + 2)
                    act.wait_ge(s_uread, i + 1)
                    a_(sg, PS[:, 0:2, 0:T], ACT.Silu).then_inc(s_gread, 1)
                    hi_split(0, g + 1, width)
                    ada_copy(u0 + 1 + it)
                    hi_split(1, g + 1, width)
                    act.wait_ge(s_uread, i + 2)
                    a_(hh[:, bass.ds(it * 2, 2), :], hf, ACT.Copy).then_inc(s_hh, 1)

                with act.Fori(0, IT_IN - 1) as it:
                    body(it, W_IN)
                body(IT_IN - 1, W_OUT)

            def ffn_out(l, f, off, uoff, n):
                def body(it, width):
                    g = l * ITS + off + it
                    if width:
                        hi_split(0, g + 1, width)
                    if uoff is not None:
                        ada_copy(START + l * UNITS + uoff + it)
                    act.wait_ge(s_used[1], g + 2)
                    squares(bass.ds(it * 2, 2), 4, 4 * n + it).then_inc(s_sqp, 1)
                    if width:
                        hi_split(1, g + 1, width)

                with act.Fori(0, IT_OUT - 1) as it:
                    body(it, W_OUT)
                body(IT_OUT - 1, W_IN if uoff is not None else 0)

            def recurrence(l):
                zf = z[:, Z_F:Z_F + 2, :]
                exp_set()
                act.wait_ge(s_za, 5 * l + 6)
                a_(zf, zf, ACT.Exp, scale=-1.0).then_inc(ev["e"], 1)
                act.wait_ge(ev["itp"], l + 1)
                a_(vtok[:, 0:2, :], PS[:, 0, 0:512], ACT.Copy)
                a_(vtok[0:64, 2, :], PS[0:64, 1, 0:256], ACT.Copy).then_inc(ev["it"], 1)
                act.wait_ge(ev["f"], l + 1)
                a_(zf, zf, ACT.Ln).then_inc(ev["g"], 1)
                for s in range(2):
                    act.wait_ge(ev["d0"], 2 * l + s + 1)
                    v = LV[:, 3 * s:3 * s + 3, :]
                    a_(v, v, ACT.Exp).then_inc(ev["e0"], 1)
                a_(eb, bb, ACT.Exp).then_inc(ev["eb"], 1)
                act.wait_ge(ev["kh0"], l + 1)
                a_(zf, zf, ACT.Exp).then_inc(ev["ends"], 1)
                act.wait_ge(ev["ktp"], l + 1)
                a_(ktok[:, 0:2, :], PS[:, 0, 0:512], ACT.Copy)
                a_(ktok[0:64, 2, :], PS[0:64, 1, 0:256], ACT.Copy).then_inc(ev["kt"], 1)
                act.wait_ge(ev["obk"], l + 1)
                o4 = z[:, Z_Q:Z_Q + 2, :].rearrange("p a (c t) -> p a c t", t=CH)
                a_(o4[:, :, 0:5:2, :], PS[:, 2, 0:6 * CH].rearrange("p (a c t) -> p a c t", a=2, c=3), ACT.Copy)
                a_(o4[:, :, 1:4:2, :], PS[:, 3, 0:4 * CH].rearrange("p (a c t) -> p a c t", a=2, c=2),
                   ACT.Copy).then_inc(ev["oev"], 1)
                act.wait_ge(ev["oev"], 2 * (l + 1))
                a_(z[:, Z_I:Z_I + 2, :], z[:, Z_Q:Z_Q + 2, :], ACT.Square).then_inc(ev["osq"], 1)
                act.wait_ge(ev["ost"], l + 1)
                ch.link(a_(z[:, Z_I:Z_I + 2, :], PS[:, 2:4, 0:T], ACT.Ln, bias=EPS, scale=1.0 / HD))
                a_(z[:, Z_I:Z_I + 2, :], z[:, Z_I:Z_I + 2, :], ACT.Exp, scale=-0.5).then_inc(ev["orr"], 1)
                act.wait_ge(ev["og"], l + 1)
                a_(hmh[:, 4:6, :], z[:, Z_Q:Z_Q + 2, :], ACT.Copy).then_inc(ev["oh"], 1)

            def attention(l):
                act.wait_ge(ev["vtp"], l + 1)
                a_(va[:, 0:2, :], PS[:, 5, 0:256], ACT.Copy)
                a_(va[0:64, 2, :], PS[0:64, 5, 256:384], ACT.Copy).then_inc(ev["vt"], 1)
                act.wait_ge(ev["ex"], l + 1)
                for h in range(NH):
                    a_(SC0[:, h, :], SC0[:, h, :], ACT.Exp, bias=mx[:, h:h + 1], accum_out=den[:, h:h + 1])
                for h in range(NH):
                    last = a_(SC1[:, h, :], SC1[:, h, :], ACT.Exp, bias=mx[:, 8 + h:9 + h],
                              accum_out=den[:, 8 + h:9 + h])
                last.then_inc(ev["exd"], 1)
                act.wait_ge(ev["sex"], l + 1)
                for n in (0, 1):
                    for g in (0, 1):
                        i = 16 + 2 * n + g
                        last = a_(SS[:, n, g, :], SS[:, n, g, :], ACT.Exp, bias=mx[:, i:i + 1],
                                  accum_out=den[:, i:i + 1])
                last.then_inc(ev["exd"], 1)
                act.wait_ge(ev["pt"], 3 * l + 1)
                a_(PT[:, 0:2, :], PS[:, 2:4, :], ACT.Copy).then_inc(ev["ptd"], 1)
                act.wait_ge(ev["pv"], 3 * l + 1)
                a_(hmh[:, 0:4, 0:P], PS[:, 4, :].rearrange("p (a t) -> p a t", a=4), ACT.Copy).then_inc(ev["pvd"], 1)
                act.wait_ge(ev["pt"], 3 * l + 2)
                a_(PT[:, :, :], PS[:, 0:4, :], ACT.Copy).then_inc(ev["ptd"], 1)
                act.wait_ge(ev["pv"], 3 * l + 2)
                a_(hmh[:, 0:4, P:TP], PS[:, 5, :].rearrange("p (a t) -> p a t", a=4), ACT.Copy).then_inc(ev["pvd"], 1)
                act.wait_ge(ev["pt"], 3 * l + 3)
                a_(PC, PS[:, 0, :], ACT.Copy)
                a_(PN, PS[0:64, 1, :], ACT.Copy).then_inc(ev["ptd"], 1)
                act.wait_ge(ev["pv"], 3 * l + 3)
                for a in range(4):
                    last = a_(hmh[:, a, TP:T].rearrange("p (b t) -> p b t", t=TS),
                              PS[:, 2, 0:256].rearrange("p (b a t) -> p a b t", a=4, t=TS)[:, a], ACT.Copy)
                last.then_inc(ev["pvd"], 1)
                act.wait_ge(ev["cv"], l + 1)
                a_(hmh[:, 6:8, :], z[:, Z_CC:Z_CC + 2, :], ACT.Copy).then_inc(ev["cst"], 1)

            act.wait_ge(s_load, 16 * 6)
            act.wait_ge(ev["kvo"], 1)
            silu_set()
            a_(cT[:, :, 0:NS], cT[:, :, 0:NS], ACT.Silu).then_inc(s_c, 1)
            act.wait_ge(ev["lbd"], 1)
            exp_set()
            a_(lbt[:, 0:DEPTH, :], lbt[:, 0:DEPTH, :], ACT.Exp).then_inc(ev["lbe"], 1)
            with act.Fori(0, START) as u:
                ada_copy(u)
            with act.Fori(0, DEPTH) as l:
                ch.base, ch.n = l * ACT_CHAIN, 0
                for slot in (0, 1):
                    hi_split(slot, l * ITS, W_IN)
                exp_set()
                x_norm(3 * l, 2)
                ffn_in(l, 0, OFF_F0I, U_A)
                ffn_out(l, 0, OFF_F0O, U_B, 3 * l)
                exp_set()
                y_norm(3 * l)
                x_norm(3 * l + 1, 0)
                silu_set()
                for it in range(IT_MI):
                    g = l * ITS + OFF_MI + it
                    act.wait_ge(s_used[0], g + 2)
                    a_(z[:, 4 * it:4 * it + 2, :], PS[:, 0:2, 0:T],
                       ACT.Silu if 4 * it == Z_G else ACT.Copy).then_inc(s_za, 1)
                    hi_split(0, g + 1, W_IN)
                    ada_copy(START + l * UNITS + U_B + 4 + it)
                    hi_split(1, g + 1, W_IN)
                recurrence(l)
                act.wait_ge(ev["dss"], l + 1)
                for e in (0, 1):
                    act.dma_start(O["sp"][l, e], DS[64 * e:64 * e + 64, 3, :, 64 * e:64 * e + 64]).then_inc(s_st, 16)
                act.wait_ge(ev["s0n"], l + 1)
                act.dma_start(O["ss"][l], s0[:]).then_inc(s_out, 16)
                attention(l)
                act.wait_ge(ev["qk"], l + 1)
                act.dma_start(O["kp"][l], z[:, Z_K, P:TP]).then_inc(s_out, 16)
                act.dma_start(O["ks"][l], kc[:, :, TS:WIN + TS]).then_inc(s_out, 16)
                act.dma_start(O["vp"][l], va[:, 1, :]).then_inc(s_out, 16)
                act.dma_start(O["vs"][l, 0:WIN - TS], vc[TS:WIN, :, :]).then_inc(s_out, 16)
                act.dma_start(O["vn"][l], va[0:64, 2, :]).then_inc(s_out, 16)
                act.dma_start(O["conv"][l], cso[:]).then_inc(s_out, 16)
                exp_set()
                ada_copy(START + l * UNITS + U_B + 9)
                for it in range(IT_MO):
                    g = l * ITS + OFF_MO + it
                    n = 12 * l + 4 + 2 * it
                    act.wait_ge(s_used[0], g + 2)
                    squares(slice(4 * it, 4 * it + 2), 0, n).then_inc(s_sqp, 1)
                    hi_split(0, g + 1, W_IN)
                    ada_copy(START + l * UNITS + U_B + 10 + it)
                    act.wait_ge(s_used[1], g + 2)
                    squares(slice(4 * it + 2, 4 * it + 4), 2, n + 1).then_inc(s_sqp, 1)
                    hi_split(1, g + 1, W_IN)
                y_norm(3 * l + 1)
                x_norm(3 * l + 2, 1)
                act.wait_ge(s_out, 16 * 7 * (l + 1))
                ffn_in(l, 1, OFF_F1I, U_C)
                ffn_out(l, 1, OFF_F1O, None, 3 * l + 2)
                exp_set()
                y_norm(3 * l + 2)
                assert ch.n == ACT_CHAIN, ch.n

        @block.vector
        def _(dve):
            v = nc.vector
            tt, ts, stt = v.tensor_tensor, v.tensor_scalar, v.scalar_tensor_tensor
            ch = Chain(dve, s_dch, DVE_CHAIN)

            def lo_split(slot, g, width):
                dve.wait_ge(s_hi[slot], g + 2)
                tt(WLO[:, slot, 0:width], raw[:, slot, 0:width], WHI[:, slot, 0:width].bitcast(F32),
                   ALU.subtract).then_inc(s_lo[slot], 1)

            def mod_out(u, m, j, bias):
                dve.wait_ge(s_adt, u + 2)
                src = PS[:, 7, 0:32].rearrange("p (i s) -> p i s", i=2)[:, :, 0:NS]
                tt(mod[m][:, bass.ds(j, 2), :], src, bias.unsqueeze(2).to_broadcast([P, 2, NS]), ALU.add)\
                    .then_inc(s_mod, 1)

            def ready(u):
                dve.wait_ge(s_mod, u + 2)

            def group_bias(m, j):
                return par[:, bass.ds(R_AB + 24 * m + j, 2)]

            def gate_ready(m, sub, weight):
                g = mod[m][:, 0:KT, :]
                post = par[:, R_POST + KT * sub:R_POST + KT * (sub + 1)]
                ch.link(stt(g, g, weight, post.unsqueeze(2).to_broadcast([P, KT, NS]), ALU.mult, ALU.mult))

            def by_seq(t, k0):
                return t[:, k0:k0 + KT, 1:NS].unsqueeze(3).to_broadcast([P, KT, NB, TS])

            def seq(t):
                return t[:, :, TP:T].rearrange("p k (b t) -> p k b t", t=TS)

            def x_norm(n, m, sub):
                sc = mod[m][:, 16:24, :]
                pre = par[:, R_PRE + KT * sub:R_PRE + KT * (sub + 1)]
                ch.link(stt(sc, sc, 1.0, pre.unsqueeze(2).to_broadcast([P, KT, NS]), ALU.add, ALU.mult))
                dve.wait_ge(s_r, n + 1)
                xs, rs = x[:, :, TP:T], rst[:, TP:T].unsqueeze(1).to_broadcast([P, KT, NB * TS])
                ch.link(tt(sq[:, :, TP:T], xs, rs, ALU.mult))
                ch.link(tt(seq(sq), seq(sq), by_seq(mod[m], 16), ALU.mult))
                tt(seq(sq), seq(sq), by_seq(mod[m], 8), ALU.add).then_inc(s_mt, 1)

                def scaled(k):
                    stt(sq[:, k, 0:TP], x[:, k, 0:TP], mod[m][:, 16 + k, 0:1], rst[:, 0:TP],
                        ALU.mult, ALU.mult).then_inc(s_mt, 1)

                def low(k):
                    dve.wait_ge(s_hmh, (KT + 1) * n + k + 2)
                    dve.wait_ge(s_mt, (KT + 1) * n + k + 2)
                    stt(hml[:, k, 0:TP], sq[:, k, 0:TP], mod[m][:, 8 + k, 0:1], hmh[:, k, 0:TP].bitcast(F32),
                        ALU.add, ALU.subtract).then_inc(s_hml, 1)

                scaled(0)
                scaled(1)
                dve.wait_ge(s_hmh, (KT + 1) * n + 1)
                dve.wait_ge(s_mt, (KT + 1) * n + 1)
                tt(hml[:, :, TP:T], sq[:, :, TP:T], hmh[:, :, TP:T].bitcast(F32), ALU.subtract).then_inc(s_hml, 1)
                for k in range(KT):
                    if k + 2 < KT:
                        scaled(k + 2)
                    low(k)

            def y_norm(n, m):
                dve.wait_ge(s_pr, n + 1)
                rs = rst2[:, TP:T].unsqueeze(1).to_broadcast([P, KT, NB * TS])
                ch.link(tt(sq[:, :, TP:T], y[:, :, TP:T], rs, ALU.mult))
                ch.link(tt(seq(sq), seq(sq), by_seq(mod[m], 0), ALU.mult))
                tt(x[:, :, TP:T], x[:, :, TP:T], sq[:, :, TP:T], ALU.add)
                done = {}

                def term(k):
                    done[k] = ch.mark(stt(sq[:, k, 0:TP], y[:, k, 0:TP], mod[m][:, k, 0:1], rst2[:, 0:TP],
                                          ALU.mult, ALU.mult))

                term(0)
                for k in range(KT):
                    if k + 1 < KT:
                        term(k + 1)
                    ch.wait(done[k])
                    tt(x[:, k, 0:TP], x[:, k, 0:TP], sq[:, k, 0:TP], ALU.add).then_inc(s_x, 1)

            def add_squares(pair_):
                dve.wait_ge(s_sqp, pair_ + 2)
                dve.wait_ge(s_acc, pair_ + 1)
                tt(acc[:], acc[:], sq[:, 0, :], ALU.add).then_inc(s_acc0, 1)
                dve.wait_ge(s_acc0, pair_ + 1)
                tt(acc[:], acc[:], sq[:, 1, :], ALU.add).then_inc(s_acc, 1)

            def ffn_in(l, f, off, uoff, m):
                u0 = START + l * UNITS + uoff
                mod_out(u0, m, 0, group_bias(m, 0))

                def body(it, width):
                    g = l * ITS + off + it
                    i = (2 * l + f) * IT_IN + it
                    lo_split(0, g + 1, width)
                    dve.wait_ge(s_used[1], g + 2)
                    dve.wait_ge(s_gread, i + 2)
                    dve.wait_ge(s_hl, i + 1)
                    tt(hf, sg, PS[:, 2:4, 0:T], ALU.mult).then_inc(s_uread, 1)
                    mod_out(u0 + 1 + it, m, 2 * it + 2, group_bias(m, 2 * it + 2))
                    lo_split(1, g + 1, width)
                    dve.wait_ge(s_hh, i + 1)
                    dve.wait_ge(s_uread, i + 2)
                    tt(hl[:, bass.ds(it * 2, 2), :], hf, hh[:, bass.ds(it * 2, 2), :].bitcast(F32),
                       ALU.subtract).then_inc(s_hl, 1)

                with dve.Fori(0, IT_IN - 1) as it:
                    body(it, W_IN)
                body(IT_IN - 1, W_OUT)

            def ffn_out(l, f, off, uoff, m, sub, n):
                ready(START + l * UNITS + (U_A if f == 0 else U_C) + 11)
                gate_ready(m, sub, 0.5)
                ch.link(v.memset(acc[:], 0.0))
                hold(dve)

                def body(it, width):
                    g = l * ITS + off + it
                    if width:
                        lo_split(0, g + 1, width)
                    if uoff is not None:
                        mod_out(START + l * UNITS + uoff + it, 1, 2 * it, group_bias(1, 2 * it))
                    if width:
                        lo_split(1, g + 1, width)
                    add_squares(4 * n + it)

                with dve.Fori(0, IT_OUT - 1) as it:
                    body(it, W_OUT)
                body(IT_OUT - 1, W_IN if uoff is not None else 0)

            def recurrence(l):
                zf = z[:, Z_F:Z_F + 2, :]
                zf1 = zf.rearrange("p a t -> p (a t)")
                zq1 = z[:, Z_Q:Z_Q + 2, :].rearrange("p a t -> p (a t)")
                dve.wait_ge(ev["e"], l + 1)
                ch.link(ts(zf, zf, 1.0, None, ALU.add))
                ch.link(v.reciprocal(zf, zf))
                for a in (0, 1):
                    last = ts(zf[:, a, :], zf[:, a, :], lbc[:, 1, a:a + 1], lbc[:, 0, a:a + 1], ALU.mult, ALU.add)
                ch.link(last)
                ts(kk, zf1, -1.0, 1.0, ALU.mult, ALU.add)
                ts(zf, zf, FMIN, None, ALU.max).then_inc(ev["f"], 1)
                dve.wait_ge(ev["g"], l + 1)
                for a in (0, 1):
                    last = v.tensor_tensor_scan(bb[:, a * T:(a + 1) * T], rset, zf[:, a, :], 0.0, ALU.mult, ALU.add)
                ch.link(last)
                for s in (0, 1):
                    for lv in range(3 * s, 3 * s + 3):
                        h = 1 << lv
                        b3 = bb.rearrange("p (n w) -> p n w", w=2 * h)
                        last = tt(LV[:, lv, :].rearrange("p (n w) -> p n w", w=2 * h), b3,
                                  b3[:, :, h - 1:h].to_broadcast([P, 2 * T // (2 * h), 2 * h]), ALU.subtract)
                    ch.link(last)
                    w = LV[:, 3 * s:3 * s + 3, :]
                    stt(w, w, -1.0, w, ALU.mult, ALU.min).then_inc(ev["d0"], 1)
                for t0, n, w in ((0, TP // CH, CH), (TP, NB, TS)):
                    b4 = bb.rearrange("p (a t) -> p a t", a=2)[:, :, t0:t0 + n * w]\
                        .rearrange("p a (n w) -> p a n w", w=w)
                    last = tt(zf[:, :, t0:t0 + n * w].rearrange("p a (n w) -> p a n w", w=w),
                              b4[:, :, :, w - 1:w].to_broadcast([P, 2, n, w]), b4, ALU.subtract)
                last.then_inc(ev["kh0"], 1)
                for s in (0, 1):
                    dve.wait_ge(ev["e0"], 2 * l + s + 1)
                    for lv in range(3 * s, 3 * s + 3):
                        h = 1 << lv
                        for side, src in ((0, kk), (1, zq1)):
                            o = LV[:, lv, :].rearrange("p (n s h) -> p n s h", s=2, h=h)[:, :, side, :]
                            last = tt(o, o, src.rearrange("p (n s h) -> p n s h", s=2, h=h)[:, :, side, :], ALU.mult)
                last.then_inc(ev["z0"], 1)
                dve.wait_ge(ev["eb"], l + 1)
                e3 = eb.rearrange("p (a t) -> p a t", a=2)
                v.tensor_copy(dec[:, :, 0:4], e3[:, :, CH - 1:TP:CH])
                ch.link(v.tensor_copy(dec[:, :, 4:12], e3[:, :, TP + TS - 1:T:TS]))
                tt(eb, eb, zq1, ALU.mult)
                dve.wait_ge(ev["ends"], l + 1)
                tt(zf1, zf1, kk, ALU.mult).then_inc(ev["kh"], 1)
                n = 0
                for h in range(4):
                    for cp in range(3):
                        rows, w = (slice(0, P), NL) if cp < 2 else (slice(0, 64), NLS)
                        dve.wait_ge(ev["gr"], 12 * l + n + 1)
                        tt(am[rows, 0:w * CH], PS[rows, 2 + n % 4, 0:w * CH], gram[rows, 0:w * CH],
                           ALU.mult).then_inc(ev["am"], 1)
                        dve.wait_ge(ev["am"], 12 * l + n + 1)
                        v.tensor_reduce(AT[rows, h, cp, :], am[rows, 0:w * CH].rearrange("p (i t) -> p t i", t=CH),
                                        AX.X, ALU.add).then_inc(ev["at"], 1)
                        n += 1
                        dve.wait_ge(ev["at"], 12 * l + n)
                dve.wait_ge(ev["ds"], l + 1)
                for par_ in (0, 1):
                    last = tt(DS[:, par_:4:2, :, :].rearrange("p c a v -> p c a v"),
                              PS[:, par_, :].rearrange("p (c a v) -> p c a v", c=2, a=2),
                              bd.unsqueeze(1).unsqueeze(1).to_broadcast([P, 2, 2, P]), ALU.mult)
                ch.link(last)
                for c in range(1, 4):
                    for a in (0, 1):
                        last = stt(DS[:, c, a, :], DS[:, c - 1, a, :], dec[:, a, c:c + 1], DS[:, c, a, :],
                                   ALU.mult, ALU.add)
                    if c < 3:
                        ch.link(last)
                last.then_inc(ev["dss"], 1)
                for h in range(4):
                    last = tt(vm[:, h], vtok[0:64, 2, 64 * h:64 * h + 64].unsqueeze(1).to_broadcast([64, NB, 64]),
                              seqm[0:64, :].unsqueeze(2).to_broadcast([64, NB, 64]), ALU.mult)
                last.then_inc(ev["vm"], 1)
                dve.wait_ge(ev["obk"], l + 1)
                dve.wait_ge(ev["oev"], 2 * l + 1)
                for e in (0, 1):
                    rows = slice(64 * e, 64 * e + 64)
                    o = z[rows, Z_Q:Z_Q + 2, TP:T]
                    last = tt(o, o, PS[rows, 4 + e, 0:128].rearrange("p (a t) -> p a t", a=2), ALU.add)
                last.then_inc(ev["oev"], 1)
                dve.wait_ge(ev["dsm"], l + 1)
                for a in (0, 1):
                    last = tt(s0[:, a], s0[:, a], dec[:, a, 4:12].unsqueeze(2).to_broadcast([P, NB, 64]), ALU.mult)
                ch.link(last)
                for a in (0, 1):
                    last = tt(s0[:, a], s0[:, a], PS[:, a, :].rearrange("p (b v) -> p b v", v=64), ALU.add)
                last.then_inc(ev["s0n"], 1)
                zo, zr = z[:, Z_Q:Z_Q + 2, :], z[:, Z_I:Z_I + 2, :]
                dve.wait_ge(ev["orr"], l + 1)
                ch.link(stt(zo, zo, par[:, R_GN:R_GN + 1], zr, ALU.mult, ALU.mult))
                tt(zo, zo, z[:, Z_G:Z_G + 2, :], ALU.mult).then_inc(ev["og"], 1)
                dve.wait_ge(ev["oh"], l + 1)
                dve.wait_ge(ev["og"], l + 1)
                tt(hml[:, 4:6, :], zo, hmh[:, 4:6, :].bitcast(F32), ALU.subtract).then_inc(ev["mixl"], 1)

            def attention(l):
                tmp = yf[:, 0:5 * T].rearrange("p (n t) -> p n t", n=5)
                dve.wait_ge(ev["rot"], l + 1)
                ch.link(tt(tmp, PS[:, 0:5, 0:T], sinT.unsqueeze(1).to_broadcast([P, 5, T]), ALU.mult))
                dve.wait_ge(ev["pc"], l + 1)
                ch.link(tt(z[:, Z_K, :], z[:, Z_K, :], tmp[:, 0, :], ALU.add))
                v.tensor_copy(kc[:, :, WIN:WIN + TS], z[:, Z_K, TP:T].rearrange("p (b t) -> p b t", t=TS))
                ch.link(tt(z[:, Z_A:Z_A + 4, :], z[:, Z_A:Z_A + 4, :], tmp[:, 1:5, :], ALU.add))
                v.tensor_copy(qs.rearrange("p b (a t) -> p a b t", t=TS), seq(z[:, Z_A:Z_A + 4, :]))\
                    .then_inc(ev["qk"], 1)
                dve.wait_ge(s_st, 32 * (l + 1))
                sink = par[:, R_SINK:R_SINK + NH].unsqueeze(2)
                v.tensor_copy(SC0[:, :, 128:129], sink)
                v.tensor_copy(SC1[:, :, 256:257], sink)
                v.tensor_copy(SS[:, :, :, 192:193],
                              par[:, R_SINKS:R_SINKS + 2].unsqueeze(2).unsqueeze(3).to_broadcast([P, 2, 2, 1]))
                dve.wait_ge(ev["sc"], l + 1)
                for n in (0, 1):
                    stt(SC0[:, 4 * n:4 * n + 4, 0:P], PS[:, 4 + n, :].rearrange("p (h k) -> p h k", h=4), SCALE,
                        mskp[:, 128:256].unsqueeze(1).to_broadcast([P, 4, P]), ALU.mult, ALU.add)
                for i in range(4):
                    last = stt(SC1[:, 2 * i:2 * i + 2, 0:256], PS[:, i, :].rearrange("p (h k) -> p h k", h=2), SCALE,
                               mskp.unsqueeze(1).to_broadcast([P, 2, 256]), ALU.mult, ALU.add)
                last.then_inc(ev["scd"], 1)
                dve.wait_ge(ev["scd"], l + 1)
                v.tensor_reduce(mx[:, 0:8], SC0, AX.X, ALU.max, negate=True)
                v.tensor_reduce(mx[:, 8:16], SC1, AX.X, ALU.max, negate=True).then_inc(ev["ex"], 1)
                dve.wait_ge(ev["ss"], l + 1)
                for n in (0, 1):
                    last = stt(SS[:, n, :, 0:192], PS[:, n, 0:384].rearrange("p (g k) -> p g k", g=2), SCALE,
                               msks, ALU.mult, ALU.add)
                ch.link(last)
                v.tensor_reduce(mx[:, 16:20], SS.rearrange("p n g k -> p (n g) k"), AX.X, ALU.max, negate=True)\
                    .then_inc(ev["sex"], 1)
                dve.wait_ge(ev["exd"], 2 * l + 1)
                ch.link(v.reciprocal(den[:, 0:16], den[:, 0:16]))
                tt(SC0[:, :, 0:P], SC0[:, :, 0:P], den[:, 0:8].unsqueeze(2).to_broadcast([P, 8, P]),
                   ALU.mult).then_inc(ev["exn"], 1)
                tt(SC1[:, :, 0:256], SC1[:, :, 0:256], den[:, 8:16].unsqueeze(2).to_broadcast([P, 8, 256]),
                   ALU.mult).then_inc(ev["ssd"], 1)
                dve.wait_ge(ev["exd"], 2 * l + 2)
                ch.link(v.reciprocal(den[:, 16:20], den[:, 16:20]))
                s3 = SS.rearrange("p n g k -> p (n g) k")[:, :, 0:192]
                tt(s3, s3, den[:, 16:20].unsqueeze(2).to_broadcast([P, 4, 192]), ALU.mult).then_inc(ev["sexn"], 1)
                for blk in (0, 1):
                    dve.wait_ge(ev["pvd"], 3 * l + blk + 1)
                    tt(hml[:, 0:4, blk * P:(blk + 1) * P], PS[:, 4 + blk, :].rearrange("p (a t) -> p a t", a=4),
                       hmh[:, 0:4, blk * P:(blk + 1) * P].bitcast(F32), ALU.subtract)
                dve.wait_ge(ev["pvd"], 3 * l + 3)
                tt(seq(hml[:, 0:4, :]), PS[:, 2, 0:256].rearrange("p (b a t) -> p a b t", a=4, t=TS),
                   seq(hmh[:, 0:4, :].bitcast(F32)), ALU.subtract).then_inc(ev["mixl"], 1)
                dve.wait_ge(ev["cst"], l + 1)
                tt(hml[:, 6:8, :], z[:, Z_CC:Z_CC + 2, :], hmh[:, 6:8, :].bitcast(F32),
                   ALU.subtract).then_inc(ev["mixl"], 1)

            dve.wait_ge(s_load, 16 * 6)
            for k in range(KT):
                v.tensor_copy(x[:, k, :], y[:, k, :]).then_inc(s_x, 1)
            ch2 = Chain(dve, s_pch2, 0)
            ch2.link(v.tensor_copy(lbt[:, 2, :], lb2[:, 0, :]))
            for d in range(1, DEPTH):
                ch2.link(tt(lbt[:, 2, :], lbt[:, 2, :], lb2[:, d, :], ALU.max))
            tt(lbt[:, 0:DEPTH, :], lb2[:], lbt[:, 2:3, :].to_broadcast([P, DEPTH, 2]), ALU.subtract)\
                .then_inc(ev["lbd"], 1)
            dve.wait_ge(ev["lbe"], 1)
            ch2.link(v.tensor_copy(lbt[:, 2, :], lbt[:, 0, :]))
            for d in range(1, DEPTH):
                ch2.link(tt(lbt[:, 2, :], lbt[:, 2, :], lbt[:, d, :], ALU.add))
            ch2.link(v.reciprocal(lbt[:, 3, :], lbt[:, 2, :]))
            ch2.link(tt(lbt[:, 0:DEPTH, :], lbt[:, 0:DEPTH, :], lbt[:, 3:4, :].to_broadcast([P, DEPTH, 2]), ALU.mult))
            ch2.link(v.tensor_copy(lbt[:, 2, :], lbt[:, 0, :]))
            for d in range(DEPTH):
                if d:
                    ch2.link(tt(lbt[:, 2, :], lbt[:, 2, :], lbt[:, d, :], ALU.add))
                ch2.link(tt(lb2[:, d, :], lbt[:, 2, :], lbt[:, 0, :], ALU.subtract))
            with dve.Fori(0, START) as u:
                mod_out(u, 2, 8 + 2 * u, par2[:, DEPTH - 1, bass.ds(R_AB + 56 + 2 * u, 2)])
            with dve.Fori(0, DEPTH) as l:
                ch.base, ch.n = l * DVE_CHAIN, 0
                for slot in (0, 1):
                    lo_split(slot, l * ITS, W_IN)
                v.tensor_copy(lbc[:, 0, :], lb2[:, l, :])
                ts(lbc[:, 1, :], lb2[:, l, :], -1.0, 1.0, ALU.mult, ALU.add)
                ch.link(v.tensor_copy(par[:], par2[:, l, :]))
                ready(START + l * UNITS - 1)
                x_norm(3 * l, 2, 0)
                ffn_in(l, 0, OFF_F0I, U_A, 0)
                ffn_out(l, 0, OFF_F0O, U_B, 0, 0, 3 * l)
                y_norm(3 * l, 0)
                x_norm(3 * l + 1, 0, 1)
                for it in range(IT_MI):
                    g = l * ITS + OFF_MI + it
                    lo_split(0, g + 1, W_IN)
                    dve.wait_ge(s_used[1], g + 2)
                    v.tensor_copy(z[:, 4 * it + 2:4 * it + 4, :], PS[:, 2:4, 0:T]).then_inc(s_zd, 1)
                    mod_out(START + l * UNITS + U_B + 4 + it, 1, 8 + 2 * it, group_bias(1, 8 + 2 * it))
                    lo_split(1, g + 1, W_IN)
                dve.wait_ge(s_zd, 5 * l + 6)
                recurrence(l)
                attention(l)
                mod_out(START + l * UNITS + U_B + 9, 1, 18, group_bias(1, 18))
                ready(START + l * UNITS + U_B + 3)
                gate_ready(1, 1, 1.0)
                ch.link(v.memset(acc[:], 0.0))
                for it in range(IT_MO):
                    g = l * ITS + OFF_MO + it
                    n = 12 * l + 4 + 2 * it
                    lo_split(0, g + 1, W_IN)
                    add_squares(n)
                    mod_out(START + l * UNITS + U_B + 10 + it, 1, 20 + 2 * it, group_bias(1, 20 + 2 * it))
                    lo_split(1, g + 1, W_IN)
                    add_squares(n + 1)
                y_norm(3 * l + 1, 1)
                ready(START + l * UNITS + U_B + 11)
                x_norm(3 * l + 2, 1, 2)
                ffn_in(l, 1, OFF_F1I, U_C, 2)
                ffn_out(l, 1, OFF_F1O, None, 2, 2, 3 * l + 2)
                y_norm(3 * l + 2, 2)
                assert ch.n == DVE_CHAIN, ch.n

        @block.gpsimd
        def _(pool):
            g_ = nc.gpsimd
            tt = g_.tensor_tensor
            ch = Chain(pool, s_pch, POOL_CHAIN)
            for s in (*s_hi, *s_lo, *s_used, s_part, s_adp, s_adt, s_mod, s_gread, s_uread, s_hl,
                      s_sqp, s_acc, s_za, s_zd):
                pool.sem_inc(s, 1)
            g_.memset(cT[:, :, NS:32], 0.0).then_inc(ev["kvo"], 1)

            def conv(l):
                zc, zh, zb = (z[:, a:a + 2, :] for a in (Z_CC, Z_CH, Z_B))

                def rows(t, start, width):
                    return t[:, :, TP + 2:SEG].rearrange("p a (b w) -> p a b w", w=TS + 2)[:, :, :, start:start + width]

                def seqs(t):
                    return t[:, :, TP:T].rearrange("p a (b t) -> p a b t", t=TS)

                pool.wait_ge(s_zd, 5 * l + 6)
                tt(rows(up, 2, TS), seqs(zc), seqs(zh), ALU.mult)
                ch.link(tt(up[:, :, 2:TP + 2], zc[:, :, 0:TP], zh[:, :, 0:TP], ALU.mult))
                hold(pool)
                g_.memset(up[:, :, 0:2], 0.0)
                g_.tensor_copy(rows(up, 0, 2), cpv[:, l, :].rearrange("p (a b t) -> p a b t", a=2, t=2))
                g_.tensor_copy(cso[:, :, 0, :], up[:, :, TP:TP + 2])
                last = g_.tensor_copy(cso[:, :, 1:NS, :], rows(up, TS, 2))
                ch.link(last)
                for j in range(3):
                    w = par[:, R_CW + 2 * j:R_CW + 2 * j + 2]
                    out = zc if j == 0 else zh
                    tt(out[:, :, 0:TP], up[:, :, j:TP + j], w.unsqueeze(2).to_broadcast([P, 2, TP]), ALU.mult)
                    ch.link(tt(seqs(out), rows(up, j, TS), w.unsqueeze(2).unsqueeze(3).to_broadcast([P, 2, NB, TS]),
                               ALU.mult))
                    if j:
                        ch.link(tt(zc, zc, zh, ALU.add))
                tt(zc, zc, zb, ALU.mult).then_inc(ev["cv"], 1)

            with pool.Fori(0, DEPTH) as l:
                ch.base, ch.n = l * POOL_CHAIN, 0
                conv(l)
                pool.wait_ge(ev["rot"], l + 1)
                tt(z[:, Z_K, :], z[:, Z_K, :], cosT, ALU.mult)
                tt(z[:, Z_A:Z_A + 4, :], z[:, Z_A:Z_A + 4, :], cosT.unsqueeze(1).to_broadcast([P, 4, T]),
                   ALU.mult).then_inc(ev["pc"], 1)
                assert ch.n == POOL_CHAIN, ch.n


def laid_out(i):
    c = np.ascontiguousarray

    def cols(a):
        a = a.reshape(*a.shape[:-1], a.shape[-1] // P, P)
        return np.moveaxis(a, (-1, -2), (0, 1))

    x = np.concatenate([i["x_prompt"][0], i["x_sample"].reshape(NB * TS, D)])
    cond = np.concatenate([i["c_prompt"], i["c_sample"]])

    def units(w):
        *lead, rows, n = w.shape
        w = w.reshape(*lead, rows // P, P, n // 256, 256)
        w = np.moveaxis(w, -2, -4)
        w = np.swapaxes(w, -3, -2)
        return w.reshape(*lead, n // 256, P, rows // P * 256)

    w_in = i["ffn_w_in"]
    gate, upw = units(w_in[..., :DFF]), units(w_in[..., DFF:])
    w_in = np.stack([gate, upw], axis=3).reshape(DEPTH, 2, 2 * IT_IN, P, W_IN)
    w_out = units(i["ffn_w_out"]).reshape(DEPTH, 2, 4, P, 2, W_OUT)
    w_out = np.swapaxes(w_out, 3, 4).reshape(DEPTH, 2, 8, P, W_OUT)
    heads = np.arange(NH * HD).reshape(NKV, NG, HD).transpose(1, 0, 2).ravel()
    at = 0
    part = {}
    for name, n in (("q", 512), ("k", 128), ("v", 128), ("qh", 256), ("f", 256), ("i", 256), ("g", 256),
                    ("b", 256), ("c", 256), ("h", 256)):
        part[name] = at + np.arange(n)
        at += n
    part["q"] = part["q"][heads]
    order = np.concatenate([part[n] for n in ("f", "qh", "i", "k", "v", "q", "c", "h", "g", "b")])
    m_in = units(i["mix_w_in"][:, :, order])
    rows = np.concatenate([heads, 512 + np.arange(512)])
    m_out = units(i["mix_w_out"][:, rows, :])
    ada = units(i["ada_w"])
    ada = np.concatenate([ada[:, 8:36], np.roll(ada[:, 0:8], -1, axis=0)], axis=1)
    ab = np.concatenate([i["ada_b"][:, 2048:], np.roll(i["ada_b"][:, :2048], -1, axis=0)], axis=1)
    par = np.empty((DEPTH, P, NR), np.float32)
    par[:, :, R_AB:R_AB + 72] = ab.reshape(DEPTH, 72, P).transpose(0, 2, 1)
    par[:, :, R_PRE:R_PRE + 24] = i["norm_pre"].reshape(DEPTH, 24, P).transpose(0, 2, 1)
    par[:, :, R_POST:R_POST + 24] = i["norm_post"].reshape(DEPTH, 24, P).transpose(0, 2, 1)
    par[:, :, R_SINK:R_SINK + NH] = i["attn_sinks"][:, None, :]
    t = np.arange(P) % 32 // TS
    for n in range(NKV):
        par[:, :, R_SINKS + n] = i["attn_sinks"][:, n * NG + t]
    par[:, :, R_GN] = np.tile(i["hgrn_gnorm"], (1, 2))
    par[:, :, R_CW:R_CW + 6] = i["conv_w"].reshape(DEPTH, 6, P).transpose(0, 2, 1)
    return {
        "x": c(cols(x)), "c": c(cols(cond)), "cst": constants(), "par": par,
        "lb": c(i["hgrn_lower_bounds"].reshape(DEPTH, 2, P).transpose(2, 0, 1)),
        "cprev": c(i["state_conv"].reshape(DEPTH, NB, 2, 2, P).transpose(4, 0, 3, 1, 2).reshape(P, DEPTH, 32)),
        "k": c(i["cache_k_win"].reshape(DEPTH, NB, WIN, P).transpose(0, 3, 1, 2)),
        "v": c(i["cache_v_win"].reshape(DEPTH, NB, WIN, P).transpose(0, 2, 1, 3)),
        "s": c(i["state_hgrn"].reshape(DEPTH, NB, 2, P, 64).transpose(0, 3, 2, 1, 4)),
        "w_in": c(w_in), "w_out": c(w_out), "m_in": c(m_in), "m_out": c(m_out), "ada_w": c(ada),
    }


OUTS = {
    "x": (P, KT, T), "kp": (DEPTH, P, WIN), "vp": (DEPTH, WIN, P), "sp": (DEPTH, 2, 64, 2, 64),
    "conv": (DEPTH, P, 2, NS, 2), "ks": (DEPTH, P, NB, WIN), "vs": (DEPTH, WIN, NB, P),
    "vn": (DEPTH, NB * TS, P), "ss": (DEPTH, P, 2, NB, 64),
}


def returned(r):
    x = r["x"].transpose(2, 1, 0).reshape(T, D)
    conv = r["conv"].transpose(0, 3, 4, 2, 1).reshape(DEPTH, NS, 2, 256)
    vs = np.concatenate([r["vs"][:, :WIN - TS].transpose(0, 2, 1, 3), r["vn"].reshape(DEPTH, NB, TS, P)], axis=2)
    return (
        x[None, :TP], x[TP:].reshape(NB, TS, D),
        r["kp"].transpose(0, 2, 1).reshape(DEPTH, 1, WIN, NKV, HD), r["vp"].reshape(DEPTH, 1, WIN, NKV, HD),
        r["sp"].transpose(0, 3, 1, 2, 4).reshape(DEPTH, 1, 4, 64, 64), conv[:, :1],
        r["ks"].transpose(0, 2, 3, 1).reshape(DEPTH, NB, WIN, NKV, HD), vs.reshape(DEPTH, NB, WIN, NKV, HD),
        r["ss"].reshape(DEPTH, 2, 64, 2, NB, 64).transpose(0, 4, 3, 1, 2, 5).reshape(DEPTH, NB, 4, 64, 64),
        conv[:, 1:],
    )


def kernel(**inputs):
    import concourse.bacc as bacc
    from concourse.bass_utils import run_bass_kernel_spmd

    arrays = laid_out({k: np.asarray(v) for k, v in inputs.items()})
    nc = bacc.Bacc("TRN2", target_bir_lowering=False, num_devices=1)
    A = {k: nc.dram_tensor("in_" + k, a.shape, F32, kind="ExternalInput").ap() for k, a in arrays.items()}
    O = {k: nc.dram_tensor("out_" + k, s, F32, kind="ExternalOutput").ap() for k, s in OUTS.items()}
    trunk(nc, A, O)
    r = run_bass_kernel_spmd(nc, [{"in_" + k: a for k, a in arrays.items()}], core_ids=[0]).results[0]
    return tuple(np.ascontiguousarray(a) for a in returned({k: r["out_" + k] for k in OUTS}))
```

```python
from contextlib import ExitStack

import numpy as np

import concourse.bass as bass
from concourse import mybir

F32 = mybir.dt.float32
F32R = mybir.dt.float32r
ACT = mybir.ActivationFunctionType
ALU = mybir.AluOpType
AX = mybir.AxisListType

P = 128
D = 1024
KT = D // P
DEPTH = 2
TP, NB, TS = 256, 8, 8
T = TP + NB * TS
NS = 1 + NB
DFF = 2816
FT = DFF // P
NH, NKV, HD, WIN = 8, 2, 64, 128
NG = NH // NKV
PAST = 2048
THETA = 10000.0
EPS = 1e-6
NEG = -1e30
SCALE = HD ** -0.5
FMIN = 2.0 ** -63

IT_IN, IT_OUT, IT_MI, IT_MO = 11, 4, 5, 2
W_IN, W_OUT = KT * 256, (FT // 2) * 256
OFF_F0I = 0
OFF_F0O = OFF_F0I + IT_IN
OFF_MI = OFF_F0O + IT_OUT
OFF_MO = OFF_MI + IT_MI
OFF_F1I = OFF_MO + IT_MO
OFF_F1O = OFF_F1I + IT_IN
ITS = OFF_F1O + IT_OUT

START = 8
UNITS = 36
U_A, U_B, U_C = 0, 12, 24

Z_F, Z_Q, Z_I, Z_K, Z_V, Z_A, Z_CC, Z_CH, Z_G, Z_B = 0, 2, 4, 6, 7, 8, 12, 14, 16, 18
NZ = 20
DIAG = -1
LEVELS = [0, 1, 2, DIAG, 3, 4, 5]
NL = len(LEVELS)
NLS = 4
CH = 64

C_ID, C_ROT, C_ONE, C_BD, C_SEL = 0, 128, 256, 384, 512
C_COS = 528
C_SIN = C_COS + T
C_MP = C_SIN + T
C_MS = C_MP + 256
C_GR = C_MS + 2 * 192
C_SQ = C_GR + NL * CH
C_RS = C_SQ + NB
NC_ = C_RS + T

R_AB, R_PRE, R_POST, R_SINK, R_SINKS, R_GN, R_CW = 0, 72, 96, 120, 128, 130, 131
NR = 137

ACT_CHAIN = 7
DVE_CHAIN = 52
POOL_CHAIN = 10

SUMMED = 5
MIXER_UNITS = 15
SEG = TP + 2 + NB * (TS + 2)


def constants():
    c = np.zeros((P, NC_), np.float32)
    i = np.arange(P)
    c[i, C_ID + i] = 1
    lo = i % HD < HD // 2
    c[(i + 32)[lo], C_ROT + i[lo]] = -1
    c[(i - 32)[~lo], C_ROT + i[~lo]] = 1
    c[:, C_ONE:C_ONE + P] = 1
    c[:, C_BD:C_BD + P] = (i[:, None] // 64 == i[None, :] // 64)
    for j in range(4):
        for s in range(NS):
            c[32 * j + s, C_SEL + s] = 1
    half = HD // 2
    inv = np.power(np.float32(THETA), -np.arange(half, dtype=np.float32) / np.float32(half)).astype(np.float32)
    pos = np.concatenate([np.arange(TP), np.tile(PAST + np.arange(TS), NB)]).astype(np.float32)
    ang = (pos[None, :] * inv[i % half][:, None]).astype(np.float32)
    c[:, C_COS:C_COS + T] = np.cos(ang)
    c[:, C_SIN:C_SIN + T] = np.sin(ang)
    k = np.arange(256)[None, :]
    c[:, C_MP:C_MP + 256] = np.where((k > i[:, None]) & (k <= i[:, None] + 128), 0, NEG)
    tok = i % TS
    for hi in range(2):
        m = np.full((P, 192), NEG, np.float32)
        m[:, :128] = np.where(np.arange(128)[None, :] > tok[:, None], 0, NEG)
        b = 4 * hi + i // 32
        n = np.arange(64)[None, :]
        m[:, 128:] = np.where((n // TS == b[:, None]) & (n % TS <= tok[:, None]), 0, NEG)
        c[:, C_MS + 192 * hi:C_MS + 192 * (hi + 1)] = m
    s, t = (i % CH)[:, None], np.arange(CH)[None, :]
    for n, lv in enumerate(LEVELS):
        h = 1 << max(lv, 0)
        m = (s == t) if lv == DIAG else (s // (2 * h) == t // (2 * h)) & (s % (2 * h) < h) & (t % (2 * h) >= h)
        c[:, C_GR + n * CH:C_GR + (n + 1) * CH] = m
    c[:, C_SQ:C_SQ + NB] = (i[:, None] // TS == np.arange(NB)[None, :])
    r = np.ones(T, np.float32)
    r[0:TP:CH] = 0
    r[TP::TS] = 0
    c[:, C_RS:C_RS + T] = r
    return c


def trunk(nc, A, O):
    ctx = ExitStack()
    with ctx:
        def sb(name, shape, dt=F32):
            return ctx.enter_context(nc.sbuf_tensor(name, shape, dt))

        def sem(name):
            return ctx.enter_context(nc.semaphore(name))

        x = sb("x", [P, KT, T])
        y = sb("y", [P, KT, T])
        sq = sb("sq", [P, KT, T])
        hmh = sb("hmh", [P, KT, T], F32R)
        hml = sb("hml", [P, KT, T], F32R)
        raw = sb("raw", [P, 2, W_OUT])
        WHI = sb("WHI", [P, 2, W_OUT], F32R)
        WLO = sb("WLO", [P, 2, W_OUT], F32R)
        ada = sb("ada", [P, 2, 1024])
        cst = sb("cst", [P, NC_])
        par2 = sb("par2", [P, DEPTH, NR])
        par = sb("par", [P, NR])
        lb2 = sb("lb2", [P, DEPTH, 2])
        lbt = sb("lbt", [P, 4, 2])
        lbc = sb("lbc", [P, 2, 2])
        cpv = sb("cpv", [P, DEPTH, 2 * NB * 2])
        cso = sb("cso", [P, 2, NS, 2])
        cT = sb("cT", [P, KT, 32])
        adp = sb("adp", [P, 256])
        mod = [sb(f"mod{g}", [P, 24, NS]) for g in "ABC"]
        rt = sb("rt", [P, T])
        rst = sb("rst", [P, T])
        rst2 = sb("rst2", [P, T])
        acc = sb("acc", [P, T])
        pre = sb("pre", [P, KT, NB, TS])
        dec = sb("dec", [P, 2, 12])
        mx = sb("mx1", [P, 20])
        den = sb("den", [P, 20])
        with ExitStack() as ffn_scope:
            hh = ffn_scope.enter_context(nc.sbuf_tensor("hh", [P, FT, T], F32R))
            hl = ffn_scope.enter_context(nc.sbuf_tensor("hl", [P, FT, T], F32R))
        z = sb("z", [P, NZ, T])
        kc = sb("kc", [P, NB, WIN + TS])
        vc = sb("vc", [P, NB, P])
        s0 = sb("s0", [P, 2, NB, 64])
        big = sb("big", [P, 4920])
        PS = ctx.enter_context(nc.psum_tensor("PS", [P, 8, 512], F32))

        sg = y[:, 0:2, :]
        hf = y[:, 2:4, :]
        yf = y[:, :, :].rearrange("p a b -> p (a b)")
        sf = sq[:, :, :].rearrange("p a b -> p (a b)")
        kk, bb, eb = yf[:, 0:640], yf[:, 640:1280], yf[:, 1280:1920]
        am = yf[:, 1920:1920 + NL * CH]
        it_, kt_, at_ = (sf[:, n * 768:(n + 1) * 768] for n in range(3))
        zfl = z[:, :, :].rearrange("p a b -> p (a b)")
        first = [zfl[:, 0:2048], zfl[:, 2048:4096], zfl[:, 4096:6144], big[:, 0:2048], big[:, 2048:4096],
                 yf[:, 0:2048], ada[:, :, :].rearrange("p a b -> p (a b)"), zfl[:, 0:2048]]
        vtok = it_.rearrange("p (a b) -> p a b", a=3)
        ktok = kt_.rearrange("p (a b) -> p a b", a=3)
        AT = at_.rearrange("p (h c t) -> p h c t", h=4, c=3)
        LV = big[:, 0:3840].rearrange("p (l a t) -> p l (a t)", l=6, a=2)
        DS = big[:, 0:1024].rearrange("p (c a v) -> p c a v", c=4, a=2)
        vm = big[0:64, 1024:3072].rearrange("p (h b v) -> p h b v", h=4, b=NB)
        SC0 = big[:, 0:8 * 129].rearrange("p (h k) -> p h k", h=8)
        SC1 = big[:, 1032:3088].rearrange("p (h k) -> p h k", h=8)
        SS = big[:, 3088:3860].rearrange("p (n g k) -> p n g k", n=2, g=2)
        va = big[:, 3860:4244].rearrange("p (a b) -> p a b", a=3)
        up = big[:, 4244:4920].rearrange("p (a t) -> p a t", a=2)
        PT = yf[:, 0:2048].rearrange("p (s t) -> p s t", s=4)
        qs = yf[:, 1600:1856].rearrange("p (b r) -> p b r", b=NB)
        PC = sf[:, 0:512]
        PN = sf[0:64, 512:1024]

        ident = cst[:, C_ID:C_ID + P]
        rotm = cst[:, C_ROT:C_ROT + P]
        ones = cst[:, C_ONE:C_ONE + P]
        bd = cst[:, C_BD:C_BD + P]
        sel = cst[:, C_SEL:C_SEL + NS]
        cosT = cst[:, C_COS:C_COS + T]
        sinT = cst[:, C_SIN:C_SIN + T]
        mskp = cst[:, C_MP:C_MP + 256]
        msks = cst[:, C_MS:C_MS + 384].rearrange("p (g k) -> p g k", g=2)
        gram = cst[:, C_GR:C_GR + NL * CH]
        seqm = cst[:, C_SQ:C_SQ + NB]
        rset = cst[:, C_RS:C_RS + T]

        s_load = sem("s_load")
        s_late = sem("s_late")
        s_xin = sem("s_xin")
        s_first = [sem(f"s_first{i}") for i in range(START)]
        s_raw = [sem(f"s_raw{i}") for i in (0, 1)]
        s_hi = [sem(f"s_hi{i}") for i in (0, 1)]
        s_lo = [sem(f"s_lo{i}") for i in (0, 1)]
        s_used = [sem(f"s_used{i}") for i in (0, 1)]
        s_ada = [sem(f"s_ada{i}") for i in (0, 1)]
        s_part = sem("s_part")
        s_adp = sem("s_adp")
        s_adt = sem("s_adt")
        s_mod = sem("s_mod")
        s_c = sem("s_c")
        s_gread = sem("s_gread")
        s_uread = sem("s_uread")
        s_hh = sem("s_hh")
        s_hl = sem("s_hl")
        s_sqp = sem("s_sqp")
        s_sqd = sem("s_sqd")
        s_acc = sem("s_acc")
        s_acc0 = sem("s_acc0")
        s_pst = sem("s_pst")
        s_pr = sem("s_pr")
        s_x = sem("s_x")
        s_xs = sem("s_xs")
        s_sqx = sem("s_sqx")
        s_sqa = sem("s_sqa")
        s_xst = sem("s_xst")
        s_r = sem("s_r")
        s_pre = sem("s_pre")
        s_mt = sem("s_mt")
        s_hmh = sem("s_hmh")
        s_hml = sem("s_hml")
        s_ms = sem("s_ms")
        s_hms = sem("s_hms")
        s_hls = sem("s_hls")
        s_za = sem("s_za")
        s_zd = sem("s_zd")
        s_cache = sem("s_cache")
        s_out = sem("s_out")
        s_st = sem("s_st")
        s_rt0 = sem("s_rt0")
        s_ach = sem("s_ach")
        s_dch = sem("s_dch")
        s_pch = sem("s_pch")
        s_held = sem("s_held")
        s_pch2 = sem("s_pch2")
        ev = {}
        for n in ("e f g b d0 e0 z0 ends eb kh0 kh itp it ktp kt gr am ds dss obk oev osq ost orr og oh "
                  "vm dsm s0n rot qk vtp vt sc scd ex exn pt ptd pv pvd ss ssd sex sexn spt sptd spv spvd "
                  "cv cst mixl kvo exd at lbd lbe pc gs d35 zl vtok dec").split():
            ev[n] = sem("e_" + n)

        WIN_ = A["w_in"].rearrange("l f u p n -> (l f u) p n")
        WOUT = A["w_out"].rearrange("l f u p n -> (l f u) p n")
        MIN_ = A["m_in"].rearrange("l u p n -> (l u) p n")
        MOUT = A["m_out"].rearrange("l u p n -> (l u) p n")
        ADA = A["ada_w"].rearrange("l u p n -> (l u) p n")

        class Chain:

            def __init__(self, eng, s, per_layer):
                self.eng, self.s, self.per, self.base, self.n = eng, s, per_layer, 0, 0

            def mark(self, ins):
                self.n += 1
                ins.then_inc(self.s, 1)
                return self.base + self.n

            def wait(self, value):
                self.eng.wait_ge(self.s, value)

            def link(self, ins):
                self.wait(self.mark(ins))

        def by_seq(t, k0):
            return t[:, k0:k0 + KT, 1:NS].unsqueeze(3).to_broadcast([P, KT, NB, TS])

        def seq(t):
            return t[:, :, TP:T].rearrange("p k (b t) -> p k b t", t=TS)

        def hold(eng):
            eng.sem_inc(s_held, 1)

        block = ctx.enter_context(nc.Block())

        @block.sync
        def _(sp):
            sp.dma_start(cT[:, :, 0:NS], A["c"]).then_inc(s_load, 16)
            sp.dma_start(cst[:, 0:C_COS], A["cst"][:, 0:C_COS]).then_inc(s_load, 16)
            sp.dma_start(par2[:], A["par"].rearrange("l p n -> p l n")).then_inc(s_load, 16)
            sp.dma_start(lb2[:], A["lb"]).then_inc(s_load, 16)
            for u in range(START):
                if u == 2:
                    sp.dma_start(x[:], A["x"]).then_inc(s_xin, 16)
                if u == START - 1:
                    sp.wait_ge(s_part, 2)
                sp.dma_start(first[u], ADA[(DEPTH - 1) * UNITS + U_C + 4 + u]).then_inc(s_first[u], 16)

            def conditioning(u, src):
                sp.wait_ge(s_part, u + 1)
                for half in (0, 1):
                    sp.dma_start(ada[:, half, :], src[:, 1024 * half:1024 * (half + 1)]).then_inc(s_ada[half], 16)

            def weights(g, slot, src, width):
                sp.wait_ge(s_hi[slot], g + 1)
                sp.wait_ge(s_lo[slot], g + 1)
                sp.dma_start(raw[:, slot, 0:width], src).then_inc(s_raw[slot], 16)

            def unit(l, u):
                conditioning(START + l * UNITS + u, ADA[l * UNITS + u])

            def ffn_in(l, f, off, uoff):
                def both(it):
                    for slot in (0, 1):
                        weights(l * ITS + off + it, slot, WIN_[(l * 2 + f) * 2 * IT_IN + it * 2 + slot], W_IN)

                both(0)
                if uoff is not None:
                    unit(l, uoff)
                    unit(l, uoff + 1)
                with sp.Fori(1, IT_IN) as it:
                    both(it)
                    if uoff is not None:
                        unit(l, uoff + 1 + it)

            def ffn_out(l, f, off, uoff):
                with sp.Fori(0, IT_OUT) as it:
                    for slot in (0, 1):
                        weights(l * ITS + off + it, slot, WOUT[(l * 2 + f) * 2 * IT_OUT + it * 2 + slot], W_OUT)
                    if uoff is not None:
                        unit(l, uoff + it)

            sp.dma_start(cst[:, C_COS:NC_], A["cst"][:, C_COS:NC_]).then_inc(s_late, 16)
            sp.dma_start(cpv[:], A["cprev"]).then_inc(s_late, 16)
            with sp.Fori(0, DEPTH) as l:
                ffn_in(l, 0, OFF_F0I, U_A)
                ffn_out(l, 0, OFF_F0O, U_B)
                for it in range(IT_MI):
                    for slot in (0, 1):
                        weights(l * ITS + OFF_MI + it, slot, MIN_[l * 2 * IT_MI + it * 2 + slot], W_IN)
                    unit(l, U_B + 4 + it)
                    if it == 0:
                        sp.wait_ge(s_used[1], l * ITS + OFF_MI + 1)
                        sp.dma_start(kc[:, :, 0:WIN], A["k"][l]).then_inc(s_cache, 16)
                        sp.dma_start(vc[:], A["v"][l]).then_inc(s_cache, 16)
                        sp.dma_start(s0[:], A["s"][l]).then_inc(s_cache, 16)
                for it in range(IT_MO):
                    for slot in (0, 1):
                        weights(l * ITS + OFF_MO + it, slot, MOUT[l * 2 * IT_MO + it * 2 + slot], W_IN)
                    for s in range(MIXER_UNITS):
                        if (s > 0) == it:
                            unit(l, U_B + 9 + s)
                ffn_in(l, 1, OFF_F1I, None)
                ffn_out(l, 1, OFF_F1O, None)
            sp.wait_ge(s_x, KT * (3 * DEPTH + 1))
            sp.wait_ge(s_xs, 3 * DEPTH + 1)
            sp.dma_start(O["x"], x[:]).then_inc(s_out, 16)
            sp.wait_ge(s_out, 16 * (1 + 7 * DEPTH))
            sp.wait_ge(s_st, 32 * DEPTH)

        @block.tensor
        def _(pe):
            mm = nc.tensor.matmul

            def mm3(out, slot, col, rhi, rlo, first, last):
                hi, lo = WHI[:, slot, col:col + P], WLO[:, slot, col:col + P]
                mm(out, hi, rhi, start=first, stop=False)
                mm(out, hi, rlo, start=False, stop=False)
                return mm(out, lo, rhi, start=False, stop=last)

            def partial(u, src=None):
                if src is None:
                    pe.wait_ge(s_ada[0], 16 * (u - START + 1))
                    pe.wait_ge(s_ada[1], 16 * (u - START + 1))
                    src = first[6]
                else:
                    pe.wait_ge(s_first[u], 16)
                pe.wait_ge(s_adp, u + 1)
                for i in (0, 1):
                    for j in range(4):
                        k = 2 * j + i
                        last = mm(PS[32 * j:32 * j + 32, 6, 0:256], cT[:, k, :], src[:, k * 256:(k + 1) * 256],
                                  start=(i == 0), stop=(i == 1))
                last.then_inc(s_part, 1)

            def summed(u):
                pe.wait_ge(s_adp, u + 2)
                pe.wait_ge(s_mod, u + 1)
                for i in (0, 1):
                    last = mm(PS[:, 7, 16 * i:16 * i + NS], adp[:, i * P:(i + 1) * P], sel, start=True, stop=True)
                last.then_inc(s_adt, 1)

            def split_ready(slot, g):
                pe.wait_ge(s_hi[slot], g + 2)
                pe.wait_ge(s_lo[slot], g + 2)

            def pair(slot, bank, norm=None, hook=None):
                if norm is not None:
                    pe.wait_ge(s_hls, norm + 1)
                for t in (0, 1):
                    for k in range(KT):
                        if norm is not None and t == 0:
                            pe.wait_ge(s_hml, KT * norm + k + 1)
                        last = mm3(PS[:, bank + t, 0:T], slot, k * 256 + t * P, hmh[:, k, :], hml[:, k, :],
                                   k == 0, k == KT - 1)
                        if hook:
                            hook(t * KT + k)
                last.then_inc(s_used[slot], 1)

            def x_stats(n):
                for k in range(SUMMED):
                    pe.wait_ge(s_sqx, KT * n + k + 1)
                    mm(PS[:, 5, 0:T], ones, sq[:, k, :], start=(k == 0), stop=False)
                pe.wait_ge(s_sqa, 2 * (n + 1))
                mm(PS[:, 5, 0:T], ones, sq[:, SUMMED, :], start=False, stop=True).then_inc(s_xst, 1)

            def y_stats(n, bank):
                pe.wait_ge(s_acc, 4 * n + 5)
                mm(PS[:, bank, 0:T], ones, acc[:], start=True, stop=True).then_inc(s_pst, 1)

            def ffn_in(l, f, off, uoff):
                if uoff is not None:
                    u0 = START + l * UNITS + uoff
                    partial(u0)

                def body(it, n=None):
                    g = l * ITS + off + it
                    split_ready(0, g)
                    pe.wait_ge(s_gread, (2 * l + f) * IT_IN + it + 1)
                    pair(0, 0, n)
                    if uoff is not None:
                        summed(u0 + it)
                        partial(u0 + 1 + it)
                    split_ready(1, g)
                    pe.wait_ge(s_uread, (2 * l + f) * IT_IN + it + 1)
                    pair(1, 2)

                body(0, 3 * l + 2 * f)
                hold(pe)
                with pe.Fori(1, IT_IN) as it:
                    body(it)
                if uoff is not None:
                    summed(u0 + IT_IN)

            def ffn_out(l, f, off, uoff):
                pe.wait_ge(s_hl, (2 * l + f) * IT_IN + (FT // 2 + 1) // 2 + 1)
                hold(pe)
                with pe.Fori(0, IT_OUT) as it:
                    g = l * ITS + off + it
                    if uoff is not None:
                        partial(START + l * UNITS + uoff + it)
                    pe.wait_ge(s_sqp, 4 * (3 * l + 2 * f) + it + 1)
                    for slot in (0, 1):
                        split_ready(slot, g)
                        if slot:
                            pe.wait_ge(s_hl, (2 * l + f + 1) * IT_IN + 1)
                        for t in (0, 1):
                            for i in range(FT // 2):
                                k = slot * (FT // 2) + i
                                last = mm3(PS[:, 4 + t, 0:T], slot, i * 256 + t * P, hh[:, k, :], hl[:, k, :],
                                           k == 0, k == FT - 1)
                        last.then_inc(s_used[slot], 1)
                    if uoff is not None:
                        summed(START + l * UNITS + uoff + it)

            def turn(src, bank, done):
                for t in range(3):
                    for a in (0, 1):
                        w = P if t < 2 else NB * TS
                        out = PS[0:w, bank + t // 2, (t % 2) * 256 + a * P:(t % 2) * 256 + (a + 1) * P]
                        last = nc.tensor.transpose(out, src(a)[:, t * P:t * P + w], ident)
                last.then_inc(done, 1)

            def between(l, s):
                u = START + l * UNITS + U_B + 9 + s
                if s:
                    summed(u - 1)
                if s < MIXER_UNITS:
                    partial(u)

            def recurrence(l):
                pe.wait_ge(s_za, 5 * l + 6)
                turn(lambda a: z[:, Z_I + a, :], 0, ev["itp"])
                for s in range(4):
                    between(l, s)
                pe.wait_ge(ev["z0"], l + 1)
                n = 0
                for h in range(4):
                    a, e = h // 2, h % 2
                    rows = slice(64 * e, 64 * e + 64)
                    for cp in range(3):
                        bank = 2 + n % 4
                        if n in (4, 8):
                            between(l, n // 4 + 3)
                        if n >= 4:
                            pe.wait_ge(ev["am"], 12 * l + n - 3)
                        hold(pe)
                        for c in ((2 * cp, 2 * cp + 1) if cp < 2 else (4,)):
                            col = a * T + c * CH
                            for i, lv in enumerate(LEVELS[:NL if cp < 2 else NLS]):
                                if lv == DIAG:
                                    left, right = kk[rows, col:col + CH], z[rows, Z_Q + a, c * CH:(c + 1) * CH]
                                else:
                                    left = right = LV[rows, lv, col:col + CH]
                                p0 = 64 * (c % 2)
                                last = mm(PS[p0:p0 + 64, bank, i * CH:(i + 1) * CH], left, right,
                                          start=True, stop=True)
                        last.then_inc(ev["gr"], 1)
                        n += 1
                pe.wait_ge(ev["kh"], l + 1)
                pe.wait_ge(ev["it"], l + 1)
                turn(lambda a: z[:, Z_F + a, :], 0, ev["ktp"])
                between(l, 6)
                pe.wait_ge(ev["kt"], l + 1)
                hold(pe)
                for c in range(4):
                    rows = slice(64 * (c % 2), 64 * (c % 2) + 64)
                    for a in (0, 1):
                        last = mm(PS[:, c % 2, (c // 2) * 256 + a * P:(c // 2) * 256 + (a + 1) * P],
                                  ktok[rows, c // 2, a * P:(a + 1) * P], vtok[rows, c // 2, a * P:(a + 1) * P],
                                  start=True, stop=True)
                last.then_inc(ev["ds"], 1)
                between(l, 7)
                pe.wait_ge(ev["dss"], l + 1)
                pe.wait_ge(ev["at"], 12 * (l + 1))
                hold(pe)
                for c in range(5):
                    rows = slice(64 * (c % 2), 64 * (c % 2) + 64)
                    for a in (0, 1):
                        w = 3 if c % 2 == 0 else 2
                        col = (a * w + c // 2) * CH
                        if 0 < c < 4:
                            mm(PS[:, 2 + c % 2, col:col + CH], DS[:, c - 1, a, :],
                               eb[:, a * T + c * CH:a * T + (c + 1) * CH], start=True, stop=False)
                        for e in (0, 1):
                            last = mm(PS[64 * e:64 * e + 64, 2 + c % 2, col:col + CH],
                                      vtok[rows, c // 2, a * P + 64 * e:a * P + 64 * e + 64],
                                      AT[rows, 2 * a + e, c // 2, :], start=(c in (0, 4)), stop=True)
                pe.wait_ge(s_cache, 48 * (l + 1))
                hold(pe)
                for e in (0, 1):
                    rows = slice(64 * e, 64 * e + 64)
                    for a in (0, 1):
                        for b in range(NB):
                            col = a * T + TP + TS * b
                            last = mm(PS[rows, 4 + e, a * 64 + TS * b:a * 64 + TS * (b + 1)],
                                      s0[rows, a, b, :], eb[rows, col:col + TS], start=True, stop=True)
                last.then_inc(ev["obk"], 1)
                between(l, 8)
                pe.wait_ge(ev["vm"], l + 1)
                hold(pe)
                for h in range(4):
                    a, e = h // 2, h % 2
                    last = mm(PS[64 * e:64 * e + 64, a, :], ktok[0:64, 2, 64 * h:64 * h + 64],
                              vm[:, h].rearrange("p b v -> p (b v)"), start=True, stop=True)
                last.then_inc(ev["dsm"], 1)
                between(l, 9)
                pe.wait_ge(ev["osq"], l + 1)
                for a in (0, 1):
                    last = mm(PS[:, 2 + a, 0:T], bd, z[:, Z_I + a, :], start=True, stop=True)
                last.then_inc(ev["ost"], 1)

            def attention(l):
                between(l, 10)
                pe.wait_ge(ev["s0n"], l + 1)
                for n, t in enumerate((Z_K, Z_A, Z_A + 1, Z_A + 2, Z_A + 3)):
                    if n == 2:
                        pe.wait_ge(ev["orr"], l + 1)
                    if n == 4:
                        pe.wait_ge(ev["oev"], 2 * (l + 1))
                    last = mm(PS[:, n, 0:T], rotm, z[:, t, :], start=True, stop=True)
                last.then_inc(ev["rot"], 1)
                for t in range(3):
                    w = P if t < 2 else NB * TS
                    last = nc.tensor.transpose(PS[0:w, 5, t * P:(t + 1) * P], z[:, Z_V, t * P:t * P + w], ident)
                last.then_inc(ev["vtp"], 1)
                between(l, 11)
                pe.wait_ge(ev["qk"], l + 1)
                pe.wait_ge(ev["vt"], l + 1)
                hold(pe)
                for n in (0, 1):
                    rows = slice(64 * n, 64 * n + 64)
                    for t in range(NG):
                        mm(PS[:, 4 + n, t * P:(t + 1) * P], z[rows, Z_A + t, 0:P], z[rows, Z_K, 0:P],
                           start=True, stop=True)
                    for t in range(NG):
                        last = mm(PS[:, 2 * n + t // 2, (t % 2) * 256:(t % 2 + 1) * 256],
                                  z[rows, Z_A + t, P:TP], z[rows, Z_K, 0:TP], start=True, stop=True)
                last.then_inc(ev["sc"], 1)
                between(l, 12)
                pe.wait_ge(ev["scd"], l + 1)
                hold(pe)
                for n in (0, 1):
                    rows = slice(64 * n, 64 * n + 64)
                    for b in range(NB):
                        q = qs[rows, b, :]
                        p0, c0 = 32 * (b % 4), 192 * (b // 4)
                        mm(PS[p0:p0 + 32, n, c0:c0 + WIN], q, kc[rows, b, 0:WIN], start=True, stop=True)
                        last = mm(PS[p0:p0 + 32, n, c0 + WIN:c0 + 192], q, kc[rows, :, WIN:WIN + TS],
                                  start=True, stop=True)
                last.then_inc(ev["ss"], 1)
                between(l, 13)
                between(l, 14)
                pe.wait_ge(ev["exn"], l + 1)
                for n in (0, 1):
                    for t in range(NG):
                        last = nc.tensor.transpose(PS[:, 2 + n, t * P:(t + 1) * P], SC0[:, NG * n + t, 0:P], ident)
                last.then_inc(ev["pt"], 1)
                pe.wait_ge(ev["ptd"], 3 * l + 1)
                hold(pe)
                for n in (0, 1):
                    last = mm(PS[64 * n:64 * n + 64, 4, :], va[:, 0, 64 * n:64 * n + 64], PT[:, n, :],
                              start=True, stop=True)
                last.then_inc(ev["pv"], 1)
                between(l, MIXER_UNITS)
                pe.wait_ge(ev["ssd"], l + 1)
                for s in range(4):
                    kb, n = s // 2, s % 2
                    for t in range(NG):
                        last = nc.tensor.transpose(PS[:, s, t * P:(t + 1) * P],
                                                   SC1[:, NG * n + t, kb * P:(kb + 1) * P], ident)
                last.then_inc(ev["pt"], 1)
                pe.wait_ge(ev["ptd"], 3 * l + 2)
                hold(pe)
                for n in (0, 1):
                    for kb in (0, 1):
                        last = mm(PS[64 * n:64 * n + 64, 5, :], va[:, kb, 64 * n:64 * n + 64], PT[:, 2 * kb + n, :],
                                  start=(kb == 0), stop=(kb == 1))
                last.then_inc(ev["pv"], 1)
                pe.wait_ge(ev["sexn"], l + 1)
                for n in (0, 1):
                    for g in (0, 1):
                        c0 = (2 * n + g) * P
                        nc.tensor.transpose(PS[:, 0, c0:c0 + P], SS[:, n, g, 0:WIN], ident)
                        last = nc.tensor.transpose(PS[0:64, 1, c0:c0 + P], SS[:, n, g, WIN:192], ident)
                last.then_inc(ev["pt"], 1)
                pe.wait_ge(ev["ptd"], 3 * l + 3)
                hold(pe)
                for n in (0, 1):
                    rows = slice(64 * n, 64 * n + 64)
                    mm(PS[rows, 2, 0:256], va[0:64, 2, rows], PN[:, 256 * n:256 * (n + 1)], start=True, stop=True)
                    for b in range(NB):
                        c0 = (b // 4) * P + 32 * (b % 4)
                        last = mm(PS[rows, 2, c0:c0 + 32], vc[:, b, rows], PC[:, 256 * n + c0:256 * n + c0 + 32],
                                  start=False, stop=True, skip_group_check=True)
                last.then_inc(ev["pv"], 1)

            pe.wait_ge(s_c, 1)
            pe.wait_ge(s_load, 16 * 4)
            for u in range(START):
                partial(u, first[u])
                if u:
                    summed(u - 1)
                if u == 4:
                    x_stats(0)
            summed(START - 1)
            with pe.Fori(0, DEPTH) as l:
                ffn_in(l, 0, OFF_F0I, U_A)
                ffn_out(l, 0, OFF_F0O, U_B)
                y_stats(3 * l, 0)
                x_stats(3 * l + 1)
                for it in range(IT_MI):
                    g = l * ITS + OFF_MI + it
                    split_ready(0, g)
                    pe.wait_ge(s_za, 5 * l + it + 1)
                    pair(0, 0, 3 * l + 1 if it == 0 else None)
                    partial(START + l * UNITS + U_B + 4 + it)
                    split_ready(1, g)
                    pe.wait_ge(s_zd, 5 * l + it + 1)
                    pair(1, 2)
                    summed(START + l * UNITS + U_B + 4 + it)
                recurrence(l)
                attention(l)
                for it in range(IT_MO):
                    g = l * ITS + OFF_MO + it
                    if it == 0:
                        pe.wait_ge(ev["mixl"], 3 * (l + 1))
                    else:
                        pe.wait_ge(s_sqp, 12 * l + 6)
                    split_ready(0, g)
                    pair(0, 0)
                    split_ready(1, g)
                    if it == 1:
                        pe.wait_ge(s_sqp, 12 * l + 7)
                    pair(1, 2)
                y_stats(3 * l + 1, 4)
                x_stats(3 * l + 2)
                ffn_in(l, 1, OFF_F1I, None)
                ffn_out(l, 1, OFF_F1O, None)
                y_stats(3 * l + 2, 0)
                x_stats(3 * l + 3)

        @block.scalar
        def _(act):
            a_ = nc.scalar.activation
            ch = Chain(act, s_ach, ACT_CHAIN)

            def hi_split(slot, g, width):
                act.wait_ge(s_raw[slot], 16 * (g + 1))
                act.wait_ge(s_used[slot], g + 1)
                a_(WHI[:, slot, 0:width], raw[:, slot, 0:width], ACT.Copy).then_inc(s_hi[slot], 1)

            def ada_copy(u):
                act.wait_ge(s_part, u + 2)
                act.wait_ge(s_adt, u + 1)
                a_(adp[:], PS[:, 6, 0:256], ACT.Copy).then_inc(s_adp, 1)

            def exp_set():
                hold(act)
                nc.scalar.preload_act_table_set("natural_log_exp_and_others")

            def silu_set():
                hold(act)
                nc.scalar.preload_act_table_set("silu_and_others")

            def rms(bank, out, done, scale, ready, value):
                act.wait_ge(ready, value)
                ch.link(a_(rt[:], PS[:, bank, 0:T], ACT.Ln, bias=EPS, scale=scale))
                a_(out, rt[:], ACT.Exp, scale=-0.5).then_inc(done, 1)

            def x_rms(n):
                act.wait_ge(s_xs, n + 1)
                for k in range(KT):
                    act.wait_ge(s_x, KT * n + k + 1)
                    a_(sq[:, k, :], x[:, k, :], ACT.Square).then_inc(s_sqx, 1)
                rms(5, rst[:], s_r, 1.0 / D, s_xst, n + 1)

            def x_norm(n, m):
                for k in range(KT):
                    act.wait_ge(s_mt, KT * n + k + 1)
                    a_(hmh[:, k, 0:TP], sq[:, k, 0:TP], ACT.Identity, bias=mod[m][:, 8 + k, 0:1]).then_inc(s_hmh, 1)
                    if k == 0:
                        act.wait_ge(s_ms, n + 1)
                        a_(seq(hmh[:]), pre[:], ACT.Copy).then_inc(s_hms, 1)

            def y_norm(n, bank):
                rms(bank, rst2[:], s_pr, 1.0 / D, s_pst, n + 1)

            def squares(out_tiles, bank, pair_):
                act.wait_ge(s_acc, pair_ + 1)
                a_(sq[:, 0:2, :], PS[:, bank:bank + 2, 0:T], ACT.Square).then_inc(s_sqd, 1)
                return a_(y[:, out_tiles, :], PS[:, bank:bank + 2, 0:T], ACT.Copy)

            def ffn_in(l, f, off, uoff):
                silu_set()
                if uoff is not None:
                    u0 = START + l * UNITS + uoff

                def body(it, width):
                    g = l * ITS + off + it
                    i = (2 * l + f) * IT_IN + it
                    act.wait_ge(s_used[0], g + 2)
                    act.wait_ge(s_uread, i + 1)
                    a_(sg, PS[:, 0:2, 0:T], ACT.Silu).then_inc(s_gread, 1)
                    hi_split(0, g + 1, width)
                    if uoff is not None:
                        ada_copy(u0 + 1 + it)
                    hi_split(1, g + 1, width)
                    act.wait_ge(s_uread, i + 2)
                    a_(hh[:, bass.ds(it * 2, 2), :], hf, ACT.Copy).then_inc(s_hh, 1)

                with act.Fori(0, IT_IN - 1) as it:
                    body(it, W_IN)
                body(IT_IN - 1, W_OUT)

            def ffn_out(l, f, off, uoff, n):
                exp_set()

                def body(it, width, end=False):
                    g = l * ITS + off + it
                    if width:
                        hi_split(0, g + 1, width)
                    if uoff is not None:
                        ada_copy(START + l * UNITS + uoff + it)
                    act.wait_ge(s_used[1], g + 2)
                    squares(bass.ds(it * 2, 2), 4, 4 * n + it).then_inc(s_sqp, 1)
                    if not end:
                        hi_split(1, g + 1, width)

                with act.Fori(0, IT_OUT - 1) as it:
                    body(it, W_OUT)
                body(IT_OUT - 1, W_IN if uoff is not None else 0, True)

            def recurrence(l):
                zf = z[:, Z_F:Z_F + 2, :]
                exp_set()
                act.wait_ge(s_za, 5 * l + 6)
                a_(zf, zf, ACT.Exp, scale=-1.0).then_inc(ev["e"], 1)
                act.wait_ge(ev["itp"], l + 1)
                a_(vtok[:, 0:2, :], PS[:, 0, 0:512], ACT.Copy)
                a_(vtok[0:64, 2, :], PS[0:64, 1, 0:256], ACT.Copy).then_inc(ev["it"], 1)
                ada_copy(START + l * UNITS + U_B + 9 + 0)
                act.wait_ge(ev["f"], l + 1)
                a_(zf, zf, ACT.Ln).then_inc(ev["g"], 1)
                ada_copy(START + l * UNITS + U_B + 9 + 1)
                for s in range(2):
                    act.wait_ge(ev["d0"], 2 * l + s + 1)
                    v = LV[:, 3 * s:3 * s + 3, :]
                    a_(v, v, ACT.Exp).then_inc(ev["e0"], 1)
                    ada_copy(START + l * UNITS + U_B + 11 + s)
                a_(eb, bb, ACT.Exp).then_inc(ev["eb"], 1)
                act.wait_ge(ev["kh0"], l + 1)
                a_(zf, zf, ACT.Exp).then_inc(ev["ends"], 1)
                ada_copy(START + l * UNITS + U_B + 9 + 4)
                ada_copy(START + l * UNITS + U_B + 9 + 5)
                act.wait_ge(ev["ktp"], l + 1)
                a_(ktok[:, 0:2, :], PS[:, 0, 0:512], ACT.Copy)
                a_(ktok[0:64, 2, :], PS[0:64, 1, 0:256], ACT.Copy).then_inc(ev["kt"], 1)
                ada_copy(START + l * UNITS + U_B + 9 + 6)
                ada_copy(START + l * UNITS + U_B + 9 + 7)
                act.wait_ge(ev["obk"], l + 1)
                o4 = z[:, Z_Q:Z_Q + 2, :].rearrange("p a (c t) -> p a c t", t=CH)
                a_(o4[:, :, 0:5:2, :], PS[:, 2, 0:6 * CH].rearrange("p (a c t) -> p a c t", a=2, c=3), ACT.Copy)
                a_(o4[:, :, 1:4:2, :], PS[:, 3, 0:4 * CH].rearrange("p (a c t) -> p a c t", a=2, c=2),
                   ACT.Copy).then_inc(ev["oev"], 1)
                act.wait_ge(ev["oev"], 2 * (l + 1))
                ada_copy(START + l * UNITS + U_B + 9 + 8)
                a_(z[:, Z_I:Z_I + 2, :], z[:, Z_Q:Z_Q + 2, :], ACT.Square).then_inc(ev["osq"], 1)
                ada_copy(START + l * UNITS + U_B + 9 + 9)
                act.wait_ge(ev["ost"], l + 1)
                ch.link(a_(z[:, Z_I:Z_I + 2, :], PS[:, 2:4, 0:T], ACT.Ln, bias=EPS, scale=1.0 / HD))
                a_(z[:, Z_I:Z_I + 2, :], z[:, Z_I:Z_I + 2, :], ACT.Exp, scale=-0.5).then_inc(ev["orr"], 1)
                act.wait_ge(ev["og"], l + 1)
                a_(hmh[:, 4:6, :], z[:, Z_Q:Z_Q + 2, :], ACT.Copy).then_inc(ev["oh"], 1)
                ada_copy(START + l * UNITS + U_B + 9 + 10)

            def attention(l):
                act.wait_ge(ev["vtp"], l + 1)
                a_(va[:, 0:2, :], PS[:, 5, 0:256], ACT.Copy)
                a_(va[0:64, 2, :], PS[0:64, 5, 256:384], ACT.Copy).then_inc(ev["vt"], 1)
                ada_copy(START + l * UNITS + U_B + 9 + 11)
                ada_copy(START + l * UNITS + U_B + 9 + 12)
                act.wait_ge(ev["ex"], l + 1)
                for h in range(NH):
                    a_(SC0[:, h, :], SC0[:, h, :], ACT.Exp, bias=mx[:, h:h + 1], accum_out=den[:, h:h + 1])
                for h in range(NH):
                    last = a_(SC1[:, h, :], SC1[:, h, :], ACT.Exp, bias=mx[:, 8 + h:9 + h],
                              accum_out=den[:, 8 + h:9 + h])
                last.then_inc(ev["exd"], 1)
                ada_copy(START + l * UNITS + U_B + 9 + 13)
                act.wait_ge(ev["sex"], l + 1)
                for n in (0, 1):
                    for g in (0, 1):
                        i = 16 + 2 * n + g
                        last = a_(SS[:, n, g, :], SS[:, n, g, :], ACT.Exp, bias=mx[:, i:i + 1],
                                  accum_out=den[:, i:i + 1])
                last.then_inc(ev["exd"], 1)
                ada_copy(START + l * UNITS + U_B + 9 + 14)
                act.wait_ge(ev["pt"], 3 * l + 1)
                a_(PT[:, 0:2, :], PS[:, 2:4, :], ACT.Copy).then_inc(ev["ptd"], 1)
                act.wait_ge(ev["pv"], 3 * l + 1)
                a_(hmh[:, 0:4, 0:P], PS[:, 4, :].rearrange("p (a t) -> p a t", a=4), ACT.Copy).then_inc(ev["pvd"], 1)
                act.wait_ge(ev["pt"], 3 * l + 2)
                a_(PT[:, :, :], PS[:, 0:4, :], ACT.Copy).then_inc(ev["ptd"], 1)
                act.wait_ge(ev["pv"], 3 * l + 2)
                a_(hmh[:, 0:4, P:TP], PS[:, 5, :].rearrange("p (a t) -> p a t", a=4), ACT.Copy).then_inc(ev["pvd"], 1)
                act.wait_ge(ev["pt"], 3 * l + 3)
                a_(PC, PS[:, 0, :], ACT.Copy)
                a_(PN, PS[0:64, 1, :], ACT.Copy).then_inc(ev["ptd"], 1)
                act.wait_ge(ev["pv"], 3 * l + 3)
                for a in range(4):
                    last = a_(hmh[:, a, TP:T].rearrange("p (b t) -> p b t", t=TS),
                              PS[:, 2, 0:256].rearrange("p (b a t) -> p a b t", a=4, t=TS)[:, a], ACT.Copy)
                last.then_inc(ev["pvd"], 1)
                act.wait_ge(ev["cv"], l + 1)
                a_(hmh[:, 6:8, :], z[:, Z_CC:Z_CC + 2, :], ACT.Copy).then_inc(ev["cst"], 1)

            act.wait_ge(s_load, 16 * 4)
            act.wait_ge(ev["kvo"], 1)
            silu_set()
            a_(cT[:, :, 0:NS], cT[:, :, 0:NS], ACT.Silu).then_inc(s_c, 1)
            act.wait_ge(ev["lbd"], 1)
            exp_set()
            a_(lbt[:, 0:DEPTH, :], lbt[:, 0:DEPTH, :], ACT.Exp).then_inc(ev["lbe"], 1)
            for u in range(START):
                ada_copy(u)
                if u == 4:
                    act.wait_ge(s_xin, 16)
                    for k in range(KT):
                        a_(sq[:, k, :], x[:, k, :], ACT.Square).then_inc(s_sqx, 1)
            act.wait_ge(s_xst, 1)
            a_(rt[:], PS[:, 5, 0:T], ACT.Ln, bias=EPS, scale=1.0 / D).then_inc(s_rt0, 1)
            act.wait_ge(s_rt0, 1)
            a_(rst[:], rt[:], ACT.Exp, scale=-0.5).then_inc(s_r, 1)
            with act.Fori(0, DEPTH) as l:
                ch.base, ch.n = l * ACT_CHAIN, 0
                hi_split(0, l * ITS, W_IN)
                ada_copy(START + l * UNITS + U_A)
                x_norm(3 * l, 2)
                hi_split(1, l * ITS, W_IN)
                ffn_in(l, 0, OFF_F0I, U_A)
                ffn_out(l, 0, OFF_F0O, U_B, 3 * l)
                y_norm(3 * l, 0)
                hi_split(1, l * ITS + OFF_MI, W_IN)
                x_rms(3 * l + 1)
                x_norm(3 * l + 1, 0)
                silu_set()
                for it in range(IT_MI):
                    g = l * ITS + OFF_MI + it
                    act.wait_ge(s_used[0], g + 2)
                    a_(z[:, 4 * it:4 * it + 2, :], PS[:, 0:2, 0:T],
                       ACT.Silu if 4 * it == Z_G else ACT.Copy).then_inc(s_za, 1)
                    hi_split(0, g + 1, W_IN)
                    ada_copy(START + l * UNITS + U_B + 4 + it)
                    hi_split(1, g + 1, W_IN)
                recurrence(l)
                act.wait_ge(ev["dss"], l + 1)
                for e in (0, 1):
                    act.dma_start(O["sp"][l, e], DS[64 * e:64 * e + 64, 3, :, 64 * e:64 * e + 64]).then_inc(s_st, 16)
                act.wait_ge(ev["s0n"], l + 1)
                act.dma_start(O["ss"][l], s0[:]).then_inc(s_out, 16)
                attention(l)
                act.wait_ge(ev["qk"], l + 1)
                act.dma_start(O["kp"][l], z[:, Z_K, P:TP]).then_inc(s_out, 16)
                act.dma_start(O["ks"][l], kc[:, :, TS:WIN + TS]).then_inc(s_out, 16)
                act.dma_start(O["vp"][l], va[:, 1, :]).then_inc(s_out, 16)
                act.dma_start(O["vs"][l, 0:WIN - TS], vc[TS:WIN, :, :]).then_inc(s_out, 16)
                act.dma_start(O["vn"][l], va[0:64, 2, :]).then_inc(s_out, 16)
                act.dma_start(O["conv"][l], cso[:]).then_inc(s_out, 16)
                exp_set()
                for it in range(IT_MO):
                    g = l * ITS + OFF_MO + it
                    n = 12 * l + 4 + 2 * it
                    act.wait_ge(s_used[0], g + 2)
                    squares(slice(4 * it, 4 * it + 2), 0, n).then_inc(s_sqp, 1)
                    hi_split(0, g + 1, W_IN)
                    act.wait_ge(s_used[1], g + 2)
                    squares(slice(4 * it + 2, 4 * it + 4), 2, n + 1).then_inc(s_sqp, 1)
                    if it < IT_MO - 1:
                        hi_split(1, g + 1, W_IN)
                y_norm(3 * l + 1, 4)
                hi_split(1, l * ITS + OFF_F1I, W_IN)
                x_rms(3 * l + 2)
                x_norm(3 * l + 2, 1)
                act.wait_ge(s_out, 16 * 7 * (l + 1))
                ffn_in(l, 1, OFF_F1I, None)
                ffn_out(l, 1, OFF_F1O, None, 3 * l + 2)
                y_norm(3 * l + 2, 0)
                x_rms(3 * l + 3)
                assert ch.n == ACT_CHAIN, ch.n

        @block.vector
        def _(dve):
            v = nc.vector
            tt, ts, stt = v.tensor_tensor, v.tensor_scalar, v.scalar_tensor_tensor
            ch = Chain(dve, s_dch, DVE_CHAIN)

            def lo_split(slot, g, width):
                dve.wait_ge(s_hi[slot], g + 2)
                tt(WLO[:, slot, 0:width], raw[:, slot, 0:width], WHI[:, slot, 0:width].bitcast(F32),
                   ALU.subtract).then_inc(s_lo[slot], 1)

            def mod_out(u, m, j, bias):
                dve.wait_ge(s_adt, u + 2)
                src = PS[:, 7, 0:32].rearrange("p (i s) -> p i s", i=2)[:, :, 0:NS]
                tt(mod[m][:, bass.ds(j, 2), :], src, bias.unsqueeze(2).to_broadcast([P, 2, NS]), ALU.add)\
                    .then_inc(s_mod, 1)

            def ready(u):
                dve.wait_ge(s_mod, u + 2)

            def group_bias(m, j):
                return par[:, bass.ds(R_AB + 24 * m + j, 2)]

            def gate_ready(m, sub, weight):
                g = mod[m][:, 0:KT, :]
                post = par[:, R_POST + KT * sub:R_POST + KT * (sub + 1)]
                ch.link(stt(g, g, weight, post.unsqueeze(2).to_broadcast([P, KT, NS]), ALU.mult, ALU.mult))

            def scale_ready(m, params):
                sc = mod[m][:, 16:24, :]
                pre = params[:, R_PRE + KT * m:R_PRE + KT * (m + 1)]
                return stt(sc, sc, 1.0, pre.unsqueeze(2).to_broadcast([P, KT, NS]), ALU.add, ALU.mult)

            def x_norm(n, m):
                dve.wait_ge(s_r, n + 1)

                def scaled(k):
                    stt(sq[:, k, 0:TP], x[:, k, 0:TP], mod[m][:, 16 + k, 0:1], rst[:, 0:TP],
                        ALU.mult, ALU.mult).then_inc(s_mt, 1)

                def low(k):
                    dve.wait_ge(s_hmh, KT * n + k + 1)
                    dve.wait_ge(s_mt, KT * n + k + 1)
                    stt(hml[:, k, 0:TP], sq[:, k, 0:TP], mod[m][:, 8 + k, 0:1], hmh[:, k, 0:TP].bitcast(F32),
                        ALU.add, ALU.subtract).then_inc(s_hml, 1)

                scaled(0)
                dve.wait_ge(s_pre, 2 * n + 1)
                done = ch.mark(tt(pre[:], pre[:], rst[:, TP:T].rearrange("p (b t) -> p b t", t=TS).unsqueeze(1)
                                  .to_broadcast([P, KT, NB, TS]), ALU.mult))
                scaled(1)
                ch.wait(done)
                tt(pre[:], pre[:], by_seq(mod[m], 8), ALU.add).then_inc(s_ms, 1)
                low(0)
                scaled(2)
                dve.wait_ge(s_hms, n + 1)
                dve.wait_ge(s_ms, n + 1)
                tt(seq(hml[:]), pre[:], seq(hmh[:].bitcast(F32)), ALU.subtract).then_inc(s_hls, 1)
                for k in range(1, KT):
                    if k + 2 < KT:
                        scaled(k + 2)
                    low(k)

            def y_norm(n, m):
                dve.wait_ge(s_pr, n + 1)
                dve.wait_ge(s_sqp, 4 * n + 5)
                done = {}

                def term(k):
                    done[k] = ch.mark(stt(sq[:, k, 0:TP], y[:, k, 0:TP], mod[m][:, k, 0:1], rst2[:, 0:TP],
                                          ALU.mult, ALU.mult))

                term(0)
                for k in range(KT):
                    if k + 1 < KT:
                        term(k + 1)
                    ch.wait(done[k])
                    tt(x[:, k, 0:TP], x[:, k, 0:TP], sq[:, k, 0:TP], ALU.add).then_inc(s_x, 1)

            def sum_squares(n):
                for i in range(2):
                    dve.wait_ge(s_sqx, KT * n + SUMMED + 2 + i)
                    if i:
                        dve.wait_ge(s_sqa, 2 * n + 1)
                    tt(sq[:, SUMMED, :], sq[:, SUMMED, :], sq[:, SUMMED + 1 + i, :], ALU.add).then_inc(s_sqa, 1)

            def add_squares(pair_):
                dve.wait_ge(s_sqd, pair_ + 1)
                dve.wait_ge(s_acc, pair_ + 1)
                tt(acc[:], acc[:], sq[:, 0, :], ALU.add).then_inc(s_acc0, 1)
                dve.wait_ge(s_acc0, pair_ + 1)
                tt(acc[:], acc[:], sq[:, 1, :], ALU.add).then_inc(s_acc, 1)

            def ffn_in(l, f, off, uoff, m):
                if uoff is not None:
                    u0 = START + l * UNITS + uoff

                def body(it, width):
                    g = l * ITS + off + it
                    i = (2 * l + f) * IT_IN + it
                    lo_split(0, g + 1, width)
                    dve.wait_ge(s_used[1], g + 2)
                    dve.wait_ge(s_gread, i + 2)
                    dve.wait_ge(s_hl, i + 1)
                    tt(hf, sg, PS[:, 2:4, 0:T], ALU.mult).then_inc(s_uread, 1)
                    if uoff is not None:
                        mod_out(u0 + it, m, 2 * it, group_bias(m, 2 * it))
                    lo_split(1, g + 1, width)
                    dve.wait_ge(s_hh, i + 1)
                    dve.wait_ge(s_uread, i + 2)
                    tt(hl[:, bass.ds(it * 2, 2), :], hf, hh[:, bass.ds(it * 2, 2), :].bitcast(F32),
                       ALU.subtract).then_inc(s_hl, 1)

                with dve.Fori(0, IT_IN - 1) as it:
                    body(it, W_IN)
                body(IT_IN - 1, W_OUT)
                if uoff is not None:
                    mod_out(u0 + IT_IN, m, 2 * IT_IN, group_bias(m, 2 * IT_IN))

            def ffn_out(l, f, off, uoff, m, sub, n):
                ready(START + l * UNITS + (U_A if f == 0 else U_C) + 11)
                gate_ready(m, sub, 0.5)
                scale_ready(m, par).then_inc(ev["gs"], 1)
                dve.wait_ge(ev["gs"], n + 2)
                ch.link(v.memset(acc[:], 0.0))
                hold(dve)

                def body(it, width, end=False):
                    g = l * ITS + off + it
                    if width:
                        lo_split(0, g + 1, width)
                    if uoff is not None and not end:
                        mod_out(START + l * UNITS + uoff + it, 1, 2 * it, group_bias(1, 2 * it))
                    add_squares(4 * n + it)
                    if not end:
                        lo_split(1, g + 1, width)

                with dve.Fori(0, IT_OUT - 1) as it:
                    body(it, W_OUT)
                body(IT_OUT - 1, W_IN if uoff is not None else 0, True)
                if uoff is not None:
                    it = IT_OUT - 1
                    mod_out(START + l * UNITS + uoff + it, 1, 2 * it, group_bias(1, 2 * it))

            def between(l, s):
                if s:
                    m, j = (1, 18 + 2 * (s - 1)) if s <= 3 else (2, 2 * (s - 4))
                    mod_out(START + l * UNITS + U_B + 9 + s - 1, m, j, group_bias(m, j))

            def recurrence(l):
                zf = z[:, Z_F:Z_F + 2, :]
                zf1 = zf.rearrange("p a t -> p (a t)")
                zq1 = z[:, Z_Q:Z_Q + 2, :].rearrange("p a t -> p (a t)")
                dve.wait_ge(ev["e"], l + 1)
                ch.link(ts(zf, zf, 1.0, None, ALU.add))
                ch.link(v.reciprocal(zf, zf))
                for a in (0, 1):
                    last = ts(zf[:, a, :], zf[:, a, :], lbc[:, 1, a:a + 1], lbc[:, 0, a:a + 1], ALU.mult, ALU.add)
                ch.link(last)
                ts(kk, zf1, -1.0, 1.0, ALU.mult, ALU.add)
                ts(zf, zf, FMIN, None, ALU.max).then_inc(ev["f"], 1)
                between(l, 1)
                dve.wait_ge(s_late, 32)
                dve.wait_ge(ev["g"], l + 1)
                for a in (0, 1):
                    last = v.tensor_tensor_scan(bb[:, a * T:(a + 1) * T], rset, zf[:, a, :], 0.0, ALU.mult, ALU.add)
                ch.link(last)
                for s in (0, 1):
                    for lv in range(3 * s, 3 * s + 3):
                        h = 1 << lv
                        b3 = bb.rearrange("p (n w) -> p n w", w=2 * h)
                        last = tt(LV[:, lv, :].rearrange("p (n w) -> p n w", w=2 * h), b3,
                                  b3[:, :, h - 1:h].to_broadcast([P, 2 * T // (2 * h), 2 * h]), ALU.subtract)
                    ch.link(last)
                    w = LV[:, 3 * s:3 * s + 3, :]
                    stt(w, w, -1.0, w, ALU.mult, ALU.min).then_inc(ev["d0"], 1)
                    if s == 0:
                        between(l, 2)
                for t0, n, w in ((0, TP // CH, CH), (TP, NB, TS)):
                    b4 = bb.rearrange("p (a t) -> p a t", a=2)[:, :, t0:t0 + n * w]\
                        .rearrange("p a (n w) -> p a n w", w=w)
                    last = tt(zf[:, :, t0:t0 + n * w].rearrange("p a (n w) -> p a n w", w=w),
                              b4[:, :, :, w - 1:w].to_broadcast([P, 2, n, w]), b4, ALU.subtract)
                last.then_inc(ev["kh0"], 1)
                for s in (0, 1):
                    dve.wait_ge(ev["e0"], 2 * l + s + 1)
                    for lv in range(3 * s, 3 * s + 3):
                        h = 1 << lv
                        for side, src in ((0, kk), (1, zq1)):
                            o = LV[:, lv, :].rearrange("p (n s h) -> p n s h", s=2, h=h)[:, :, side, :]
                            last = tt(o, o, src.rearrange("p (n s h) -> p n s h", s=2, h=h)[:, :, side, :], ALU.mult)
                last.then_inc(ev["z0"], 1)
                dve.wait_ge(ev["eb"], l + 1)
                e3 = eb.rearrange("p (a t) -> p a t", a=2)
                v.tensor_copy(dec[:, :, 0:4], e3[:, :, CH - 1:TP:CH])
                ch.link(v.tensor_copy(dec[:, :, 4:12], e3[:, :, TP + TS - 1:T:TS]))
                tt(eb, eb, zq1, ALU.mult)
                dve.wait_ge(ev["ends"], l + 1)
                tt(zf1, zf1, kk, ALU.mult).then_inc(ev["kh"], 1)
                n = 0
                between(l, 3)
                for h in range(4):
                    for cp in range(3):
                        if n in (6, 10):
                            between(l, n // 4 + 3)
                        rows, w = (slice(0, P), NL) if cp < 2 else (slice(0, 64), NLS)
                        dve.wait_ge(ev["gr"], 12 * l + n + 1)
                        tt(am[rows, 0:w * CH], PS[rows, 2 + n % 4, 0:w * CH], gram[rows, 0:w * CH],
                           ALU.mult).then_inc(ev["am"], 1)
                        dve.wait_ge(ev["am"], 12 * l + n + 1)
                        v.tensor_reduce(AT[rows, h, cp, :], am[rows, 0:w * CH].rearrange("p (i t) -> p t i", t=CH),
                                        AX.X, ALU.add).then_inc(ev["at"], 1)
                        n += 1
                        dve.wait_ge(ev["at"], 12 * l + n)
                between(l, 6)
                dve.wait_ge(ev["ds"], l + 1)
                for par_ in (0, 1):
                    last = tt(DS[:, par_:4:2, :, :].rearrange("p c a v -> p c a v"),
                              PS[:, par_, :].rearrange("p (c a v) -> p c a v", c=2, a=2),
                              bd.unsqueeze(1).unsqueeze(1).to_broadcast([P, 2, 2, P]), ALU.mult)
                ch.link(last)
                for c in range(1, 4):
                    for a in (0, 1):
                        last = stt(DS[:, c, a, :], DS[:, c - 1, a, :], dec[:, a, c:c + 1], DS[:, c, a, :],
                                   ALU.mult, ALU.add)
                    if c < 3:
                        ch.link(last)
                last.then_inc(ev["dss"], 1)
                for h in range(4):
                    last = tt(vm[:, h], vtok[0:64, 2, 64 * h:64 * h + 64].unsqueeze(1).to_broadcast([64, NB, 64]),
                              seqm[0:64, :].unsqueeze(2).to_broadcast([64, NB, 64]), ALU.mult)
                last.then_inc(ev["vm"], 1)
                between(l, 7)
                dve.wait_ge(ev["obk"], l + 1)
                dve.wait_ge(ev["oev"], 2 * l + 1)
                for e in (0, 1):
                    rows = slice(64 * e, 64 * e + 64)
                    o = z[rows, Z_Q:Z_Q + 2, TP:T]
                    last = tt(o, o, PS[rows, 4 + e, 0:128].rearrange("p (a t) -> p a t", a=2), ALU.add)
                last.then_inc(ev["oev"], 1)
                dve.wait_ge(ev["dsm"], l + 1)
                for a in (0, 1):
                    last = tt(s0[:, a], s0[:, a], dec[:, a, 4:12].unsqueeze(2).to_broadcast([P, NB, 64]), ALU.mult)
                ch.link(last)
                for a in (0, 1):
                    last = tt(s0[:, a], s0[:, a], PS[:, a, :].rearrange("p (b v) -> p b v", v=64), ALU.add)
                last.then_inc(ev["s0n"], 1)
                between(l, 8)
                between(l, 9)
                zo, zr = z[:, Z_Q:Z_Q + 2, :], z[:, Z_I:Z_I + 2, :]
                dve.wait_ge(ev["orr"], l + 1)
                ch.link(stt(zo, zo, par[:, R_GN:R_GN + 1], zr, ALU.mult, ALU.mult))
                tt(zo, zo, z[:, Z_G:Z_G + 2, :], ALU.mult).then_inc(ev["og"], 1)
                dve.wait_ge(ev["oh"], l + 1)
                dve.wait_ge(ev["og"], l + 1)
                tt(hml[:, 4:6, :], zo, hmh[:, 4:6, :].bitcast(F32), ALU.subtract).then_inc(ev["mixl"], 1)

            def attention(l):
                tmp = yf[:, 0:5 * T].rearrange("p (n t) -> p n t", n=5)
                between(l, 10)
                dve.wait_ge(ev["rot"], l + 1)
                ch.link(tt(tmp, PS[:, 0:5, 0:T], sinT.unsqueeze(1).to_broadcast([P, 5, T]), ALU.mult))
                dve.wait_ge(ev["pc"], l + 1)
                ch.link(tt(z[:, Z_K, :], z[:, Z_K, :], tmp[:, 0, :], ALU.add))
                v.tensor_copy(kc[:, :, WIN:WIN + TS], z[:, Z_K, TP:T].rearrange("p (b t) -> p b t", t=TS))
                ch.link(tt(z[:, Z_A:Z_A + 4, :], z[:, Z_A:Z_A + 4, :], tmp[:, 1:5, :], ALU.add))
                v.tensor_copy(qs.rearrange("p b (a t) -> p a b t", t=TS), seq(z[:, Z_A:Z_A + 4, :]))\
                    .then_inc(ev["qk"], 1)
                dve.wait_ge(s_st, 32 * (l + 1))
                sink = par[:, R_SINK:R_SINK + NH].unsqueeze(2)
                v.tensor_copy(SC0[:, :, 128:129], sink)
                v.tensor_copy(SC1[:, :, 256:257], sink)
                v.tensor_copy(SS[:, :, :, 192:193],
                              par[:, R_SINKS:R_SINKS + 2].unsqueeze(2).unsqueeze(3).to_broadcast([P, 2, 2, 1]))
                between(l, 11)
                dve.wait_ge(ev["sc"], l + 1)
                for n in (0, 1):
                    stt(SC0[:, 4 * n:4 * n + 4, 0:P], PS[:, 4 + n, :].rearrange("p (h k) -> p h k", h=4), SCALE,
                        mskp[:, 128:256].unsqueeze(1).to_broadcast([P, 4, P]), ALU.mult, ALU.add)
                for i in range(4):
                    last = stt(SC1[:, 2 * i:2 * i + 2, 0:256], PS[:, i, :].rearrange("p (h k) -> p h k", h=2), SCALE,
                               mskp.unsqueeze(1).to_broadcast([P, 2, 256]), ALU.mult, ALU.add)
                last.then_inc(ev["scd"], 1)
                dve.wait_ge(ev["scd"], l + 1)
                v.tensor_reduce(mx[:, 0:8], SC0, AX.X, ALU.max, negate=True)
                v.tensor_reduce(mx[:, 8:16], SC1, AX.X, ALU.max, negate=True).then_inc(ev["ex"], 1)
                between(l, 12)
                dve.wait_ge(ev["ss"], l + 1)
                for n in (0, 1):
                    last = stt(SS[:, n, :, 0:192], PS[:, n, 0:384].rearrange("p (g k) -> p g k", g=2), SCALE,
                               msks, ALU.mult, ALU.add)
                ch.link(last)
                v.tensor_reduce(mx[:, 16:20], SS.rearrange("p n g k -> p (n g) k"), AX.X, ALU.max, negate=True)\
                    .then_inc(ev["sex"], 1)
                between(l, 13)
                dve.wait_ge(ev["exd"], 2 * l + 1)
                ch.link(v.reciprocal(den[:, 0:16], den[:, 0:16]))
                tt(SC0[:, :, 0:P], SC0[:, :, 0:P], den[:, 0:8].unsqueeze(2).to_broadcast([P, 8, P]),
                   ALU.mult).then_inc(ev["exn"], 1)
                tt(SC1[:, :, 0:256], SC1[:, :, 0:256], den[:, 8:16].unsqueeze(2).to_broadcast([P, 8, 256]),
                   ALU.mult).then_inc(ev["ssd"], 1)
                dve.wait_ge(ev["exd"], 2 * l + 2)
                ch.link(v.reciprocal(den[:, 16:20], den[:, 16:20]))
                s3 = SS.rearrange("p n g k -> p (n g) k")[:, :, 0:192]
                tt(s3, s3, den[:, 16:20].unsqueeze(2).to_broadcast([P, 4, 192]), ALU.mult).then_inc(ev["sexn"], 1)
                between(l, 14)
                for blk in (0, 1):
                    dve.wait_ge(ev["pvd"], 3 * l + blk + 1)
                    tt(hml[:, 0:4, blk * P:(blk + 1) * P], PS[:, 4 + blk, :].rearrange("p (a t) -> p a t", a=4),
                       hmh[:, 0:4, blk * P:(blk + 1) * P].bitcast(F32), ALU.subtract)
                dve.wait_ge(ev["pvd"], 3 * l + 3)
                tt(seq(hml[:, 0:4, :]), PS[:, 2, 0:256].rearrange("p (b a t) -> p a b t", a=4, t=TS),
                   seq(hmh[:, 0:4, :].bitcast(F32)), ALU.subtract).then_inc(ev["mixl"], 1)
                between(l, MIXER_UNITS)
                dve.wait_ge(ev["cst"], l + 1)
                tt(hml[:, 6:8, :], z[:, Z_CC:Z_CC + 2, :], hmh[:, 6:8, :].bitcast(F32),
                   ALU.subtract).then_inc(ev["mixl"], 1)

            dve.wait_ge(s_load, 16 * 4)
            ch2 = Chain(dve, s_pch2, 0)
            ch2.link(v.tensor_copy(lbt[:, 2, :], lb2[:, 0, :]))
            for d in range(1, DEPTH):
                ch2.link(tt(lbt[:, 2, :], lbt[:, 2, :], lb2[:, d, :], ALU.max))
            tt(lbt[:, 0:DEPTH, :], lb2[:], lbt[:, 2:3, :].to_broadcast([P, DEPTH, 2]), ALU.subtract)\
                .then_inc(ev["lbd"], 1)
            dve.wait_ge(ev["lbe"], 1)
            ch2.link(v.tensor_copy(lbt[:, 2, :], lbt[:, 0, :]))
            for d in range(1, DEPTH):
                ch2.link(tt(lbt[:, 2, :], lbt[:, 2, :], lbt[:, d, :], ALU.add))
            ch2.link(v.reciprocal(lbt[:, 3, :], lbt[:, 2, :]))
            ch2.link(tt(lbt[:, 0:DEPTH, :], lbt[:, 0:DEPTH, :], lbt[:, 3:4, :].to_broadcast([P, DEPTH, 2]), ALU.mult))
            ch2.link(v.tensor_copy(lbt[:, 2, :], lbt[:, 0, :]))
            for d in range(DEPTH):
                if d:
                    ch2.link(tt(lbt[:, 2, :], lbt[:, 2, :], lbt[:, d, :], ALU.add))
                ch2.link(tt(lb2[:, d, :], lbt[:, 2, :], lbt[:, 0, :], ALU.subtract))
            for u in range(START):
                mod_out(u, 2, 8 + 2 * u, par2[:, DEPTH - 1, R_AB + 56 + 2 * u:R_AB + 58 + 2 * u])
                if u == 3:
                    sum_squares(0)
            ready(START - 1)
            scale_ready(2, par2[:, DEPTH - 1, :]).then_inc(ev["gs"], 1)
            dve.wait_ge(ev["gs"], 1)
            with dve.Fori(0, DEPTH) as l:
                ch.base, ch.n = l * DVE_CHAIN, 0
                lo_split(0, l * ITS, W_IN)
                v.tensor_copy(lbc[:, 0, :], lb2[:, l, :])
                ts(lbc[:, 1, :], lb2[:, l, :], -1.0, 1.0, ALU.mult, ALU.add)
                ch.link(v.tensor_copy(par[:], par2[:, l, :]))
                x_norm(3 * l, 2)
                lo_split(1, l * ITS, W_IN)
                ffn_in(l, 0, OFF_F0I, U_A, 0)
                ffn_out(l, 0, OFF_F0O, U_B, 0, 0, 3 * l)
                y_norm(3 * l, 0)
                sum_squares(3 * l + 1)
                lo_split(1, l * ITS + OFF_MI, W_IN)
                x_norm(3 * l + 1, 0)
                for it in range(IT_MI):
                    g = l * ITS + OFF_MI + it
                    lo_split(0, g + 1, W_IN)
                    dve.wait_ge(s_used[1], g + 2)
                    v.tensor_copy(z[:, 4 * it + 2:4 * it + 4, :], PS[:, 2:4, 0:T]).then_inc(s_zd, 1)
                    mod_out(START + l * UNITS + U_B + 4 + it, 1, 8 + 2 * it, group_bias(1, 8 + 2 * it))
                    lo_split(1, g + 1, W_IN)
                dve.wait_ge(s_zd, 5 * l + 6)
                recurrence(l)
                attention(l)
                ready(START + l * UNITS + U_B + 11)
                gate_ready(1, 1, 1.0)
                scale_ready(1, par).then_inc(ev["gs"], 1)
                dve.wait_ge(ev["gs"], 3 * l + 3)
                ch.link(v.memset(acc[:], 0.0))
                for it in range(IT_MO):
                    g = l * ITS + OFF_MO + it
                    n = 12 * l + 4 + 2 * it
                    add_squares(n)
                    lo_split(0, g + 1, W_IN)
                    add_squares(n + 1)
                    if it < IT_MO - 1:
                        lo_split(1, g + 1, W_IN)
                y_norm(3 * l + 1, 1)
                sum_squares(3 * l + 2)
                lo_split(1, l * ITS + OFF_F1I, W_IN)
                x_norm(3 * l + 2, 1)
                ffn_in(l, 1, OFF_F1I, None, 2)
                ffn_out(l, 1, OFF_F1O, None, 2, 2, 3 * l + 2)
                y_norm(3 * l + 2, 2)
                sum_squares(3 * l + 3)
                assert ch.n == DVE_CHAIN, ch.n

        @block.gpsimd
        def _(pool):
            g_ = nc.gpsimd
            tt = g_.tensor_tensor
            ch = Chain(pool, s_pch, POOL_CHAIN)
            for s in (*s_hi, *s_lo, *s_used, s_part, s_adp, s_adt, s_mod, s_gread, s_uread, s_hl,
                      s_sqp, s_acc, s_za, s_zd):
                pool.sem_inc(s, 1)
            g_.memset(cT[:, :, NS:32], 0.0).then_inc(ev["kvo"], 1)
            pool.wait_ge(s_xin, 16)
            pool.sem_inc(s_xs, 1)
            pool.sem_inc(s_x, KT)
            rs2 = rst2[:, TP:T].rearrange("p (b t) -> p b t", t=TS).unsqueeze(1).to_broadcast([P, KT, NB, TS])

            def x_scaled(n, m):
                pool.wait_ge(ev["gs"], n + 1)
                pool.wait_ge(s_xs, n + 1)
                tt(pre[:], seq(x[:]), by_seq(mod[m], 16), ALU.mult).then_inc(s_pre, 1)

            def y_norm(n, m):
                pool.wait_ge(ev["gs"], n + 2)
                pool.wait_ge(s_sqp, 4 * n + 5)
                tt(pre[:], seq(y[:]), by_seq(mod[m], 0), ALU.mult).then_inc(s_pre, 1)
                pool.wait_ge(s_pre, 2 * n + 2)
                pool.wait_ge(s_pr, n + 1)
                ch.link(tt(pre[:], pre[:], rs2, ALU.mult))
                tt(seq(x[:]), seq(x[:]), pre[:], ALU.add).then_inc(s_xs, 1)

            def conv(l):
                zc, zh, zb = (z[:, a:a + 2, :] for a in (Z_CC, Z_CH, Z_B))

                def rows(t, start, width):
                    return t[:, :, TP + 2:SEG].rearrange("p a (b w) -> p a b w", w=TS + 2)[:, :, :, start:start + width]

                def seqs(t):
                    return t[:, :, TP:T].rearrange("p a (b t) -> p a b t", t=TS)

                pool.wait_ge(s_late, 32)
                hold(pool)
                pool.wait_ge(s_zd, 5 * l + 6)
                tt(rows(up, 2, TS), seqs(zc), seqs(zh), ALU.mult)
                ch.link(tt(up[:, :, 2:TP + 2], zc[:, :, 0:TP], zh[:, :, 0:TP], ALU.mult))
                hold(pool)
                g_.memset(up[:, :, 0:2], 0.0)
                g_.tensor_copy(rows(up, 0, 2), cpv[:, l, :].rearrange("p (a b t) -> p a b t", a=2, t=2))
                g_.tensor_copy(cso[:, :, 0, :], up[:, :, TP:TP + 2])
                last = g_.tensor_copy(cso[:, :, 1:NS, :], rows(up, TS, 2))
                ch.link(last)
                for j in range(3):
                    w = par[:, R_CW + 2 * j:R_CW + 2 * j + 2]
                    out = zc if j == 0 else zh
                    tt(out[:, :, 0:TP], up[:, :, j:TP + j], w.unsqueeze(2).to_broadcast([P, 2, TP]), ALU.mult)
                    ch.link(tt(seqs(out), rows(up, j, TS), w.unsqueeze(2).unsqueeze(3).to_broadcast([P, 2, NB, TS]),
                               ALU.mult))
                    if j:
                        ch.link(tt(zc, zc, zh, ALU.add))
                tt(zc, zc, zb, ALU.mult).then_inc(ev["cv"], 1)

            with pool.Fori(0, DEPTH) as l:
                ch.base, ch.n = l * POOL_CHAIN, 0
                x_scaled(3 * l, 2)
                y_norm(3 * l, 0)
                x_scaled(3 * l + 1, 0)
                conv(l)
                pool.wait_ge(ev["rot"], l + 1)
                tt(z[:, Z_K, :], z[:, Z_K, :], cosT, ALU.mult)
                tt(z[:, Z_A:Z_A + 4, :], z[:, Z_A:Z_A + 4, :], cosT.unsqueeze(1).to_broadcast([P, 4, T]),
                   ALU.mult).then_inc(ev["pc"], 1)
                y_norm(3 * l + 1, 1)
                x_scaled(3 * l + 2, 1)
                y_norm(3 * l + 2, 2)
                assert ch.n == POOL_CHAIN, ch.n


def laid_out(i):
    c = np.ascontiguousarray

    def cols(a):
        a = a.reshape(*a.shape[:-1], a.shape[-1] // P, P)
        return np.moveaxis(a, (-1, -2), (0, 1))

    x = np.concatenate([i["x_prompt"][0], i["x_sample"].reshape(NB * TS, D)])
    cond = np.concatenate([i["c_prompt"], i["c_sample"]])

    def units(w):
        *lead, rows, n = w.shape
        w = w.reshape(*lead, rows // P, P, n // 256, 256)
        w = np.moveaxis(w, -2, -4)
        w = np.swapaxes(w, -3, -2)
        return w.reshape(*lead, n // 256, P, rows // P * 256)

    w_in = i["ffn_w_in"]
    gate, upw = units(w_in[..., :DFF]), units(w_in[..., DFF:])
    w_in = np.stack([gate, upw], axis=3).reshape(DEPTH, 2, 2 * IT_IN, P, W_IN)
    w_out = units(i["ffn_w_out"]).reshape(DEPTH, 2, 4, P, 2, W_OUT)
    w_out = np.swapaxes(w_out, 3, 4).reshape(DEPTH, 2, 8, P, W_OUT)
    heads = np.arange(NH * HD).reshape(NKV, NG, HD).transpose(1, 0, 2).ravel()
    at = 0
    part = {}
    for name, n in (("q", 512), ("k", 128), ("v", 128), ("qh", 256), ("f", 256), ("i", 256), ("g", 256),
                    ("b", 256), ("c", 256), ("h", 256)):
        part[name] = at + np.arange(n)
        at += n
    part["q"] = part["q"][heads]
    order = np.concatenate([part[n] for n in ("f", "qh", "i", "k", "v", "q", "c", "h", "g", "b")])
    m_in = units(i["mix_w_in"][:, :, order])
    rows = np.concatenate([heads, 512 + np.arange(512)])
    m_out = units(i["mix_w_out"][:, rows, :])
    ada = units(i["ada_w"])
    ada = np.concatenate([ada[:, 8:36], np.roll(ada[:, 0:8], -1, axis=0)], axis=1)
    ab = np.concatenate([i["ada_b"][:, 2048:], np.roll(i["ada_b"][:, :2048], -1, axis=0)], axis=1)
    par = np.empty((DEPTH, P, NR), np.float32)
    par[:, :, R_AB:R_AB + 72] = ab.reshape(DEPTH, 72, P).transpose(0, 2, 1)
    pre = np.roll(i["norm_pre"].reshape(3 * DEPTH, KT, P), -1, axis=0)
    par[:, :, R_PRE:R_PRE + 24] = pre.reshape(DEPTH, 24, P).transpose(0, 2, 1)
    par[:, :, R_POST:R_POST + 24] = i["norm_post"].reshape(DEPTH, 24, P).transpose(0, 2, 1)
    par[:, :, R_SINK:R_SINK + NH] = i["attn_sinks"][:, None, :]
    t = np.arange(P) % 32 // TS
    for n in range(NKV):
        par[:, :, R_SINKS + n] = i["attn_sinks"][:, n * NG + t]
    par[:, :, R_GN] = np.tile(i["hgrn_gnorm"], (1, 2))
    par[:, :, R_CW:R_CW + 6] = i["conv_w"].reshape(DEPTH, 6, P).transpose(0, 2, 1)
    return {
        "x": c(cols(x)), "c": c(cols(cond)), "cst": constants(), "par": par,
        "lb": c(i["hgrn_lower_bounds"].reshape(DEPTH, 2, P).transpose(2, 0, 1)),
        "cprev": c(i["state_conv"].reshape(DEPTH, NB, 2, 2, P).transpose(4, 0, 3, 1, 2).reshape(P, DEPTH, 32)),
        "k": c(i["cache_k_win"].reshape(DEPTH, NB, WIN, P).transpose(0, 3, 1, 2)),
        "v": c(i["cache_v_win"].reshape(DEPTH, NB, WIN, P).transpose(0, 2, 1, 3)),
        "s": c(i["state_hgrn"].reshape(DEPTH, NB, 2, P, 64).transpose(0, 3, 2, 1, 4)),
        "w_in": c(w_in), "w_out": c(w_out), "m_in": c(m_in), "m_out": c(m_out), "ada_w": c(ada),
    }


OUTS = {
    "x": (P, KT, T), "kp": (DEPTH, P, WIN), "vp": (DEPTH, WIN, P), "sp": (DEPTH, 2, 64, 2, 64),
    "conv": (DEPTH, P, 2, NS, 2), "ks": (DEPTH, P, NB, WIN), "vs": (DEPTH, WIN, NB, P),
    "vn": (DEPTH, NB * TS, P), "ss": (DEPTH, P, 2, NB, 64),
}


def returned(r):
    x = r["x"].transpose(2, 1, 0).reshape(T, D)
    conv = r["conv"].transpose(0, 3, 4, 2, 1).reshape(DEPTH, NS, 2, 256)
    vs = np.concatenate([r["vs"][:, :WIN - TS].transpose(0, 2, 1, 3), r["vn"].reshape(DEPTH, NB, TS, P)], axis=2)
    return (
        x[None, :TP], x[TP:].reshape(NB, TS, D),
        r["kp"].transpose(0, 2, 1).reshape(DEPTH, 1, WIN, NKV, HD), r["vp"].reshape(DEPTH, 1, WIN, NKV, HD),
        r["sp"].transpose(0, 3, 1, 2, 4).reshape(DEPTH, 1, 4, 64, 64), conv[:, :1],
        r["ks"].transpose(0, 2, 3, 1).reshape(DEPTH, NB, WIN, NKV, HD), vs.reshape(DEPTH, NB, WIN, NKV, HD),
        r["ss"].reshape(DEPTH, 2, 64, 2, NB, 64).transpose(0, 4, 3, 1, 2, 5).reshape(DEPTH, NB, 4, 64, 64),
        conv[:, 1:],
    )


def kernel(**inputs):
    import concourse.bacc as bacc
    from concourse.bass_utils import run_bass_kernel_spmd

    arrays = laid_out({k: np.asarray(v) for k, v in inputs.items()})
    nc = bacc.Bacc("TRN2", target_bir_lowering=False, num_devices=1)
    A = {k: nc.dram_tensor("in_" + k, a.shape, F32, kind="ExternalInput").ap() for k, a in arrays.items()}
    O = {k: nc.dram_tensor("out_" + k, s, F32, kind="ExternalOutput").ap() for k, s in OUTS.items()}
    trunk(nc, A, O)
    r = run_bass_kernel_spmd(nc, [{"in_" + k: a for k, a in arrays.items()}], core_ids=[0]).results[0]
    return tuple(np.ascontiguousarray(a) for a in returned({k: r["out_" + k] for k in OUTS}))
```

```python
from contextlib import ExitStack

import numpy as np

import concourse.bass as bass
from concourse import mybir

F32 = mybir.dt.float32
F32R = mybir.dt.float32r
ACT = mybir.ActivationFunctionType
ALU = mybir.AluOpType
AX = mybir.AxisListType

P = 128
D = 1024
KT = D // P
DEPTH = 2
TP, NB, TS = 256, 8, 8
T = TP + NB * TS
NS = 1 + NB
DFF = 2816
FT = DFF // P
NH, NKV, HD, WIN = 8, 2, 64, 128
NG = NH // NKV
PAST = 2048
THETA = 10000.0
EPS = 1e-6
NEG = -1e30
SCALE = HD ** -0.5
FMIN = 2.0 ** -63

IT_IN, IT_OUT, IT_MI, IT_MO = 11, 4, 5, 2
W_IN, W_OUT = KT * 256, (FT // 2) * 256
OFF_F0I = 0
OFF_F0O = OFF_F0I + IT_IN
OFF_MI = OFF_F0O + IT_OUT
OFF_MO = OFF_MI + IT_MI
OFF_F1I = OFF_MO + IT_MO
OFF_F1O = OFF_F1I + IT_IN
ITS = OFF_F1O + IT_OUT

START = 8
UNITS = 36
U_A, U_B, U_C = 0, 12, 24

Z_F, Z_Q, Z_I, Z_K, Z_V, Z_A, Z_CC, Z_CH, Z_G, Z_B = 0, 2, 4, 6, 7, 8, 12, 14, 16, 18
NZ = 20
DIAG = -1
LEVELS = [0, 1, 2, DIAG, 3, 4, 5]
NL = len(LEVELS)
NLS = 4
CH = 64

C_ID, C_ROT, C_ONE, C_BD, C_SEL = 0, 128, 256, 384, 512
C_COS = 528
C_SIN = C_COS + T
C_MP = C_SIN + T
C_MS = C_MP + 256
C_GR = C_MS + 2 * 192
C_SQ = C_GR + NL * CH
C_RS = C_SQ + NB
NC_ = C_RS + T

R_AB, R_PRE, R_POST, R_SINK, R_SINKS, R_GN, R_CW = 0, 72, 96, 120, 128, 130, 131
NR = 137

ACT_CHAIN = 7
DVE_CHAIN = 45
POOL_CHAIN = 13

SUMMED = 5
SEG = TP + 2 + NB * (TS + 2)


def constants():
    c = np.zeros((P, NC_), np.float32)
    i = np.arange(P)
    c[i, C_ID + i] = 1
    lo = i % HD < HD // 2
    c[(i + 32)[lo], C_ROT + i[lo]] = -1
    c[(i - 32)[~lo], C_ROT + i[~lo]] = 1
    c[:, C_ONE:C_ONE + P] = 1
    c[:, C_BD:C_BD + P] = (i[:, None] // 64 == i[None, :] // 64)
    for j in range(4):
        for s in range(NS):
            c[32 * j + s, C_SEL + s] = 1
    half = HD // 2
    inv = np.power(np.float32(THETA), -np.arange(half, dtype=np.float32) / np.float32(half)).astype(np.float32)
    pos = np.concatenate([np.arange(TP), np.tile(PAST + np.arange(TS), NB)]).astype(np.float32)
    ang = (pos[None, :] * inv[i % half][:, None]).astype(np.float32)
    c[:, C_COS:C_COS + T] = np.cos(ang)
    c[:, C_SIN:C_SIN + T] = np.sin(ang)
    k = np.arange(256)[None, :]
    c[:, C_MP:C_MP + 256] = np.where((k > i[:, None]) & (k <= i[:, None] + 128), 0, NEG)
    tok = i % TS
    for hi in range(2):
        m = np.full((P, 192), NEG, np.float32)
        m[:, :128] = np.where(np.arange(128)[None, :] > tok[:, None], 0, NEG)
        b = 4 * hi + i // 32
        n = np.arange(64)[None, :]
        m[:, 128:] = np.where((n // TS == b[:, None]) & (n % TS <= tok[:, None]), 0, NEG)
        c[:, C_MS + 192 * hi:C_MS + 192 * (hi + 1)] = m
    s, t = (i % CH)[:, None], np.arange(CH)[None, :]
    for n, lv in enumerate(LEVELS):
        h = 1 << max(lv, 0)
        m = (s == t) if lv == DIAG else (s // (2 * h) == t // (2 * h)) & (s % (2 * h) < h) & (t % (2 * h) >= h)
        c[:, C_GR + n * CH:C_GR + (n + 1) * CH] = m
    c[:, C_SQ:C_SQ + NB] = (i[:, None] // TS == np.arange(NB)[None, :])
    r = np.ones(T, np.float32)
    r[0:TP:CH] = 0
    r[TP::TS] = 0
    c[:, C_RS:C_RS + T] = r
    return c


def trunk(nc, A, O):
    ctx = ExitStack()
    with ctx:
        def sb(name, shape, dt=F32):
            return ctx.enter_context(nc.sbuf_tensor(name, shape, dt))

        def sem(name):
            return ctx.enter_context(nc.semaphore(name))

        x = sb("x", [P, KT, T])
        y = sb("y", [P, KT, T])
        sq = sb("sq", [P, KT, T])
        hmh = sb("hmh", [P, KT, T], F32R)
        hml = sb("hml", [P, KT, T], F32R)
        raw = sb("raw", [P, 2, W_OUT])
        WHI = sb("WHI", [P, 2, W_OUT], F32R)
        WLO = sb("WLO", [P, 2, W_OUT], F32R)
        ada = sb("ada", [P, 2, 1024])
        cst = sb("cst", [P, NC_])
        par2 = sb("par2", [P, DEPTH, NR])
        par = sb("par", [P, NR])
        lb2 = sb("lb2", [P, DEPTH, 2])
        lbt = sb("lbt", [P, 4, 2])
        lbc = sb("lbc", [P, 2, 2])
        cpv = sb("cpv", [P, DEPTH, 2 * NB * 2])
        cso = sb("cso", [P, 2, NS, 2])
        cT = sb("cT", [P, KT, 32])
        adp = sb("adp", [P, 256])
        mod = [sb(f"mod{g}", [P, 24, NS]) for g in "ABC"]
        rt = sb("rt", [P, T])
        rst = sb("rst", [P, T])
        rst2 = sb("rst2", [P, T])
        acc = sb("acc", [P, T])
        pre = sb("pre", [P, KT, NB, TS])
        dec = sb("dec", [P, 2, 12])
        mx = sb("mx1", [P, 20])
        den = sb("den", [P, 20])
        with ExitStack() as ffn_scope:
            hh = ffn_scope.enter_context(nc.sbuf_tensor("hh", [P, FT, T], F32R))
            hl = ffn_scope.enter_context(nc.sbuf_tensor("hl", [P, FT, T], F32R))
        z = sb("z", [P, NZ, T])
        kc = sb("kc", [P, NB, WIN + TS])
        vc = sb("vc", [P, NB, P])
        s0 = sb("s0", [P, 2, NB, 64])
        big = sb("big", [P, 4920])
        PS = ctx.enter_context(nc.psum_tensor("PS", [P, 8, 512], F32))

        sg = y[:, 0:2, :]
        hf = y[:, 2:4, :]
        yf = y[:, :, :].rearrange("p a b -> p (a b)")
        sf = sq[:, :, :].rearrange("p a b -> p (a b)")
        kk, bb, eb = yf[:, 0:640], yf[:, 640:1280], yf[:, 1280:1920]
        tail = raw[:, :, W_IN:W_OUT]
        am = tail[:, :, 0:NL * CH]
        it_, kt_, at_ = (sf[:, n * 768:(n + 1) * 768] for n in range(3))
        zfl = z[:, :, :].rearrange("p a b -> p (a b)")
        first = [zfl[:, 0:2048], zfl[:, 2048:4096], zfl[:, 4096:6144], big[:, 0:2048], big[:, 2048:4096],
                 yf[:, 0:2048], ada[:, :, :].rearrange("p a b -> p (a b)"), zfl[:, 0:2048]]
        vtok = it_.rearrange("p (a b) -> p a b", a=3)
        ktok = kt_.rearrange("p (a b) -> p a b", a=3)
        AT = at_.rearrange("p (h c t) -> p h c t", h=4, c=3)
        LV = big[:, 0:3840].rearrange("p (l a t) -> p l (a t)", l=6, a=2)
        DS = tail[:, :, 0:512].rearrange("p s (c a v) -> p s c a v", c=2, a=2)
        vm = yf[0:64, 0:2048].rearrange("p (h b v) -> p h b v", h=4, b=NB)
        SC0 = big[:, 0:8 * 129].rearrange("p (h k) -> p h k", h=8)
        SC1 = big[:, 1032:3088].rearrange("p (h k) -> p h k", h=8)
        SS = big[:, 3088:3860].rearrange("p (n g k) -> p n g k", n=2, g=2)
        va = big[:, 3860:4244].rearrange("p (a b) -> p a b", a=3)
        up = big[:, 4244:4920].rearrange("p (a t) -> p a t", a=2)
        PT = yf[:, 0:2048].rearrange("p (s t) -> p s t", s=4)
        qs = tail[:, 1, 512:768].rearrange("p (b r) -> p b r", b=NB)
        PT0 = sf[:, 0:1024].rearrange("p (s t) -> p s t", s=2)
        PC = sf[:, 0:512]
        PN = sf[0:64, 512:1024]

        ident = cst[:, C_ID:C_ID + P]
        rotm = cst[:, C_ROT:C_ROT + P]
        ones = cst[:, C_ONE:C_ONE + P]
        bd = cst[:, C_BD:C_BD + P]
        sel = cst[:, C_SEL:C_SEL + NS]
        cosT = cst[:, C_COS:C_COS + T]
        sinT = cst[:, C_SIN:C_SIN + T]
        mskp = cst[:, C_MP:C_MP + 256]
        msks = cst[:, C_MS:C_MS + 384].rearrange("p (g k) -> p g k", g=2)
        gram = cst[:, C_GR:C_GR + NL * CH]
        seqm = cst[:, C_SQ:C_SQ + NB]
        rset = cst[:, C_RS:C_RS + T]

        adps = [adp[:, :], yf[:, 2048:2304]]

        s_load = sem("s_load")
        s_late = sem("s_late")
        s_xin = sem("s_xin")
        s_first = [sem(f"s_first{i}") for i in range(START)]
        s_raw = [sem(f"s_raw{i}") for i in (0, 1)]
        s_hi = [sem(f"s_hi{i}") for i in (0, 1)]
        s_lo = [sem(f"s_lo{i}") for i in (0, 1)]
        s_used = [sem(f"s_used{i}") for i in (0, 1)]
        s_ada = [sem(f"s_ada{i}") for i in (0, 1)]
        s_part = sem("s_part")
        s_adp = sem("s_adp")
        s_adt = sem("s_adt")
        s_mod = sem("s_mod")
        s_c = sem("s_c")
        s_gread = sem("s_gread")
        s_uread = sem("s_uread")
        s_hh = sem("s_hh")
        s_hl = sem("s_hl")
        s_sqp = sem("s_sqp")
        s_sqd = sem("s_sqd")
        s_acc = sem("s_acc")
        s_acc0 = sem("s_acc0")
        s_pst = sem("s_pst")
        s_pr = sem("s_pr")
        s_x = sem("s_x")
        s_xs = sem("s_xs")
        s_sqx = sem("s_sqx")
        s_sqa = sem("s_sqa")
        s_xst = sem("s_xst")
        s_r = sem("s_r")
        s_pre = sem("s_pre")
        s_mt = sem("s_mt")
        s_hmh = sem("s_hmh")
        s_hml = sem("s_hml")
        s_ms = sem("s_ms")
        s_hms = sem("s_hms")
        s_hls = sem("s_hls")
        s_za = sem("s_za")
        s_zd = sem("s_zd")
        s_cache = sem("s_cache")
        s_out = sem("s_out")
        s_st = sem("s_st")
        s_rt0 = sem("s_rt0")
        s_ach = sem("s_ach")
        s_dch = sem("s_dch")
        s_pch = sem("s_pch")
        s_held = sem("s_held")
        s_pch2 = sem("s_pch2")
        ev = {}
        events = """
            lb_less_max: the forget bounds less their maximum
            lb_exp: their exponentials
            c_padded: cT's padding is zero
            gates_scales: a group's gates and scales are final (the first group's at the start)
            forget: 1 / (1 + exp(-f)) within its bounds
            log_forget: its logarithm
            cum_log: its sum within each chunk
            level_dist: three levels' distances
            level_decay: their exponentials
            levels: all levels times q or k
            decay: decay since the chunk's start
            chunk_decay: decay over whole chunks, copied
            q_decayed: decay times q
            end_dist: distance from the chunk's end
            end_decay: its exponential
            k_decayed: times k
            i_turned: recurrence's values, token-major, in PSUM
            i_token: in SBUF
            kd_turned: decayed keys, token-major, in PSUM
            kd_token: in SBUF
            gram_raw: a unit of Gram matrices, in PSUM
            gram_masked: a bank of them masked
            gram_sum: summed over the levels
            state_added: what each chunk adds to the state, in PSUM
            states: states after each chunk
            rec_out: the recurrence's outputs, in PSUM
            rec_out_s0: the samples' part from their states, in PSUM
            rec_copied: outputs copied; that part added
            rec_sq: their squares
            rec_ms: sums over each head
            rec_rstd: reciprocal root mean squares
            rec_gated: normalised and gated
            rec_hi: hi of it
            v_by_seq: samples' values by sequence
            s0_decayed: samples' states times the decay
            s0_added: what their tokens add, in PSUM
            s0_new: their new states
            rotated: a round of rotated queries and keys, in PSUM
            sines: times the sine
            roped: a round of the rotary embedding is done
            qk_by_seq: samples' queries and keys by sequence
            v_turned: attention's values, token-major, in PSUM
            v_token: in SBUF
            scores1: half of the second block's scores, in PSUM
            scores0: the first block's
            scores_read: scaled and masked in SBUF
            maxima: a block's maxima
            exps: exponentials and sums (blocks, then samples)
            probs0: first block's probabilities
            probs1: second block's
            scores_s: samples' scores, in PSUM
            scores_s_read: in SBUF
            maxima_s: their maxima
            probs_s: their probabilities
            probs_turned: probabilities, key-major, in PSUM
            probs_keys: in SBUF
            attn_out: attention outputs, in PSUM
            attn_hi: hi of them
            conv_done: the convolution's output
            conv_hi: hi of it
            mixed_lo: lo of a part of the output projection's input
            """
        for line in events.strip().splitlines():
            n = line.split(":")[0].strip()
            ev[n] = sem("e_" + n)

        WIN_ = A["w_in"].rearrange("l f u p n -> (l f u) p n")
        WOUT = A["w_out"].rearrange("l f u p n -> (l f u) p n")
        MIN_ = A["m_in"].rearrange("l u p n -> (l u) p n")
        MOUT = A["m_out"].rearrange("l u p n -> (l u) p n")
        ADA = A["ada_w"].rearrange("l u p n -> (l u) p n")

        class Chain:

            def __init__(self, eng, s, per_layer):
                self.eng, self.s, self.per, self.base, self.n = eng, s, per_layer, 0, 0

            def mark(self, ins):
                self.n += 1
                ins.then_inc(self.s, 1)
                return self.base + self.n

            def wait(self, value):
                self.eng.wait_ge(self.s, value)

            def link(self, ins):
                self.wait(self.mark(ins))

        def by_seq(t, k0):
            return t[:, k0:k0 + KT, 1:NS].unsqueeze(3).to_broadcast([P, KT, NB, TS])

        def seq(t):
            return t[:, :, TP:T].rearrange("p k (b t) -> p k b t", t=TS)

        def hold(eng):
            eng.sem_inc(s_held, 1)

        block = ctx.enter_context(nc.Block())

        @block.sync
        def _(sp):
            sp.dma_start(cT[:, :, 0:NS], A["c"]).then_inc(s_load, 16)
            sp.dma_start(cst[:, 0:C_COS], A["cst"][:, 0:C_COS]).then_inc(s_load, 16)
            sp.dma_start(par2[:], A["par"].rearrange("l p n -> p l n")).then_inc(s_load, 16)
            sp.dma_start(lb2[:], A["lb"]).then_inc(s_load, 16)
            sp.dma_start(x[:], A["x"]).then_inc(s_xin, 16)
            for u in range(START):
                if u == START - 1:
                    sp.wait_ge(s_part, 2)
                sp.dma_start(first[u], ADA[(DEPTH - 1) * UNITS + U_C + 4 + u]).then_inc(s_first[u], 16)

            def conditioning(u, src):
                sp.wait_ge(s_part, u + 1)
                for half in (0, 1):
                    sp.dma_start(ada[:, half, :], src[:, 1024 * half:1024 * (half + 1)]).then_inc(s_ada[half], 16)

            def weights(g, slot, src, width):
                sp.wait_ge(s_hi[slot], g + 1)
                sp.wait_ge(s_lo[slot], g + 1)
                sp.dma_start(raw[:, slot, 0:width], src).then_inc(s_raw[slot], 16)

            def unit(l, u):
                conditioning(START + l * UNITS + u, ADA[l * UNITS + u])

            def ffn_in(l, f, off, uoff):
                def both(it):
                    for slot in (0, 1):
                        weights(l * ITS + off + it, slot, WIN_[(l * 2 + f) * 2 * IT_IN + it * 2 + slot], W_IN)

                both(0)
                if uoff is not None:
                    unit(l, uoff)
                    unit(l, uoff + 1)
                with sp.Fori(1, IT_IN) as it:
                    both(it)
                    if uoff is not None:
                        unit(l, uoff + 1 + it)

            def ffn_out(l, f, off, uoff):
                with sp.Fori(0, IT_OUT) as it:
                    for slot in (0, 1):
                        weights(l * ITS + off + it, slot, WOUT[(l * 2 + f) * 2 * IT_OUT + it * 2 + slot], W_OUT)
                    if uoff is not None:
                        unit(l, uoff + it)

            with sp.Fori(0, DEPTH) as l:
                ffn_in(l, 0, OFF_F0I, U_A)
                ffn_out(l, 0, OFF_F0O, U_B)
                for it in range(IT_MI):
                    for slot in (0, 1):
                        weights(l * ITS + OFF_MI + it, slot, MIN_[l * 2 * IT_MI + it * 2 + slot], W_IN)
                    if it == 0:
                        unit(l, U_B + 4)
                        unit(l, U_B + 5)
                    unit(l, U_B + 6 + it)
                    if it == 0:
                        sp.wait_ge(s_used[1], l * ITS + OFF_MI + 1)
                        sp.dma_start(kc[:, :, 0:WIN], A["k"][l]).then_inc(s_cache, 16)
                        sp.dma_start(vc[:], A["v"][l]).then_inc(s_cache, 16)
                        sp.dma_start(s0[:], A["s"][l]).then_inc(s_cache, 16)
                for it in range(IT_MO):
                    for slot in (0, 1):
                        weights(l * ITS + OFF_MO + it, slot, MOUT[l * 2 * IT_MO + it * 2 + slot], W_IN)
                    if it == 0:
                        unit(l, U_B + 11)
                ffn_in(l, 1, OFF_F1I, U_C)
                ffn_out(l, 1, OFF_F1O, None)
            sp.wait_ge(s_xs, 3 * DEPTH + 1)
            for k in range(0, KT, 2):
                sp.wait_ge(s_x, KT * 3 * DEPTH + k + 2)
                sp.dma_start(O["x"][:, k:k + 2, :], x[:, k:k + 2, :]).then_inc(s_out, 16)
            sp.wait_ge(s_out, 16 * (KT // 2 + 7 * DEPTH))
            sp.wait_ge(s_st, 32 * DEPTH)

        @block.tensor
        def _(pe):
            mm = nc.tensor.matmul

            def mm3(out, slot, col, rhi, rlo, first, last):
                hi, lo = WHI[:, slot, col:col + P], WLO[:, slot, col:col + P]
                mm(out, hi, rhi, start=first, stop=False)
                mm(out, hi, rlo, start=False, stop=False)
                return mm(out, lo, rhi, start=False, stop=last)

            def partial(u, src=None):
                if src is None:
                    pe.wait_ge(s_ada[0], 16 * (u - START + 1))
                    pe.wait_ge(s_ada[1], 16 * (u - START + 1))
                    src = first[6]
                    bank = 6
                    pe.wait_ge(s_adp, u + 1)
                else:
                    pe.wait_ge(s_first[u], 16)
                    bank = 6 - 2 * (u % 2)
                    if u > 1:
                        pe.wait_ge(s_adp, u)
                for i in (0, 1):
                    for j in range(4):
                        k = 2 * j + i
                        last = mm(PS[32 * j:32 * j + 32, bank, 0:256], cT[:, k, :], src[:, k * 256:(k + 1) * 256],
                                  start=(i == 0), stop=(i == 1))
                last.then_inc(s_part, 1)

            def summed(u, adp=adp):
                pe.wait_ge(s_adp, u + 2)
                pe.wait_ge(s_mod, u + 1)
                for i in (0, 1):
                    last = mm(PS[:, 7, 16 * i:16 * i + NS], adp[:, i * P:(i + 1) * P], sel, start=True, stop=True)
                last.then_inc(s_adt, 1)

            def split_ready(slot, g):
                pe.wait_ge(s_hi[slot], g + 2)
                pe.wait_ge(s_lo[slot], g + 2)

            def pair(slot, bank, norm=None, hook=None):
                if norm is not None:
                    pe.wait_ge(s_hls, norm + 1)
                for t in (0, 1):
                    for k in range(KT):
                        if norm is not None and t == 0:
                            pe.wait_ge(s_hml, KT * norm + k + 1)
                        last = mm3(PS[:, bank + t, 0:T], slot, k * 256 + t * P, hmh[:, k, :], hml[:, k, :],
                                   k == 0, k == KT - 1)
                        if hook:
                            hook(t * KT + k)
                last.then_inc(s_used[slot], 1)

            def keep_busy(n, bank, t):
                for _ in range(n):
                    mm(PS[:, bank, 0:T], t[:, 0:P], t[:, 0:T], start=True, stop=True)

            def x_stats(n):
                for k in range(SUMMED):
                    pe.wait_ge(s_sqx, KT * n + k + 1)
                    mm(PS[:, 5, 0:T], ones, sq[:, k, :], start=(k == 0), stop=False)
                pe.wait_ge(s_sqa, 2 * (n + 1))
                mm(PS[:, 5, 0:T], ones, sq[:, SUMMED, :], start=False, stop=True).then_inc(s_xst, 1)

            def y_stats(n, bank):
                pe.wait_ge(s_acc, 4 * n + 5)
                mm(PS[:, bank, 0:T], ones, acc[:], start=True, stop=True).then_inc(s_pst, 1)
                keep_busy(8, 1, hmh[:, 0])

            def ffn_in(l, f, off, uoff):
                if uoff is not None:
                    u0 = START + l * UNITS + uoff
                    partial(u0)

                def body(it, n=None):
                    g = l * ITS + off + it
                    split_ready(0, g)
                    pe.wait_ge(s_gread, (2 * l + f) * IT_IN + it + 1)
                    pair(0, 0, n)
                    if uoff is not None:
                        summed(u0 + it)
                        partial(u0 + 1 + it)
                    split_ready(1, g)
                    pe.wait_ge(s_uread, (2 * l + f) * IT_IN + it + 1)
                    pair(1, 2)

                body(0, 3 * l + 2 * f)
                hold(pe)
                with pe.Fori(1, IT_IN) as it:
                    body(it)
                if uoff is not None:
                    summed(u0 + IT_IN)

            def ffn_out(l, f, off, uoff):
                pe.wait_ge(s_hl, (2 * l + f) * IT_IN + (FT // 2 + 1) // 2 + 1)
                hold(pe)
                with pe.Fori(0, IT_OUT) as it:
                    g = l * ITS + off + it
                    if uoff is not None:
                        partial(START + l * UNITS + uoff + it)
                    pe.wait_ge(s_sqp, 4 * (3 * l + 2 * f) + it + 1)
                    for slot in (0, 1):
                        split_ready(slot, g)
                        if slot:
                            pe.wait_ge(s_hl, (2 * l + f + 1) * IT_IN + 1)
                        for t in (0, 1):
                            for i in range(FT // 2):
                                k = slot * (FT // 2) + i
                                last = mm3(PS[:, 4 + t, 0:T], slot, i * 256 + t * P, hh[:, k, :], hl[:, k, :],
                                           k == 0, k == FT - 1)
                        last.then_inc(s_used[slot], 1)
                    if uoff is not None:
                        summed(START + l * UNITS + uoff + it)

            def turn(src, bank, done):
                for t in range(3):
                    for a in (0, 1):
                        w = P if t < 2 else NB * TS
                        out = PS[0:w, bank + t // 2, (t % 2) * 256 + a * P:(t % 2) * 256 + (a + 1) * P]
                        last = nc.tensor.transpose(out, src(a)[:, t * P:t * P + w], ident)
                last.then_inc(done, 1)

            def rotated(tiles):
                for n, t in enumerate(tiles):
                    last = mm(PS[:, 4 + n, 0:T], rotm, z[:, t, :], start=True, stop=True)
                last.then_inc(ev["rotated"], 1)

            def values(l):
                for t in range(3):
                    w = P if t < 2 else NB * TS
                    last = nc.tensor.transpose(PS[0:w, 5, t * P:(t + 1) * P], z[:, Z_V, t * P:t * P + w], ident)
                last.then_inc(ev["v_turned"], 1)

            def mixer(l):
                pe.wait_ge(ev["k_decayed"], l + 1)
                pe.wait_ge(ev["sines"], 3 * l + 3)
                pe.wait_ge(ev["v_token"], l + 1)
                turn(lambda a: z[:, Z_F + a, :], 4, ev["kd_turned"])
                pe.wait_ge(ev["levels"], l + 1)
                pe.wait_ge(s_za, 5 * l + 6)
                pe.wait_ge(s_zd, 5 * l + 6)
                n = 0
                for a in (0, 1):
                    for cp in range(3):
                        bank = 2 - 2 * (n % 2)
                        if n >= 2:
                            pe.wait_ge(ev["gram_masked"], 12 * l + 2 * n - 2)
                        hold(pe)
                        for i, lv in enumerate(LEVELS[:NL if cp < 2 else NLS]):
                            for c in ((2 * cp, 2 * cp + 1) if cp < 2 else (4,)):
                                for e in (0, 1):
                                    rows = slice(64 * e, 64 * e + 64)
                                    col = a * T + c * CH
                                    if lv == DIAG:
                                        left, right = kk[rows, col:col + CH], z[rows, Z_Q + a, c * CH:(c + 1) * CH]
                                    else:
                                        left = right = LV[rows, lv, col:col + CH]
                                    p0 = 64 * (c % 2)
                                    last = mm(PS[p0:p0 + 64, bank + e, i * CH:(i + 1) * CH], left, right,
                                              start=True, stop=True)
                        last.then_inc(ev["gram_raw"], 1)
                        n += 1
                        if n < 5:
                            keep_busy(3, 6, WHI[:, 0])
                        if n == 2:
                            pe.wait_ge(ev["kd_token"], l + 1)
                            hold(pe)
                            for c2 in (0, 1):
                                for b in (0, 1):
                                    for c in (0, 1):
                                        rows = slice(64 * c, 64 * c + 64)
                                        last = mm(PS[:, 4 + c, c2 * 256 + b * P:c2 * 256 + (b + 1) * P],
                                                  ktok[rows, c2, b * P:(b + 1) * P], vtok[rows, c2, b * P:(b + 1) * P],
                                                  start=True, stop=True)
                            last.then_inc(ev["state_added"], 1)
                        if n == 4:
                            partial(START + l * UNITS + U_B + 11)
                        if n == 5:
                            summed(START + l * UNITS + U_B + 11)
                            keep_busy(6, 6, WHI[:, 0])
                pe.wait_ge(ev["roped"], 3 * l + 3)
                pe.wait_ge(ev["gram_masked"], 12 * (l + 1))
                hold(pe)
                for t in range(NG):
                    for n in (0, 1):
                        rows = slice(64 * n, 64 * n + 64)
                        last = mm(PS[:, 2 * n + t // 2, (t % 2) * 256:(t % 2 + 1) * 256],
                                  z[rows, Z_A + t, P:TP], z[rows, Z_K, 0:TP], start=True, stop=True)
                    if t % 2:
                        last.then_inc(ev["scores1"], 1)
                        keep_busy(3, 6, WHI[:, 0])
                pe.wait_ge(ev["states"], l + 1)
                pe.wait_ge(ev["gram_sum"], 12 * (l + 1))
                pe.wait_ge(ev["q_decayed"], l + 1)
                hold(pe)
                for c in range(5):
                    rows = slice(64 * (c % 2), 64 * (c % 2) + 64)
                    for a in (0, 1):
                        w = 3 if c % 2 == 0 else 2
                        col = (a * w + c // 2) * CH
                        if 0 < c < 4:
                            d = c - 1
                            mm(PS[:, 4 + c % 2, col:col + CH], DS[:, d // 2, d % 2, a, :],
                               eb[:, a * T + c * CH:a * T + (c + 1) * CH], start=True, stop=False)
                        for e in (0, 1):
                            last = mm(PS[64 * e:64 * e + 64, 4 + c % 2, col:col + CH],
                                      vtok[rows, c // 2, a * P + 64 * e:a * P + 64 * e + 64],
                                      AT[rows, 2 * a + e, c // 2, :], start=(c in (0, 4)), stop=True)
                last.then_inc(ev["rec_out"], 1)
                pe.wait_ge(s_cache, 48 * (l + 1))
                pe.wait_ge(ev["scores_read"], 3 * l + 1)
                hold(pe)
                for a in (0, 1):
                    for b in range(NB):
                        for e in (0, 1):
                            rows = slice(64 * e, 64 * e + 64)
                            col = a * T + TP + TS * b
                            last = mm(PS[rows, e, a * 64 + TS * b:a * 64 + TS * (b + 1)],
                                      s0[rows, a, b, :], eb[rows, col:col + TS], start=True, stop=True)
                last.then_inc(ev["rec_out_s0"], 1)
                for t in range(NG):
                    for n in (0, 1):
                        rows = slice(64 * n, 64 * n + 64)
                        last = mm(PS[:, 2 + n, t * P:(t + 1) * P], z[rows, Z_A + t, 0:P], z[rows, Z_K, 0:P],
                                  start=True, stop=True)
                last.then_inc(ev["scores0"], 1)
                pe.wait_ge(ev["rec_sq"], l + 1)
                for a in (0, 1):
                    last = mm(PS[:, 4 + a, 0:T], bd, z[:, Z_I + a, :], start=True, stop=True)
                last.then_inc(ev["rec_ms"], 1)
                keep_busy(4, 6, WHI[:, 0])
                pe.wait_ge(ev["v_by_seq"], l + 1)
                pe.wait_ge(ev["rec_copied"], 2 * (l + 1))
                hold(pe)
                for a in (0, 1):
                    for e in (0, 1):
                        h = 2 * a + e
                        last = mm(PS[64 * e:64 * e + 64, a, :], ktok[0:64, 2, 64 * h:64 * h + 64],
                                  vm[:, h].rearrange("p b v -> p (b v)"), start=True, stop=True)
                last.then_inc(ev["s0_added"], 1)
                pe.wait_ge(ev["scores_read"], 3 * l + 3)
                pe.wait_ge(ev["qk_by_seq"], l + 1)
                hold(pe)
                for b in range(NB):
                    for n in (0, 1):
                        rows = slice(64 * n, 64 * n + 64)
                        q = qs[rows, b, :]
                        p0, c0 = 32 * (b % 4), 192 * (b // 4)
                        mm(PS[p0:p0 + 32, 2 + n, c0:c0 + WIN], q, kc[rows, b, 0:WIN], start=True, stop=True)
                        last = mm(PS[p0:p0 + 32, 2 + n, c0 + WIN:c0 + 192], q, kc[rows, :, WIN:WIN + TS],
                                  start=True, stop=True)
                last.then_inc(ev["scores_s"], 1)
                pe.wait_ge(ev["probs0"], l + 1)
                pe.wait_ge(ev["rec_rstd"], l + 1)
                for n in (0, 1):
                    for t in range(NG):
                        last = nc.tensor.transpose(PS[:, 4 + n, t * P:(t + 1) * P], SC0[:, NG * n + t, 0:P], ident)
                last.then_inc(ev["probs_turned"], 1)
                pe.wait_ge(ev["probs_keys"], 4 * l + 1)
                pe.wait_ge(ev["probs1"], l + 1)
                pe.wait_ge(ev["scores_s_read"], l + 1)
                for s in range(4):
                    kb, n = s // 2, s % 2
                    for t in range(NG):
                        last = nc.tensor.transpose(PS[:, 2 + s, t * P:(t + 1) * P],
                                                   SC1[:, NG * n + t, kb * P:(kb + 1) * P], ident)
                    if n:
                        last.then_inc(ev["probs_turned"], 1)
                pe.wait_ge(ev["s0_new"], l + 1)
                hold(pe)
                for n in (0, 1):
                    last = mm(PS[64 * n:64 * n + 64, 0, :], va[:, 0, 64 * n:64 * n + 64], PT0[:, n, :],
                              start=True, stop=True)
                last.then_inc(ev["attn_out"], 1)
                pe.wait_ge(ev["probs_keys"], 4 * l + 3)
                hold(pe)
                for n in (0, 1):
                    for kb in (0, 1):
                        last = mm(PS[64 * n:64 * n + 64, 1, :], va[:, kb, 64 * n:64 * n + 64], PT[:, 2 * kb + n, :],
                                  start=(kb == 0), stop=(kb == 1))
                last.then_inc(ev["attn_out"], 1)
                pe.wait_ge(ev["probs_s"], l + 1)
                for n in (0, 1):
                    for g in (0, 1):
                        c0 = (2 * n + g) * P
                        nc.tensor.transpose(PS[:, 4, c0:c0 + P], SS[:, n, g, 0:WIN], ident)
                        last = nc.tensor.transpose(PS[0:64, 5, c0:c0 + P], SS[:, n, g, WIN:192], ident)
                last.then_inc(ev["probs_turned"], 1)
                pe.wait_ge(ev["probs_keys"], 4 * l + 4)
                hold(pe)
                for n in (0, 1):
                    rows = slice(64 * n, 64 * n + 64)
                    mm(PS[rows, 2, 0:256], va[0:64, 2, rows], PN[:, 256 * n:256 * (n + 1)], start=True, stop=True)
                    for b in range(NB):
                        c0 = (b // 4) * P + 32 * (b % 4)
                        last = mm(PS[rows, 2, c0:c0 + 32], vc[:, b, rows], PC[:, 256 * n + c0:256 * n + c0 + 32],
                                  start=False, stop=True, skip_group_check=True)
                last.then_inc(ev["attn_out"], 1)

            pe.wait_ge(s_c, 1)
            pe.wait_ge(s_load, 16 * 4)
            x_stats(0)
            for u in range(START):
                partial(u, first[u])
                if u:
                    summed(u - 1, adps[(u - 1) % 2])
            summed(START - 1, adps[(START - 1) % 2])
            with pe.Fori(0, DEPTH) as l:
                ffn_in(l, 0, OFF_F0I, U_A)
                ffn_out(l, 0, OFF_F0O, U_B)
                y_stats(3 * l, 0)
                partial(START + l * UNITS + U_B + 4)
                x_stats(3 * l + 1)
                summed(START + l * UNITS + U_B + 4)
                partial(START + l * UNITS + U_B + 5)
                for it in range(IT_MI):
                    g = l * ITS + OFF_MI + it
                    split_ready(0, g)
                    pe.wait_ge(s_za, 5 * l + it + 1)
                    pair(0, 0, 3 * l + 1 if it == 0 else None)
                    if it == 2:
                        pe.wait_ge(s_za, 5 * l + 3)
                        pe.wait_ge(s_pr, 3 * l + 1)
                        turn(lambda a: z[:, Z_I + a, :], 4, ev["i_turned"])
                    if it == 3:
                        pe.wait_ge(s_za, 5 * l + 4)
                        pe.wait_ge(s_zd, 5 * l + 4)
                        pe.wait_ge(ev["i_token"], l + 1)
                        rotated((Z_K, Z_A))
                    if it == 4:
                        pe.wait_ge(ev["sines"], 3 * l + 2)
                        rotated((Z_A + 3,))
                        values(l)
                    if it == 0:
                        summed(START + l * UNITS + U_B + 5)
                    partial(START + l * UNITS + U_B + 6 + it)
                    split_ready(1, g)
                    pe.wait_ge(s_zd, 5 * l + it + 1)
                    pair(1, 2)
                    if it == 3:
                        pe.wait_ge(ev["sines"], 3 * l + 1)
                        rotated((Z_A + 1, Z_A + 2))
                    summed(START + l * UNITS + U_B + 6 + it)
                mixer(l)
                for it in range(IT_MO):
                    g = l * ITS + OFF_MO + it
                    split_ready(0, g)
                    if it == 0:
                        pe.wait_ge(ev["mixed_lo"], 4 * l + 3)
                        for ks in (range(4, KT), range(4)):
                            if ks[0] == 0:
                                pe.wait_ge(ev["mixed_lo"], 4 * (l + 1))
                            for t in (0, 1):
                                for k in ks:
                                    last = mm3(PS[:, t, 0:T], 0, k * 256 + t * P, hmh[:, k, :], hml[:, k, :],
                                               k == 4, k == 3)
                        last.then_inc(s_used[0], 1)
                    else:
                        pe.wait_ge(s_sqp, 12 * l + 6)
                        pair(0, 0)
                    split_ready(1, g)
                    if it == 1:
                        pe.wait_ge(s_sqp, 12 * l + 7)
                    pair(1, 2)
                y_stats(3 * l + 1, 4)
                x_stats(3 * l + 2)
                ffn_in(l, 1, OFF_F1I, U_C)
                ffn_out(l, 1, OFF_F1O, None)
                y_stats(3 * l + 2, 0)
                x_stats(3 * l + 3)

        @block.scalar
        def _(act):
            a_ = nc.scalar.activation
            ch = Chain(act, s_ach, ACT_CHAIN)

            def hi_split(slot, g, width):
                act.wait_ge(s_raw[slot], 16 * (g + 1))
                act.wait_ge(s_used[slot], g + 1)
                a_(WHI[:, slot, 0:width], raw[:, slot, 0:width], ACT.Copy).then_inc(s_hi[slot], 1)

            def ada_copy(u):
                act.wait_ge(s_part, u + 2)
                act.wait_ge(s_adt, u + 1)
                a_(adp[:], PS[:, 6, 0:256], ACT.Copy).then_inc(s_adp, 1)

            def exp_set():
                hold(act)
                nc.scalar.preload_act_table_set("natural_log_exp_and_others")

            def silu_set():
                hold(act)
                nc.scalar.preload_act_table_set("silu_and_others")

            def rms(bank, out, done, scale, ready, value):
                act.wait_ge(ready, value)
                ch.link(a_(rt[:], PS[:, bank, 0:T], ACT.Ln, bias=EPS, scale=scale))
                a_(out, rt[:], ACT.Exp, scale=-0.5).then_inc(done, 1)

            def x_rms(n):
                act.wait_ge(s_xs, n + 1)
                for k in range(KT):
                    act.wait_ge(s_x, KT * n + k + 1)
                    a_(sq[:, k, :], x[:, k, :], ACT.Square).then_inc(s_sqx, 1)
                rms(5, rst[:], s_r, 1.0 / D, s_xst, n + 1)

            def x_norm(n, m):
                for k in range(KT):
                    act.wait_ge(s_mt, KT * n + k + 1)
                    a_(hmh[:, k, 0:TP], sq[:, k, 0:TP], ACT.Identity, bias=mod[m][:, 8 + k, 0:1]).then_inc(s_hmh, 1)
                    if k == 0:
                        act.wait_ge(s_ms, n + 1)
                        a_(seq(hmh[:]), pre[:], ACT.Copy).then_inc(s_hms, 1)

            def y_norm(n, bank):
                rms(bank, rst2[:], s_pr, 1.0 / D, s_pst, n + 1)

            def squares(out_tiles, bank, pair_):
                act.wait_ge(s_acc, pair_ + 1)
                a_(sq[:, 0:2, :], PS[:, bank:bank + 2, 0:T], ACT.Square).then_inc(s_sqd, 1)
                return a_(y[:, out_tiles, :], PS[:, bank:bank + 2, 0:T], ACT.Copy)

            def ffn_in(l, f, off, uoff):
                silu_set()
                u0 = START + l * UNITS + uoff

                def body(it, width):
                    g = l * ITS + off + it
                    i = (2 * l + f) * IT_IN + it
                    act.wait_ge(s_used[0], g + 2)
                    act.wait_ge(s_uread, i + 1)
                    a_(sg, PS[:, 0:2, 0:T], ACT.Silu).then_inc(s_gread, 1)
                    hi_split(0, g + 1, width)
                    if uoff is not None:
                        ada_copy(u0 + 1 + it)
                    hi_split(1, g + 1, width)
                    act.wait_ge(s_uread, i + 2)
                    a_(hh[:, bass.ds(it * 2, 2), :], hf, ACT.Copy).then_inc(s_hh, 1)

                with act.Fori(0, IT_IN - 1) as it:
                    body(it, W_IN)
                body(IT_IN - 1, W_OUT)

            def ffn_out(l, f, off, uoff, n):
                exp_set()

                def body(it, width, end=False):
                    g = l * ITS + off + it
                    if width:
                        hi_split(0, g + 1, width)
                    if uoff is not None:
                        ada_copy(START + l * UNITS + uoff + it)
                    act.wait_ge(s_used[1], g + 2)
                    squares(bass.ds(it * 2, 2), 4, 4 * n + it).then_inc(s_sqp, 1)
                    if not end:
                        hi_split(1, g + 1, width)

                with act.Fori(0, IT_OUT - 1) as it:
                    body(it, W_OUT)
                body(IT_OUT - 1, W_IN if uoff is not None else 0, True)

            def forget(l, it):
                zf = z[:, Z_F:Z_F + 2, :]
                if it == 1:
                    act.wait_ge(ev["forget"], l + 1)
                    a_(zf, zf, ACT.Ln).then_inc(ev["log_forget"], 1)
                if it == 2:
                    act.wait_ge(ev["i_turned"], l + 1)
                    a_(vtok[:, 0:2, :], PS[:, 4, 0:512], ACT.Copy)
                    a_(vtok[0:64, 2, :], PS[0:64, 5, 0:256], ACT.Copy).then_inc(ev["i_token"], 1)
                    act.wait_ge(ev["level_dist"], 2 * l + 1)
                    a_(LV[:, 0:3, :], LV[:, 0:3, :], ACT.Exp).then_inc(ev["level_decay"], 1)
                    a_(eb, bb, ACT.Exp).then_inc(ev["decay"], 1)
                if it == 3:
                    act.wait_ge(ev["level_dist"], 2 * l + 2)
                    a_(LV[:, 3:6, :], LV[:, 3:6, :], ACT.Exp).then_inc(ev["level_decay"], 1)
                    act.wait_ge(ev["end_dist"], l + 1)
                    a_(zf, zf, ACT.Exp).then_inc(ev["end_decay"], 1)
                if it == 4:
                    act.wait_ge(ev["v_turned"], l + 1)
                    a_(va[:, 0:2, :], PS[:, 5, 0:256], ACT.Copy)
                    a_(va[0:64, 2, :], PS[0:64, 5, 256:384], ACT.Copy).then_inc(ev["v_token"], 1)

            def mixer(l):
                act.wait_ge(ev["kd_turned"], l + 1)
                a_(ktok[:, 0:2, :], PS[:, 4, 0:512], ACT.Copy)
                a_(ktok[0:64, 2, :], PS[0:64, 5, 0:256], ACT.Copy).then_inc(ev["kd_token"], 1)
                ada_copy(START + l * UNITS + U_B + 11)
                act.wait_ge(ev["conv_done"], l + 1)
                a_(hmh[:, 6:8, :], z[:, Z_CC:Z_CC + 2, :], ACT.Copy).then_inc(ev["conv_hi"], 1)
                act.wait_ge(ev["rec_out"], l + 1)
                o4 = z[:, Z_Q:Z_Q + 2, :].rearrange("p a (c t) -> p a c t", t=CH)
                a_(o4[:, :, 0:5:2, :], PS[:, 4, 0:6 * CH].rearrange("p (a c t) -> p a c t", a=2, c=3), ACT.Copy)
                a_(o4[:, :, 1:4:2, :], PS[:, 5, 0:4 * CH].rearrange("p (a c t) -> p a c t", a=2, c=2),
                   ACT.Copy).then_inc(ev["rec_copied"], 1)
                act.wait_ge(ev["maxima"], 2 * l + 1)
                for h in range(NH):
                    a_(SC1[:, h, :], SC1[:, h, :], ACT.Exp, bias=mx[:, 8 + h:9 + h], accum_out=den[:, 8 + h:9 + h])
                act.wait_ge(ev["rec_copied"], 2 * (l + 1))
                a_(z[:, Z_I:Z_I + 2, :], z[:, Z_Q:Z_Q + 2, :], ACT.Square).then_inc(ev["rec_sq"], 1)
                act.wait_ge(ev["maxima"], 2 * l + 2)
                for h in range(NH):
                    last = a_(SC0[:, h, :], SC0[:, h, :], ACT.Exp, bias=mx[:, h:h + 1], accum_out=den[:, h:h + 1])
                last.then_inc(ev["exps"], 1)
                act.wait_ge(ev["rec_ms"], l + 1)
                ch.link(a_(z[:, Z_I:Z_I + 2, :], PS[:, 4:6, 0:T], ACT.Ln, bias=EPS, scale=1.0 / HD))
                a_(z[:, Z_I:Z_I + 2, :], z[:, Z_I:Z_I + 2, :], ACT.Exp, scale=-0.5).then_inc(ev["rec_rstd"], 1)
                act.wait_ge(ev["probs_turned"], 4 * l + 1)
                a_(PT0, PS[:, 4:6, :], ACT.Copy).then_inc(ev["probs_keys"], 1)
                act.wait_ge(ev["maxima_s"], l + 1)
                for n in (0, 1):
                    for g in (0, 1):
                        i = 16 + 2 * n + g
                        last = a_(SS[:, n, g, :], SS[:, n, g, :], ACT.Exp, bias=mx[:, i:i + 1],
                                  accum_out=den[:, i:i + 1])
                last.then_inc(ev["exps"], 1)
                act.wait_ge(ev["rec_gated"], l + 1)
                a_(hmh[:, 4:6, :], z[:, Z_Q:Z_Q + 2, :], ACT.Copy).then_inc(ev["rec_hi"], 1)
                for i in (0, 1):
                    act.wait_ge(ev["probs_turned"], 4 * l + i + 2)
                    a_(PT[:, 2 * i:2 * i + 2, :], PS[:, 2 * i + 2:2 * i + 4, :], ACT.Copy).then_inc(ev["probs_keys"], 1)
                act.wait_ge(ev["attn_out"], 3 * l + 1)
                a_(hmh[:, 0:4, 0:P], PS[:, 0, :].rearrange("p (a t) -> p a t", a=4), ACT.Copy).then_inc(ev["attn_hi"], 1)
                act.wait_ge(ev["probs_turned"], 4 * l + 4)
                a_(PC, PS[:, 4, :], ACT.Copy)
                a_(PN, PS[0:64, 5, :], ACT.Copy).then_inc(ev["probs_keys"], 1)
                act.wait_ge(ev["attn_out"], 3 * l + 2)
                a_(hmh[:, 0:4, P:TP], PS[:, 1, :].rearrange("p (a t) -> p a t", a=4), ACT.Copy).then_inc(ev["attn_hi"], 1)
                act.wait_ge(ev["attn_out"], 3 * l + 3)
                for a in range(4):
                    last = a_(hmh[:, a, TP:T].rearrange("p (b t) -> p b t", t=TS),
                              PS[:, 2, 0:256].rearrange("p (b a t) -> p a b t", a=4, t=TS)[:, a], ACT.Copy)
                last.then_inc(ev["attn_hi"], 1)

            act.wait_ge(s_load, 16 * 4)
            act.wait_ge(ev["c_padded"], 1)
            silu_set()
            a_(cT[:, :, 0:NS], cT[:, :, 0:NS], ACT.Silu).then_inc(s_c, 1)
            act.wait_ge(ev["lb_less_max"], 1)
            exp_set()
            a_(lbt[:, 0:DEPTH, :], lbt[:, 0:DEPTH, :], ACT.Exp).then_inc(ev["lb_exp"], 1)
            act.wait_ge(s_xin, 16)
            for k in range(KT):
                a_(sq[:, k, :], x[:, k, :], ACT.Square).then_inc(s_sqx, 1)
            for u in range(START):
                act.wait_ge(s_part, u + 2)
                if u > 1:
                    act.wait_ge(s_adt, u)
                a_(adps[u % 2], PS[:, 6 - 2 * (u % 2), 0:256], ACT.Copy).then_inc(s_adp, 1)
                if u == 0:
                    act.wait_ge(s_xst, 1)
                    a_(rt[:], PS[:, 5, 0:T], ACT.Ln, bias=EPS, scale=1.0 / D).then_inc(s_rt0, 1)
                    act.wait_ge(s_rt0, 1)
                    a_(rst[:], rt[:], ACT.Exp, scale=-0.5).then_inc(s_r, 1)
            with act.Fori(0, DEPTH) as l:
                ch.base, ch.n = l * ACT_CHAIN, 0
                hi_split(0, l * ITS, W_IN)
                x_norm(3 * l, 2)
                ada_copy(START + l * UNITS + U_A)
                hi_split(1, l * ITS, W_IN)
                ffn_in(l, 0, OFF_F0I, U_A)
                ffn_out(l, 0, OFF_F0O, U_B, 3 * l)
                y_norm(3 * l, 0)
                ada_copy(START + l * UNITS + U_B + 4)
                hi_split(1, l * ITS + OFF_MI, W_IN)
                x_rms(3 * l + 1)
                x_norm(3 * l + 1, 0)
                ada_copy(START + l * UNITS + U_B + 5)
                for it in range(IT_MI):
                    g = l * ITS + OFF_MI + it
                    if 4 * it == Z_G:
                        silu_set()
                    act.wait_ge(s_used[0], g + 2)
                    a_(z[:, 4 * it:4 * it + 2, :], PS[:, 0:2, 0:T],
                       {Z_F: ACT.Exp, Z_G: ACT.Silu}.get(4 * it, ACT.Copy),
                       scale=-1.0 if 4 * it == Z_F else 1.0).then_inc(s_za, 1)
                    hi_split(0, g + 1, W_IN)
                    ada_copy(START + l * UNITS + U_B + 6 + it)
                    if it == 4:
                        forget(l, it)
                    hi_split(1, g + 1, W_IN)
                    if it < 4:
                        forget(l, it)
                exp_set()
                mixer(l)
                act.wait_ge(ev["states"], l + 1)
                for e in (0, 1):
                    act.dma_start(O["sp"][l, e],
                                  DS[64 * e:64 * e + 64, 1, 1, :, 64 * e:64 * e + 64]).then_inc(s_st, 16)
                act.wait_ge(ev["s0_new"], l + 1)
                act.dma_start(O["ss"][l], s0[:]).then_inc(s_out, 16)
                act.wait_ge(ev["qk_by_seq"], l + 1)
                act.dma_start(O["kp"][l], z[:, Z_K, P:TP]).then_inc(s_out, 16)
                act.dma_start(O["ks"][l], kc[:, :, TS:WIN + TS]).then_inc(s_out, 16)
                act.dma_start(O["vp"][l], va[:, 1, :]).then_inc(s_out, 16)
                act.dma_start(O["vs"][l, 0:WIN - TS], vc[TS:WIN, :, :]).then_inc(s_out, 16)
                act.dma_start(O["vn"][l], va[0:64, 2, :]).then_inc(s_out, 16)
                act.dma_start(O["conv"][l], cso[:]).then_inc(s_out, 16)
                for it in range(IT_MO):
                    g = l * ITS + OFF_MO + it
                    n = 12 * l + 4 + 2 * it
                    act.wait_ge(s_used[0], g + 2)
                    squares(slice(4 * it, 4 * it + 2), 0, n).then_inc(s_sqp, 1)
                    hi_split(0, g + 1, W_IN)
                    act.wait_ge(s_used[1], g + 2)
                    squares(slice(4 * it + 2, 4 * it + 4), 2, n + 1).then_inc(s_sqp, 1)
                    if it < IT_MO - 1:
                        hi_split(1, g + 1, W_IN)
                y_norm(3 * l + 1, 4)
                hi_split(1, l * ITS + OFF_F1I, W_IN)
                x_rms(3 * l + 2)
                x_norm(3 * l + 2, 1)
                act.wait_ge(s_out, 16 * 7 * (l + 1))
                act.wait_ge(s_st, 32 * (l + 1))
                ada_copy(START + l * UNITS + U_C)
                ffn_in(l, 1, OFF_F1I, U_C)
                ffn_out(l, 1, OFF_F1O, None, 3 * l + 2)
                y_norm(3 * l + 2, 0)
                x_rms(3 * l + 3)
                assert ch.n == ACT_CHAIN, ch.n

        @block.vector
        def _(dve):
            v = nc.vector
            tt, ts, stt = v.tensor_tensor, v.tensor_scalar, v.scalar_tensor_tensor
            ch = Chain(dve, s_dch, DVE_CHAIN)

            def lo_split(slot, g, width):
                dve.wait_ge(s_hi[slot], g + 2)
                tt(WLO[:, slot, 0:width], raw[:, slot, 0:width], WHI[:, slot, 0:width].bitcast(F32),
                   ALU.subtract).then_inc(s_lo[slot], 1)

            def mod_out(u, m, j, bias):
                dve.wait_ge(s_adt, u + 2)
                src = PS[:, 7, 0:32].rearrange("p (i s) -> p i s", i=2)[:, :, 0:NS]
                tt(mod[m][:, bass.ds(j, 2), :], src, bias.unsqueeze(2).to_broadcast([P, 2, NS]), ALU.add)\
                    .then_inc(s_mod, 1)

            def ready(u):
                dve.wait_ge(s_mod, u + 2)

            def group_bias(m, j):
                return par[:, bass.ds(R_AB + 24 * m + j, 2)]

            def gate_ready(m, sub, weight):
                g = mod[m][:, 0:KT, :]
                post = par[:, R_POST + KT * sub:R_POST + KT * (sub + 1)]
                ch.link(stt(g, g, weight, post.unsqueeze(2).to_broadcast([P, KT, NS]), ALU.mult, ALU.mult))

            def scale_ready(m, params):
                sc = mod[m][:, 16:24, :]
                pre = params[:, R_PRE + KT * m:R_PRE + KT * (m + 1)]
                return stt(sc, sc, 1.0, pre.unsqueeze(2).to_broadcast([P, KT, NS]), ALU.add, ALU.mult)

            def x_norm(n, m, also=None):
                dve.wait_ge(s_r, n + 1)

                def scaled(k):
                    stt(sq[:, k, 0:TP], x[:, k, 0:TP], mod[m][:, 16 + k, 0:1], rst[:, 0:TP],
                        ALU.mult, ALU.mult).then_inc(s_mt, 1)

                def low(k):
                    dve.wait_ge(s_hmh, KT * n + k + 1)
                    dve.wait_ge(s_mt, KT * n + k + 1)
                    stt(hml[:, k, 0:TP], sq[:, k, 0:TP], mod[m][:, 8 + k, 0:1], hmh[:, k, 0:TP].bitcast(F32),
                        ALU.add, ALU.subtract).then_inc(s_hml, 1)

                scaled(0)
                dve.wait_ge(s_pre, 2 * n + 1)
                done = ch.mark(tt(pre[:], pre[:], rst[:, TP:T].rearrange("p (b t) -> p b t", t=TS).unsqueeze(1)
                                  .to_broadcast([P, KT, NB, TS]), ALU.mult))
                scaled(1)
                ch.wait(done)
                tt(pre[:], pre[:], by_seq(mod[m], 8), ALU.add).then_inc(s_ms, 1)
                if also:
                    also()
                low(0)
                scaled(2)
                dve.wait_ge(s_hms, n + 1)
                dve.wait_ge(s_ms, n + 1)
                tt(seq(hml[:]), pre[:], seq(hmh[:].bitcast(F32)), ALU.subtract).then_inc(s_hls, 1)
                for k in range(1, KT):
                    if k + 2 < KT:
                        scaled(k + 2)
                    low(k)

            def y_norm(n, m):
                dve.wait_ge(s_pr, n + 1)
                dve.wait_ge(s_sqp, 4 * n + 5)
                done = {}

                def term(k):
                    done[k] = ch.mark(stt(sq[:, k, 0:TP], y[:, k, 0:TP], mod[m][:, k, 0:1], rst2[:, 0:TP],
                                          ALU.mult, ALU.mult))

                term(0)
                for k in range(KT):
                    if k + 1 < KT:
                        term(k + 1)
                    ch.wait(done[k])
                    tt(x[:, k, 0:TP], x[:, k, 0:TP], sq[:, k, 0:TP], ALU.add).then_inc(s_x, 1)

            def sum_squares(n):
                for i in range(2):
                    dve.wait_ge(s_sqx, KT * n + SUMMED + 2 + i)
                    if i:
                        dve.wait_ge(s_sqa, 2 * n + 1)
                    tt(sq[:, SUMMED, :], sq[:, SUMMED, :], sq[:, SUMMED + 1 + i, :], ALU.add).then_inc(s_sqa, 1)

            def add_squares(pair_):
                dve.wait_ge(s_sqd, pair_ + 1)
                dve.wait_ge(s_acc, pair_ + 1)
                tt(acc[:], acc[:], sq[:, 0, :], ALU.add).then_inc(s_acc0, 1)
                dve.wait_ge(s_acc0, pair_ + 1)
                tt(acc[:], acc[:], sq[:, 1, :], ALU.add).then_inc(s_acc, 1)

            def ffn_in(l, f, off, uoff, m):
                if uoff is not None:
                    u0 = START + l * UNITS + uoff

                def body(it, width):
                    g = l * ITS + off + it
                    i = (2 * l + f) * IT_IN + it
                    lo_split(0, g + 1, width)
                    dve.wait_ge(s_used[1], g + 2)
                    dve.wait_ge(s_gread, i + 2)
                    dve.wait_ge(s_hl, i + 1)
                    tt(hf, sg, PS[:, 2:4, 0:T], ALU.mult).then_inc(s_uread, 1)
                    if uoff is not None:
                        mod_out(u0 + it, m, 2 * it, group_bias(m, 2 * it))
                    lo_split(1, g + 1, width)
                    dve.wait_ge(s_hh, i + 1)
                    dve.wait_ge(s_uread, i + 2)
                    tt(hl[:, bass.ds(it * 2, 2), :], hf, hh[:, bass.ds(it * 2, 2), :].bitcast(F32),
                       ALU.subtract).then_inc(s_hl, 1)

                with dve.Fori(0, IT_IN - 1) as it:
                    body(it, W_IN)
                body(IT_IN - 1, W_OUT)
                if uoff is not None:
                    mod_out(u0 + IT_IN, m, 2 * IT_IN, group_bias(m, 2 * IT_IN))

            def ffn_out(l, f, off, uoff, m, sub, n):
                ready(START + l * UNITS + (U_A if f == 0 else U_C) + 11)
                gate_ready(m, sub, 0.5)
                scale_ready(m, par).then_inc(ev["gates_scales"], 1)
                dve.wait_ge(ev["gates_scales"], n + 2)
                ch.link(v.memset(acc[:], 0.0))
                hold(dve)

                def body(it, width, end=False):
                    g = l * ITS + off + it
                    if width:
                        lo_split(0, g + 1, width)
                    if uoff is not None and not end:
                        mod_out(START + l * UNITS + uoff + it, 1, 2 * it, group_bias(1, 2 * it))
                    add_squares(4 * n + it)
                    if not end:
                        lo_split(1, g + 1, width)

                with dve.Fori(0, IT_OUT - 1) as it:
                    body(it, W_OUT)
                body(IT_OUT - 1, W_IN if uoff is not None else 0, True)
                if uoff is not None:
                    it = IT_OUT - 1
                    mod_out(START + l * UNITS + uoff + it, 1, 2 * it, group_bias(1, 2 * it))

            def forget(l, it):
                zf = z[:, Z_F:Z_F + 2, :]
                zq1 = z[:, Z_Q:Z_Q + 2, :].rearrange("p a t -> p (a t)")
                if it == 0:
                    dve.wait_ge(s_za, 5 * l + 2)
                    ch.link(ts(zf, zf, 1.0, None, ALU.add))
                    ch.link(v.reciprocal(zf, zf))
                    for a in (0, 1):
                        last = ts(zf[:, a, :], zf[:, a, :], lbc[:, 1, a:a + 1], lbc[:, 0, a:a + 1],
                                  ALU.mult, ALU.add)
                    ch.link(last)
                    ts(kk, zf.rearrange("p a t -> p (a t)"), -1.0, 1.0, ALU.mult, ALU.add)
                    ts(zf, zf, FMIN, None, ALU.max).then_inc(ev["forget"], 1)
                if it == 1:
                    dve.wait_ge(s_late, 32)
                    dve.wait_ge(ev["log_forget"], l + 1)
                    for a in (0, 1):
                        last = v.tensor_tensor_scan(bb[:, a * T:(a + 1) * T], rset, zf[:, a, :], 0.0,
                                                    ALU.mult, ALU.add)
                    last.then_inc(ev["cum_log"], 1)
                    dve.wait_ge(ev["cum_log"], l + 1)
                if it in (1, 2):
                    s = it - 1
                    for lv in range(3 * s, 3 * s + 3):
                        h = 1 << lv
                        b3 = bb.rearrange("p (n w) -> p n w", w=2 * h)
                        last = tt(LV[:, lv, :].rearrange("p (n w) -> p n w", w=2 * h), b3,
                                  b3[:, :, h - 1:h].to_broadcast([P, 2 * T // (2 * h), 2 * h]), ALU.subtract)
                    ch.link(last)
                    w = LV[:, 3 * s:3 * s + 3, :]
                    stt(w, w, -1.0, w, ALU.mult, ALU.min).then_inc(ev["level_dist"], 1)
                if it in (3, 4):
                    s = it - 3
                    dve.wait_ge(ev["level_decay"], 2 * l + s + 1)
                    for lv in range(3 * s, 3 * s + 3):
                        h = 1 << lv
                        for side, src in ((0, kk), (1, zq1)):
                            o = LV[:, lv, :].rearrange("p (n s h) -> p n s h", s=2, h=h)[:, :, side, :]
                            last = tt(o, o, src.rearrange("p (n s h) -> p n s h", s=2, h=h)[:, :, side, :], ALU.mult)
                    if s:
                        last.then_inc(ev["levels"], 1)
                if it == 3:
                    dve.wait_ge(ev["decay"], l + 1)
                    e3 = eb.rearrange("p (a t) -> p a t", a=2)
                    v.tensor_copy(dec[:, :, 0:4], e3[:, :, CH - 1:TP:CH])
                    v.tensor_copy(dec[:, :, 4:12], e3[:, :, TP + TS - 1:T:TS]).then_inc(ev["chunk_decay"], 1)

            def sines(l, r):
                w = 2 if r < 2 else 1
                dve.wait_ge(ev["rotated"], 3 * l + r + 1)
                if r == 2:
                    dve.wait_ge(ev["roped"], 3 * l + 1)
                tt(tail[:, r % 2, 0:w * T].rearrange("p (n t) -> p n t", n=w), PS[:, 4:4 + w, 0:T],
                   sinT.unsqueeze(1).to_broadcast([P, w, T]), ALU.mult).then_inc(ev["sines"], 1)

            def mixer(l):
                dve.wait_ge(ev["roped"], 3 * l + 3)
                n = 0
                for a in (0, 1):
                    for cp in range(3):
                        rows, w = (slice(0, P), NL) if cp < 2 else (slice(0, 64), NLS)
                        dve.wait_ge(ev["gram_raw"], 6 * l + n + 1)
                        for e in (0, 1):
                            if n:
                                dve.wait_ge(ev["gram_sum"], 12 * l + 2 * n + e - 1)
                            tt(am[rows, e, 0:w * CH], PS[rows, 2 - 2 * (n % 2) + e, 0:w * CH], gram[rows, 0:w * CH],
                               ALU.mult).then_inc(ev["gram_masked"], 1)
                        for e in (0, 1):
                            dve.wait_ge(ev["gram_masked"], 12 * l + 2 * n + e + 1)
                            v.tensor_reduce(AT[rows, 2 * a + e, cp, :],
                                            am[rows, e, 0:w * CH].rearrange("p (i t) -> p t i", t=CH),
                                            AX.X, ALU.add).then_inc(ev["gram_sum"], 1)
                        n += 1
                dve.wait_ge(ev["gram_sum"], 12 * (l + 1))
                mod_out(START + l * UNITS + U_B + 11, 1, 22, group_bias(1, 22))
                dve.wait_ge(ev["state_added"], l + 1)
                for c in (0, 1):
                    last = tt(DS[:, :, c], PS[:, 4 + c, :].rearrange("p (c a v) -> p c a v", c=2, a=2),
                              bd.unsqueeze(1).unsqueeze(1).to_broadcast([P, 2, 2, P]), ALU.mult)
                ch.link(last)
                for c in range(1, 4):
                    d, b = DS[:, c // 2, c % 2], DS[:, (c - 1) // 2, (c - 1) % 2]
                    for a in (0, 1):
                        last = stt(d[:, a, :], b[:, a, :], dec[:, a, c:c + 1], d[:, a, :], ALU.mult, ALU.add)
                    if c < 3:
                        ch.link(last)
                last.then_inc(ev["states"], 1)
                sink = par[:, R_SINK:R_SINK + NH].unsqueeze(2)
                v.tensor_copy(SC0[:, :, 128:129], sink)
                v.tensor_copy(SC1[:, :, 256:257], sink)
                v.tensor_copy(SS[:, :, :, 192:193],
                              par[:, R_SINKS:R_SINKS + 2].unsqueeze(2).unsqueeze(3).to_broadcast([P, 2, 2, 1]))
                for i in (0, 2, 1, 3):
                    dve.wait_ge(ev["scores1"], 2 * l + i % 2 + 1)
                    last = stt(SC1[:, 2 * i:2 * i + 2, 0:256], PS[:, i, :].rearrange("p (h k) -> p h k", h=2), SCALE,
                               mskp.unsqueeze(1).to_broadcast([P, 2, 256]), ALU.mult, ALU.add)
                last.then_inc(ev["scores_read"], 1)
                dve.wait_ge(ev["scores_read"], 3 * l + 1)
                v.tensor_reduce(mx[:, 8:16], SC1, AX.X, ALU.max, negate=True).then_inc(ev["maxima"], 1)
                dve.wait_ge(ev["rec_out_s0"], l + 1)
                dve.wait_ge(ev["rec_copied"], 2 * l + 1)
                for e in (0, 1):
                    rows = slice(64 * e, 64 * e + 64)
                    o = z[rows, Z_Q:Z_Q + 2, TP:T]
                    last = tt(o, o, PS[rows, e, 0:128].rearrange("p (a t) -> p a t", a=2), ALU.add)
                last.then_inc(ev["rec_copied"], 1)
                dve.wait_ge(ev["scores0"], l + 1)
                for n in (0, 1):
                    last = stt(SC0[:, 4 * n:4 * n + 4, 0:P], PS[:, 2 + n, :].rearrange("p (h k) -> p h k", h=4), SCALE,
                               mskp[:, 128:256].unsqueeze(1).to_broadcast([P, 4, P]), ALU.mult, ALU.add)
                    last.then_inc(ev["scores_read"], 1)
                dve.wait_ge(ev["scores_read"], 3 * l + 3)
                v.tensor_reduce(mx[:, 0:8], SC0, AX.X, ALU.max, negate=True).then_inc(ev["maxima"], 1)
                v.tensor_copy(kc[:, :, WIN:WIN + TS], z[:, Z_K, TP:T].rearrange("p (b t) -> p b t", t=TS))
                v.tensor_copy(qs.rearrange("p b (a t) -> p a b t", t=TS), seq(z[:, Z_A:Z_A + 4, :]))\
                    .then_inc(ev["qk_by_seq"], 1)
                dve.wait_ge(ev["exps"], 2 * l + 1)
                ch.link(v.reciprocal(den[:, 0:16], den[:, 0:16]))
                tt(SC0[:, :, 0:P], SC0[:, :, 0:P], den[:, 0:8].unsqueeze(2).to_broadcast([P, 8, P]),
                   ALU.mult).then_inc(ev["probs0"], 1)
                dve.wait_ge(ev["s0_added"], l + 1)
                dve.wait_ge(ev["s0_decayed"], l + 1)
                for a in (0, 1):
                    last = tt(s0[:, a], s0[:, a], PS[:, a, :].rearrange("p (b v) -> p b v", v=64), ALU.add)
                last.then_inc(ev["s0_new"], 1)
                tt(SC1[:, :, 0:256], SC1[:, :, 0:256], den[:, 8:16].unsqueeze(2).to_broadcast([P, 8, 256]),
                   ALU.mult).then_inc(ev["probs1"], 1)
                dve.wait_ge(ev["scores_s"], l + 1)
                for n in (0, 1):
                    last = stt(SS[:, n, :, 0:192], PS[:, 2 + n, 0:384].rearrange("p (g k) -> p g k", g=2), SCALE,
                               msks, ALU.mult, ALU.add)
                last.then_inc(ev["scores_s_read"], 1)
                dve.wait_ge(ev["scores_s_read"], l + 1)
                v.tensor_reduce(mx[:, 16:20], SS.rearrange("p n g k -> p (n g) k"), AX.X, ALU.max, negate=True)\
                    .then_inc(ev["maxima_s"], 1)
                zo, zr = z[:, Z_Q:Z_Q + 2, :], z[:, Z_I:Z_I + 2, :]
                dve.wait_ge(ev["rec_rstd"], l + 1)
                ch.link(stt(zo, zo, par[:, R_GN:R_GN + 1], zr, ALU.mult, ALU.mult))
                tt(zo, zo, z[:, Z_G:Z_G + 2, :], ALU.mult).then_inc(ev["rec_gated"], 1)
                dve.wait_ge(ev["exps"], 2 * l + 2)
                ch.link(v.reciprocal(den[:, 16:20], den[:, 16:20]))
                s3 = SS.rearrange("p n g k -> p (n g) k")[:, :, 0:192]
                tt(s3, s3, den[:, 16:20].unsqueeze(2).to_broadcast([P, 4, 192]), ALU.mult).then_inc(ev["probs_s"], 1)
                dve.wait_ge(ev["rec_hi"], l + 1)
                dve.wait_ge(ev["rec_gated"], l + 1)
                tt(hml[:, 4:6, :], zo, hmh[:, 4:6, :].bitcast(F32), ALU.subtract).then_inc(ev["mixed_lo"], 1)
                dve.wait_ge(ev["conv_hi"], l + 1)
                tt(hml[:, 6:8, :], z[:, Z_CC:Z_CC + 2, :], hmh[:, 6:8, :].bitcast(F32),
                   ALU.subtract).then_inc(ev["mixed_lo"], 1)
                for blk in (0, 1):
                    dve.wait_ge(ev["attn_hi"], 3 * l + blk + 1)
                    last = tt(hml[:, 0:4, blk * P:(blk + 1) * P], PS[:, blk, :].rearrange("p (a t) -> p a t", a=4),
                              hmh[:, 0:4, blk * P:(blk + 1) * P].bitcast(F32), ALU.subtract)
                last.then_inc(ev["mixed_lo"], 1)
                dve.wait_ge(ev["attn_hi"], 3 * l + 3)
                tt(seq(hml[:, 0:4, :]), PS[:, 2, 0:256].rearrange("p (b a t) -> p a b t", a=4, t=TS),
                   seq(hmh[:, 0:4, :].bitcast(F32)), ALU.subtract).then_inc(ev["mixed_lo"], 1)

            dve.wait_ge(s_load, 16 * 4)
            ch2 = Chain(dve, s_pch2, 0)
            ch2.link(v.tensor_copy(lbt[:, 2, :], lb2[:, 0, :]))
            for d in range(1, DEPTH):
                ch2.link(tt(lbt[:, 2, :], lbt[:, 2, :], lb2[:, d, :], ALU.max))
            tt(lbt[:, 0:DEPTH, :], lb2[:], lbt[:, 2:3, :].to_broadcast([P, DEPTH, 2]), ALU.subtract)\
                .then_inc(ev["lb_less_max"], 1)
            dve.wait_ge(ev["lb_exp"], 1)
            ch2.link(v.tensor_copy(lbt[:, 2, :], lbt[:, 0, :]))
            for d in range(1, DEPTH):
                ch2.link(tt(lbt[:, 2, :], lbt[:, 2, :], lbt[:, d, :], ALU.add))
            ch2.link(v.reciprocal(lbt[:, 3, :], lbt[:, 2, :]))
            ch2.link(tt(lbt[:, 0:DEPTH, :], lbt[:, 0:DEPTH, :], lbt[:, 3:4, :].to_broadcast([P, DEPTH, 2]), ALU.mult))
            ch2.link(v.tensor_copy(lbt[:, 2, :], lbt[:, 0, :]))
            for d in range(DEPTH):
                if d:
                    ch2.link(tt(lbt[:, 2, :], lbt[:, 2, :], lbt[:, d, :], ALU.add))
                ch2.link(tt(lb2[:, d, :], lbt[:, 2, :], lbt[:, 0, :], ALU.subtract))
            sum_squares(0)
            for u in range(START):
                mod_out(u, 2, 8 + 2 * u, par2[:, DEPTH - 1, R_AB + 56 + 2 * u:R_AB + 58 + 2 * u])
            ready(START - 1)
            scale_ready(2, par2[:, DEPTH - 1, :]).then_inc(ev["gates_scales"], 1)
            dve.wait_ge(ev["gates_scales"], 1)
            with dve.Fori(0, DEPTH) as l:
                ch.base, ch.n = l * DVE_CHAIN, 0
                v.tensor_copy(lbc[:, 0, :], lb2[:, l, :])
                ts(lbc[:, 1, :], lb2[:, l, :], -1.0, 1.0, ALU.mult, ALU.add)
                ch.link(v.tensor_copy(par[:], par2[:, l, :]))
                x_norm(3 * l, 2, lambda: lo_split(0, l * ITS, W_IN))
                lo_split(1, l * ITS, W_IN)
                ffn_in(l, 0, OFF_F0I, U_A, 0)
                ffn_out(l, 0, OFF_F0O, U_B, 0, 0, 3 * l)
                y_norm(3 * l, 0)
                sum_squares(3 * l + 1)
                lo_split(1, l * ITS + OFF_MI, W_IN)
                x_norm(3 * l + 1, 0)
                mod_out(START + l * UNITS + U_B + 4, 1, 8, group_bias(1, 8))
                for it in range(IT_MI):
                    g = l * ITS + OFF_MI + it
                    if it == 4:
                        forget(l, it)
                    lo_split(0, g + 1, W_IN)
                    if it == 3:
                        sines(l, 0)
                    if it == 4:
                        sines(l, 2)
                    dve.wait_ge(s_used[1], g + 2)
                    v.tensor_copy(z[:, 4 * it + 2:4 * it + 4, :], PS[:, 2:4, 0:T]).then_inc(s_zd, 1)
                    if it == 0:
                        mod_out(START + l * UNITS + U_B + 5, 1, 10, group_bias(1, 10))
                    mod_out(START + l * UNITS + U_B + 6 + it, 1, 12 + 2 * it, group_bias(1, 12 + 2 * it))
                    lo_split(1, g + 1, W_IN)
                    if it == 3:
                        sines(l, 1)
                    if it < 4:
                        forget(l, it)
                mixer(l)
                ready(START + l * UNITS + U_B + 11)
                gate_ready(1, 1, 1.0)
                scale_ready(1, par).then_inc(ev["gates_scales"], 1)
                dve.wait_ge(ev["gates_scales"], 3 * l + 3)
                ch.link(v.memset(acc[:], 0.0))
                for it in range(IT_MO):
                    g = l * ITS + OFF_MO + it
                    n = 12 * l + 4 + 2 * it
                    add_squares(n)
                    lo_split(0, g + 1, W_IN)
                    add_squares(n + 1)
                    if it < IT_MO - 1:
                        lo_split(1, g + 1, W_IN)
                y_norm(3 * l + 1, 1)
                sum_squares(3 * l + 2)
                lo_split(1, l * ITS + OFF_F1I, W_IN)
                x_norm(3 * l + 2, 1)
                ffn_in(l, 1, OFF_F1I, U_C, 2)
                ffn_out(l, 1, OFF_F1O, None, 2, 2, 3 * l + 2)
                y_norm(3 * l + 2, 2)
                sum_squares(3 * l + 3)
                assert ch.n == DVE_CHAIN, ch.n

        @block.gpsimd
        def _(pool):
            g_ = nc.gpsimd
            tt = g_.tensor_tensor
            ch = Chain(pool, s_pch, POOL_CHAIN)
            for s in (*s_hi, *s_lo, *s_used, s_part, s_adp, s_adt, s_mod, s_gread, s_uread, s_hl,
                      s_sqp, s_acc, s_za, s_zd):
                pool.sem_inc(s, 1)
            g_.memset(cT[:, :, NS:32], 0.0).then_inc(ev["c_padded"], 1)
            pool.wait_ge(s_xin, 16)
            pool.sem_inc(s_xs, 1)
            pool.sem_inc(s_x, KT)
            rs2 = rst2[:, TP:T].rearrange("p (b t) -> p b t", t=TS).unsqueeze(1).to_broadcast([P, KT, NB, TS])

            def x_scaled(n, m):
                pool.wait_ge(ev["gates_scales"], n + 1)
                pool.wait_ge(s_xs, n + 1)
                tt(pre[:], seq(x[:]), by_seq(mod[m], 16), ALU.mult).then_inc(s_pre, 1)

            def y_norm(n, m):
                pool.wait_ge(ev["gates_scales"], n + 2)
                pool.wait_ge(s_sqp, 4 * n + 5)
                tt(pre[:], seq(y[:]), by_seq(mod[m], 0), ALU.mult).then_inc(s_pre, 1)
                pool.wait_ge(s_pre, 2 * n + 2)
                pool.wait_ge(s_pr, n + 1)
                ch.link(tt(pre[:], pre[:], rs2, ALU.mult))
                tt(seq(x[:]), seq(x[:]), pre[:], ALU.add).then_inc(s_xs, 1)

            def conv(l):
                zc, zh, zb = (z[:, a:a + 2, :] for a in (Z_CC, Z_CH, Z_B))

                def rows(t, start, width):
                    return t[:, :, TP + 2:SEG].rearrange("p a (b w) -> p a b w", w=TS + 2)[:, :, :, start:start + width]

                def seqs(t):
                    return t[:, :, TP:T].rearrange("p a (b t) -> p a b t", t=TS)

                pool.wait_ge(s_late, 32)
                hold(pool)
                pool.wait_ge(s_zd, 5 * l + 6)
                tt(rows(up, 2, TS), seqs(zc), seqs(zh), ALU.mult)
                ch.link(tt(up[:, :, 2:TP + 2], zc[:, :, 0:TP], zh[:, :, 0:TP], ALU.mult))
                hold(pool)
                g_.memset(up[:, :, 0:2], 0.0)
                g_.tensor_copy(rows(up, 0, 2), cpv[:, l, :].rearrange("p (a b t) -> p a b t", a=2, t=2))
                g_.tensor_copy(cso[:, :, 0, :], up[:, :, TP:TP + 2])
                last = g_.tensor_copy(cso[:, :, 1:NS, :], rows(up, TS, 2))
                ch.link(last)
                for j in range(3):
                    w = par[:, R_CW + 2 * j:R_CW + 2 * j + 2]
                    out = zc if j == 0 else zh
                    tt(out[:, :, 0:TP], up[:, :, j:TP + j], w.unsqueeze(2).to_broadcast([P, 2, TP]), ALU.mult)
                    ch.link(tt(seqs(out), rows(up, j, TS), w.unsqueeze(2).unsqueeze(3).to_broadcast([P, 2, NB, TS]),
                               ALU.mult))
                    if j:
                        ch.link(tt(zc, zc, zh, ALU.add))
                tt(zc, zc, zb, ALU.mult).then_inc(ev["conv_done"], 1)

            x_scaled(0, 2)
            pool.wait_ge(s_ada[1], 16)
            pool.dma_start(cst[:, C_COS:NC_], A["cst"][:, C_COS:NC_]).then_inc(s_late, 16)
            pool.dma_start(cpv[:], A["cprev"]).then_inc(s_late, 16)
            with pool.Fori(0, DEPTH) as l:
                ch.base, ch.n = l * POOL_CHAIN, 0
                y_norm(3 * l, 0)
                x_scaled(3 * l + 1, 0)
                zf, zf1 = z[:, Z_F:Z_F + 2, :], z[:, Z_F:Z_F + 2, :].rearrange("p a t -> p (a t)")
                pool.wait_ge(ev["cum_log"], l + 1)
                for t0, n, w in ((0, TP // CH, CH), (TP, NB, TS)):
                    b4 = bb.rearrange("p (a t) -> p a t", a=2)[:, :, t0:t0 + n * w]\
                        .rearrange("p a (n w) -> p a n w", w=w)
                    last = tt(zf[:, :, t0:t0 + n * w].rearrange("p a (n w) -> p a n w", w=w),
                              b4[:, :, :, w - 1:w].to_broadcast([P, 2, n, w]), b4, ALU.subtract)
                last.then_inc(ev["end_dist"], 1)
                for r, (t0, t1, step) in enumerate(((Z_K, Z_A + 1, 2), (Z_A + 1, Z_A + 3, 1), (Z_A + 3, Z_A + 4, 1))):
                    w = 2 if r < 2 else 1
                    zr = z[:, t0:t1:step, :]
                    pool.wait_ge(ev["rotated"], 3 * l + r + 1)
                    ch.link(tt(zr, zr, cosT.unsqueeze(1).to_broadcast([P, w, T]), ALU.mult))
                    pool.wait_ge(ev["sines"], 3 * l + r + 1)
                    tt(zr, zr, tail[:, r % 2, 0:w * T].rearrange("p (n t) -> p n t", n=w),
                       ALU.add).then_inc(ev["roped"], 1)
                    if r == 0:
                        pool.wait_ge(ev["end_decay"], l + 1)
                        tt(zf1, zf1, kk, ALU.mult).then_inc(ev["k_decayed"], 1)
                        pool.wait_ge(ev["chunk_decay"], l + 1)
                        tt(eb, eb, z[:, Z_Q:Z_Q + 2, :].rearrange("p a t -> p (a t)"), ALU.mult)\
                            .then_inc(ev["q_decayed"], 1)
                conv(l)
                pool.wait_ge(ev["rec_out_s0"], l + 1)
                for h in range(4):
                    last = tt(vm[:, h], vtok[0:64, 2, 64 * h:64 * h + 64].unsqueeze(1).to_broadcast([64, NB, 64]),
                              seqm[0:64, :].unsqueeze(2).to_broadcast([64, NB, 64]), ALU.mult)
                last.then_inc(ev["v_by_seq"], 1)
                for a in (0, 1):
                    last = tt(s0[:, a], s0[:, a], dec[:, a, 4:12].unsqueeze(2).to_broadcast([P, NB, 64]), ALU.mult)
                last.then_inc(ev["s0_decayed"], 1)
                y_norm(3 * l + 1, 1)
                x_scaled(3 * l + 2, 1)
                y_norm(3 * l + 2, 2)
                x_scaled(3 * l + 3, 2)
                assert ch.n == POOL_CHAIN, ch.n


def laid_out(i):
    c = np.ascontiguousarray

    def cols(a):
        a = a.reshape(*a.shape[:-1], a.shape[-1] // P, P)
        return np.moveaxis(a, (-1, -2), (0, 1))

    x = np.concatenate([i["x_prompt"][0], i["x_sample"].reshape(NB * TS, D)])
    cond = np.concatenate([i["c_prompt"], i["c_sample"]])

    def units(w):
        *lead, rows, n = w.shape
        w = w.reshape(*lead, rows // P, P, n // 256, 256)
        w = np.moveaxis(w, -2, -4)
        w = np.swapaxes(w, -3, -2)
        return w.reshape(*lead, n // 256, P, rows // P * 256)

    w_in = i["ffn_w_in"]
    gate, upw = units(w_in[..., :DFF]), units(w_in[..., DFF:])
    w_in = np.stack([gate, upw], axis=3).reshape(DEPTH, 2, 2 * IT_IN, P, W_IN)
    w_out = units(i["ffn_w_out"]).reshape(DEPTH, 2, 4, P, 2, W_OUT)
    w_out = np.swapaxes(w_out, 3, 4).reshape(DEPTH, 2, 8, P, W_OUT)
    heads = np.arange(NH * HD).reshape(NKV, NG, HD).transpose(1, 0, 2).ravel()
    at = 0
    part = {}
    for name, n in (("q", 512), ("k", 128), ("v", 128), ("qh", 256), ("f", 256), ("i", 256), ("g", 256),
                    ("b", 256), ("c", 256), ("h", 256)):
        part[name] = at + np.arange(n)
        at += n
    part["q"] = part["q"][heads]
    order = np.concatenate([part[n] for n in ("f", "qh", "i", "k", "v", "q", "c", "h", "g", "b")])
    m_in = units(i["mix_w_in"][:, :, order])
    rows = np.concatenate([heads, 512 + np.arange(512)])
    m_out = units(i["mix_w_out"][:, rows, :])
    ada = units(i["ada_w"])
    ada = np.concatenate([ada[:, 8:36], np.roll(ada[:, 0:8], -1, axis=0)], axis=1)
    ab = np.concatenate([i["ada_b"][:, 2048:], np.roll(i["ada_b"][:, :2048], -1, axis=0)], axis=1)
    par = np.empty((DEPTH, P, NR), np.float32)
    par[:, :, R_AB:R_AB + 72] = ab.reshape(DEPTH, 72, P).transpose(0, 2, 1)
    pre = np.roll(i["norm_pre"].reshape(3 * DEPTH, KT, P), -1, axis=0)
    par[:, :, R_PRE:R_PRE + 24] = pre.reshape(DEPTH, 24, P).transpose(0, 2, 1)
    par[:, :, R_POST:R_POST + 24] = i["norm_post"].reshape(DEPTH, 24, P).transpose(0, 2, 1)
    par[:, :, R_SINK:R_SINK + NH] = i["attn_sinks"][:, None, :]
    t = np.arange(P) % 32 // TS
    for n in range(NKV):
        par[:, :, R_SINKS + n] = i["attn_sinks"][:, n * NG + t]
    par[:, :, R_GN] = np.tile(i["hgrn_gnorm"], (1, 2))
    par[:, :, R_CW:R_CW + 6] = i["conv_w"].reshape(DEPTH, 6, P).transpose(0, 2, 1)
    return {
        "x": c(cols(x)), "c": c(cols(cond)), "cst": constants(), "par": par,
        "lb": c(i["hgrn_lower_bounds"].reshape(DEPTH, 2, P).transpose(2, 0, 1)),
        "cprev": c(i["state_conv"].reshape(DEPTH, NB, 2, 2, P).transpose(4, 0, 3, 1, 2).reshape(P, DEPTH, 32)),
        "k": c(i["cache_k_win"].reshape(DEPTH, NB, WIN, P).transpose(0, 3, 1, 2)),
        "v": c(i["cache_v_win"].reshape(DEPTH, NB, WIN, P).transpose(0, 2, 1, 3)),
        "s": c(i["state_hgrn"].reshape(DEPTH, NB, 2, P, 64).transpose(0, 3, 2, 1, 4)),
        "w_in": c(w_in), "w_out": c(w_out), "m_in": c(m_in), "m_out": c(m_out), "ada_w": c(ada),
    }


OUTS = {
    "x": (P, KT, T), "kp": (DEPTH, P, WIN), "vp": (DEPTH, WIN, P), "sp": (DEPTH, 2, 64, 2, 64),
    "conv": (DEPTH, P, 2, NS, 2), "ks": (DEPTH, P, NB, WIN), "vs": (DEPTH, WIN, NB, P),
    "vn": (DEPTH, NB * TS, P), "ss": (DEPTH, P, 2, NB, 64),
}


def returned(r):
    x = r["x"].transpose(2, 1, 0).reshape(T, D)
    conv = r["conv"].transpose(0, 3, 4, 2, 1).reshape(DEPTH, NS, 2, 256)
    vs = np.concatenate([r["vs"][:, :WIN - TS].transpose(0, 2, 1, 3), r["vn"].reshape(DEPTH, NB, TS, P)], axis=2)
    return (
        x[None, :TP], x[TP:].reshape(NB, TS, D),
        r["kp"].transpose(0, 2, 1).reshape(DEPTH, 1, WIN, NKV, HD), r["vp"].reshape(DEPTH, 1, WIN, NKV, HD),
        r["sp"].transpose(0, 3, 1, 2, 4).reshape(DEPTH, 1, 4, 64, 64), conv[:, :1],
        r["ks"].transpose(0, 2, 3, 1).reshape(DEPTH, NB, WIN, NKV, HD), vs.reshape(DEPTH, NB, WIN, NKV, HD),
        r["ss"].reshape(DEPTH, 2, 64, 2, NB, 64).transpose(0, 4, 3, 1, 2, 5).reshape(DEPTH, NB, 4, 64, 64),
        conv[:, 1:],
    )


def kernel(**inputs):
    import concourse.bacc as bacc
    from concourse.bass_utils import run_bass_kernel_spmd

    arrays = laid_out({k: np.asarray(v) for k, v in inputs.items()})
    nc = bacc.Bacc("TRN2", target_bir_lowering=False, num_devices=1)
    A = {k: nc.dram_tensor("in_" + k, a.shape, F32, kind="ExternalInput").ap() for k, a in arrays.items()}
    O = {k: nc.dram_tensor("out_" + k, s, F32, kind="ExternalOutput").ap() for k, s in OUTS.items()}
    trunk(nc, A, O)
    r = run_bass_kernel_spmd(nc, [{"in_" + k: a for k, a in arrays.items()}], core_ids=[0]).results[0]
    return tuple(np.ascontiguousarray(a) for a in returned({k: r["out_" + k] for k in OUTS}))
```
